# Optimizing a Trainium2 kernel written in Bass

```python
import math
import jax
import jax.numpy as jnp
from jax import lax
import numpy as np

D_MODEL = 1024
BATCH = 1
SEQ = 1024
DEPTH = 2

N_MIXERS = 2
DN_HEADS = 8
DN_HEAD_DIM = 128
DN_WIDTH = DN_HEADS * DN_HEAD_DIM
DN_CONV = 5
DN_CHUNK = 64
DN_IN = 4 * DN_WIDTH + 4 * DN_HEADS
CF_CONV = 31
N_EXPERTS = 16
EXPERT_FF = 1024
EC_CAPACITY_FACTOR = 2
EPS = 1e-6
N_A = (DEPTH + 1) // 2
N_B = DEPTH // 2

kernel_name = 'hybrid_gdn_conformer_ec_moe'

def rms_norm(x, g):
    x32 = x.astype(jnp.float32)
    y = x32 * lax.rsqrt(jnp.mean(x32 * x32, axis=-1, keepdims=True) + EPS)
    return (y * g.astype(jnp.float32)).astype(x.dtype)

def layer_norm(x, g, b):
    x32 = x.astype(jnp.float32)
    xc = x32 - jnp.mean(x32, axis=-1, keepdims=True)
    y = xc * lax.rsqrt(jnp.mean(xc * xc, axis=-1, keepdims=True) + EPS)
    return (y * g.astype(jnp.float32) + b.astype(jnp.float32)).astype(x.dtype)

def l2_normalize(a):
    return a * lax.rsqrt(jnp.sum(a * a, axis=-1, keepdims=True) + EPS)

def centred_depthwise_conv(x, w):
    width, ch = w.shape
    pad = width // 2
    return lax.conv_general_dilated(
        x, w[:, None, :].astype(x.dtype), window_strides=(1,), padding=[(pad, pad)],
        dimension_numbers=('NWC', 'WIO', 'NWC'), feature_group_count=ch)

def chunk_gated_delta_rule(q, k, v, log_g, beta):
    b, h, t, dk = q.shape
    dv = v.shape[-1]
    c = DN_CHUNK
    n = t // c
    q, k, v = [a.reshape(b, h, n, c, a.shape[-1]) for a in (q, k, v)]
    beta = beta.reshape(b, h, n, c)
    gc = jnp.cumsum(log_g.reshape(b, h, n, c), axis=-1)
    idx = jnp.arange(c)
    incl = idx[:, None] >= idx[None, :]
    strict = idx[:, None] > idx[None, :]
    decay = jnp.exp(jnp.where(incl, gc[..., :, None] - gc[..., None, :], -jnp.inf))
    kb = k * beta[..., None]
    lower = jnp.where(strict, jnp.einsum('bhncd,bhnsd->bhncs', kb, k) * decay, 0.0)
    eye = jnp.eye(c, dtype=q.dtype)
    rhs = jnp.concatenate([v * beta[..., None], kb * jnp.exp(gc)[..., None]], axis=-1)
    sol = lax.linalg.triangular_solve(eye + lower, rhs, left_side=True, lower=True, unit_diagonal=True)
    u, w = sol[..., :dv], sol[..., dv:]
    intra = jnp.einsum('bhncd,bhnsd->bhncs', q, k) * decay

    def step(state, inp):
        q_i, k_i, u_i, w_i, intra_i, g_i = inp
        v_new = u_i - jnp.einsum('bhcd,bhde->bhce', w_i, state)
        o = (jnp.einsum('bhcd,bhde->bhce', q_i * jnp.exp(g_i)[..., None], state)
             + jnp.einsum('bhcs,bhse->bhce', intra_i, v_new))
        g_last = g_i[..., -1]
        state = (state * jnp.exp(g_last)[..., None, None]
                 + jnp.einsum('bhcd,bhce->bhde', k_i * jnp.exp(g_last[..., None] - g_i)[..., None], v_new))
        return state, o

    xs = tuple(jnp.moveaxis(a, 2, 0) for a in (q, k, u, w, intra, gc))
    state0 = jnp.zeros((b, h, dk, dv), q.dtype)
    _, o = lax.scan(step, state0, xs)
    return jnp.moveaxis(o, 0, 2).reshape(b, h, t, dv)

def gated_deltanet_mixer(hn, w_in, conv_w, a_log, dt_bias, norm_w, w_out):
    b, t, _ = hn.shape
    f32 = jnp.float32
    proj = hn @ w_in
    qkv, z, gates = jnp.split(proj, [3 * DN_WIDTH, 4 * DN_WIDTH], axis=-1)
    qkv = jax.nn.silu(centred_depthwise_conv(qkv, conv_w))
    q, k, v = [a.reshape(b, t, DN_HEADS, DN_HEAD_DIM).transpose(0, 2, 1, 3).astype(f32)
               for a in jnp.split(qkv, 3, axis=-1)]
    q = l2_normalize(q) * (DN_HEAD_DIM ** -0.5)
    k = l2_normalize(k)
    gates = gates.astype(f32).reshape(b, t, 2, 2, DN_HEADS)
    beta = jax.nn.sigmoid(gates[:, :, :, 0, :]).transpose(2, 0, 3, 1)
    log_g = (-jnp.exp(a_log.astype(f32)) * jax.nn.softplus(gates[:, :, :, 1, :] + dt_bias.astype(f32))
             ).transpose(2, 0, 3, 1)
    flip = lambda a: jnp.flip(a, axis=2)
    o_fwd = chunk_gated_delta_rule(q, k, v, log_g[0], beta[0])
    o_bwd = flip(chunk_gated_delta_rule(flip(q), flip(k), flip(v), flip(log_g[1]), flip(beta[1])))
    o = (o_fwd + o_bwd).transpose(0, 2, 1, 3)
    zz = z.reshape(b, t, DN_HEADS, DN_HEAD_DIM).astype(f32)
    o = o * lax.rsqrt(jnp.mean(o * o, axis=-1, keepdims=True) + EPS) * norm_w.astype(f32) * jax.nn.silu(zz)
    return o.reshape(b, t, DN_WIDTH).astype(hn.dtype) @ w_out

def conformer_conv_mixer(hn, w_pw1, b_pw1, dw_w, dw_b, ln_g, ln_b, w_pw2, b_pw2):
    a, gate = jnp.split(hn @ w_pw1 + b_pw1, 2, axis=-1)
    u = a * jax.nn.sigmoid(gate)
    u = centred_depthwise_conv(u, dw_w) + dw_b
    u = jax.nn.silu(layer_norm(u, ln_g, ln_b))
    return u @ w_pw2 + b_pw2

def expert_choice_moe(hn, w_router, w_gate, w_up, w_down):
    b, t, _ = hn.shape
    cap = EC_CAPACITY_FACTOR * t // N_EXPERTS
    probs = jax.nn.softmax((hn @ w_router).astype(jnp.float32), axis=-1)
    aff, tok = lax.top_k(probs.transpose(0, 2, 1), cap)
    bidx = jnp.arange(b)[:, None, None]
    xin = hn[bidx, tok]
    hid = (jax.nn.silu(jnp.einsum('becd,edf->becf', xin, w_gate))
           * jnp.einsum('becd,edf->becf', xin, w_up))
    y = jnp.einsum('becf,efd->becd', hid, w_down) * aff[..., None].astype(hn.dtype)
    return jnp.zeros_like(hn).at[bidx, tok].add(y)

def setup_inputs(seed: int = 0) -> dict:
    key = jax.random.key(seed)
    ks = jax.random.split(key, 24)
    d = D_MODEL

    def nrm(k, shape, scale):
        return jax.random.normal(k, shape, jnp.float32) * scale

    def gain(k, shape):
        return 1.0 + 0.02 * jax.random.normal(k, shape, jnp.float32)

    dt = jnp.exp(jax.random.uniform(ks[6], (N_A, 2, DN_HEADS), jnp.float32,
                                    math.log(1e-3), math.log(1e-1)))
    return {
        'x': nrm(ks[0], (BATCH, SEQ, d), 1.0),
        'norm_mix': gain(ks[1], (DEPTH, d)),
        'norm_ffn': gain(ks[2], (DEPTH, d)),
        'dn_w_in': nrm(ks[3], (N_A, d, DN_IN), d ** -0.5),
        'dn_conv_w': nrm(ks[4], (N_A, DN_CONV, 3 * DN_WIDTH), DN_CONV ** -0.5),
        'dn_a_log': jnp.log(jax.random.uniform(ks[5], (N_A, 2, DN_HEADS), jnp.float32, 1.0, 16.0)),
        'dn_dt_bias': dt + jnp.log(-jnp.expm1(-dt)),
        'dn_norm_w': gain(ks[7], (N_A, DN_HEAD_DIM)),
        'dn_w_out': nrm(ks[8], (N_A, DN_WIDTH, d), DN_WIDTH ** -0.5),
        'cf_w_pw1': nrm(ks[9], (N_B, d, 2 * d), d ** -0.5),
        'cf_b_pw1': nrm(ks[10], (N_B, 2 * d), 0.01),
        'cf_dw_w': nrm(ks[11], (N_B, CF_CONV, d), CF_CONV ** -0.5),
        'cf_dw_b': nrm(ks[12], (N_B, d), 0.01),
        'cf_ln_g': gain(ks[13], (N_B, d)),
        'cf_ln_b': nrm(ks[14], (N_B, d), 0.01),
        'cf_w_pw2': nrm(ks[15], (N_B, d, d), d ** -0.5),
        'cf_b_pw2': nrm(ks[16], (N_B, d), 0.01),
        'moe_w_router': nrm(ks[17], (DEPTH, d, N_EXPERTS), d ** -0.5),
        'moe_w_gate': nrm(ks[18], (DEPTH, N_EXPERTS, d, EXPERT_FF), d ** -0.5),
        'moe_w_up': nrm(ks[19], (DEPTH, N_EXPERTS, d, EXPERT_FF), d ** -0.5),
        'moe_w_down': nrm(ks[20], (DEPTH, N_EXPERTS, EXPERT_FF, d), EXPERT_FF ** -0.5),
        'final_norm': gain(ks[21], (d,)),
    }

def reference(x, norm_mix, norm_ffn, dn_w_in, dn_conv_w, dn_a_log, dn_dt_bias, dn_norm_w, dn_w_out,
              cf_w_pw1, cf_b_pw1, cf_dw_w, cf_dw_b, cf_ln_g, cf_ln_b, cf_w_pw2, cf_b_pw2,
              moe_w_router, moe_w_gate, moe_w_up, moe_w_down, final_norm):
    for i in range(DEPTH):
        j = i // N_MIXERS
        hn = rms_norm(x, norm_mix[i])
        if i % N_MIXERS == 0:
            mix = gated_deltanet_mixer(hn, dn_w_in[j], dn_conv_w[j], dn_a_log[j], dn_dt_bias[j],
                                       dn_norm_w[j], dn_w_out[j])
        else:
            mix = conformer_conv_mixer(hn, cf_w_pw1[j], cf_b_pw1[j], cf_dw_w[j], cf_dw_b[j],
                                       cf_ln_g[j], cf_ln_b[j], cf_w_pw2[j], cf_b_pw2[j])
        x = x + mix
        x = x + expert_choice_moe(rms_norm(x, norm_ffn[i]), moe_w_router[i], moe_w_gate[i],
                                  moe_w_up[i], moe_w_down[i])
    return rms_norm(x, final_norm)


_drawn_inputs = setup_inputs


def setup_inputs(seed=0):
    import zlib

    import numpy as np

    out = dict(_drawn_inputs(seed))
    spreads = {}
    factors = {'norm_ffn': 2.914,
     'dn_norm_w': 3.149,
     'cf_b_pw1': 7.662,
     'cf_dw_b': 5.542,
     'cf_ln_g': 3.985,
     'cf_ln_b': 8.0,
     'cf_b_pw2': 6.168,
     'final_norm': 2.742}
    for name, (base, spread) in spreads.items():
        noise = np.random.default_rng([zlib.crc32(name.encode()), seed]).standard_normal(out[name].shape)
        drawn = base * np.exp(spread * noise) if base else spread * noise
        out[name] = jnp.asarray(drawn.astype(out[name].dtype))
    for name, factor in factors.items():
        out[name] = (out[name] * factor).astype(out[name].dtype)
    return out
```

```python
from contextlib import ExitStack

import numpy as np
import concourse.bass as bass
from concourse import mybir

P = 128
T = 1024
D = 1024
NT = T // P
KT = D // P
H = 8
TAPS = 5
CF_TAPS = 31
E = 16
CAP = 2 * T // E
EPS = 1e-6
HALF = 512
LEVELS = 6
PROJ = 4 * H
NEG = -1e30

ALU = mybir.AluOpType
ACT = mybir.ActivationFunctionType
AX = mybir.AxisListType
F32 = mybir.dt.float32
U32 = mybir.dt.uint32
ds = bass.ds

C_IDENT, C_ONES, C_UF, C_UB, C_NEGF, C_NEGB, C_M0F, C_M0B = (P * n for n in range(8))
C_LM = 8 * P
C_SEL = C_LM + 2 * LEVELS * (P // 2)
C_END = C_SEL + H * P


def constants():
    c = np.zeros((P, C_END), np.float32)
    r, t = np.arange(P)[:, None], np.arange(P)[None, :]
    c[:, C_IDENT:C_IDENT + P] = r == t
    c[:, C_ONES:C_ONES + P] = 1.0
    c[:, C_UF:C_UF + P] = r <= t
    c[:, C_UB:C_UB + P] = r >= t
    c[:, C_NEGF:C_NEGF + P] = np.where(t >= r, 0.0, NEG)
    c[:, C_NEGB:C_NEGB + P] = np.where(t <= r, 0.0, NEG)
    c[:, C_M0F:C_M0F + P] = -1.0 * ((t == r + 1) & (r % 2 == 0))
    c[:, C_M0B:C_M0B + P] = -1.0 * ((t == r - 1) & (r % 2 == 1))
    for d in range(2):
        for j in range(LEVELS):
            b = 2 << j
            cols = (t[0] // b) % 2 == d
            block = t[0][cols] // b
            partner = block + 1 if d == 0 else block - 1
            a = C_LM + (d * LEVELS + j) * (P // 2)
            c[:, a:a + P // 2] = -1.0 * ((r // b) == partner[None, :])
    for h in range(H):
        c[h, C_SEL + h * P:C_SEL + (h + 1) * P] = 1.0
    return c


PE_STEPS = (["dec", "kk", "qk", "x0", "p0"] + [s for j in range(LEVELS) for s in
            ([f"xp{j}", f"p{j + 1}", f"t{j}"] if j < LEVELS - 1 else [f"xp{j}", f"t{j}"])]
            + ["ks", "qs", "xr", "iv", "kv"])
DVE_STEPS = (["sc", "arg", "mt", "intra", "xa", "xt0"] + [s for j in range(LEVELS) for s in (f"pn{j}", f"x{j}")]
             + ["r", "o", "s"])
ACT_STEPS = ["dec", "x0"] + [f"t{j}" for j in range(LEVELS)] + ["oq", "vn"]


def build(nc, a, out, dbg=None):
    ctx = ExitStack()
    with ctx:
        _build(nc, ctx, a, out, dbg or {})


def _build(nc, ctx, a, out, dbg):
    def sem(name):
        return ctx.enter_context(nc.semaphore(name))

    def sems(name, n):
        return [sem(f"{name}{i}") for i in range(n)]

    qk_t = nc.dram_tensor("qk_t", (2 * H, P, T), F32, kind="Internal").ap()
    nat = nc.dram_tensor("nat", (NT, P, PROJ, P), F32, kind="Internal").ap()
    o_dir = nc.dram_tensor("o_dir", (2, NT, P, D), F32, kind="Internal").ap()
    hn_d = [nc.dram_tensor(f"hn_d{l}", (T, D), F32, kind="Internal").ap() for l in range(2)]
    acc_d = [nc.dram_tensor(f"acc_d{l}", (T, D), F32, kind="Internal").ap() for l in range(2)]

    K = 256
    arena = ctx.enter_context(nc.sbuf_tensor("arena", [P, 196 * K], F32))
    cst = ctx.enter_context(nc.sbuf_tensor("cst", [P, 2 * P], F32))
    gain = ctx.enter_context(nc.sbuf_tensor("gain", [P, D], F32))
    small = ctx.enter_context(nc.sbuf_tensor("small", [P, 256], F32))
    idxu = ctx.enter_context(nc.sbuf_tensor("idxu", [P, E + CAP + 4], U32))
    ps = ctx.enter_context(nc.psum_tensor("ps", [P, 8, HALF], F32))

    def part(kib, n):
        at = int(kib * K)
        assert at + n <= 196 * K
        return arena[:, at:at + n]

    def tiles(kib, n, w):
        return part(kib, n * w).rearrange("p (n w) -> p n w", n=n)

    def pair(b):
        return ps[:, b:b + 2, :].rearrange("p b n -> p (b n)")

    def heads(ap):
        return ap.rearrange("p (h n) -> p h n", h=H)

    ident, ones = cst[:, 0:P], cst[:, P:2 * P]
    X = tiles(128, NT, D)
    HT = tiles(96, KT, T)
    xs = tiles(160, 2, D)
    junk = part(168, D)

    ss, rstd = small[:, 0:8], small[:, 8:16]
    epsb = small[:, 16:17]
    lnq = small[:, 17:19]

    s_cst, s_x, s_eps = sem("constants_loaded"), sem("x_loaded"), sem("eps_set")
    gain_loaded, gain_used = sem("gain_loaded"), sem("gain_used")
    stage_done = sem("stage_done")

    def stage_end(eng, n):
        eng.drain().then_inc(stage_done, 1)
        eng.wait_ge(stage_done, 4 * n)

    sq_done, ln_done, rstd_done = sems("sq_done", 5), sems("ln_done", 5), sems("rstd_done", 5)
    xs_done, tp_done, ht_done = sems("xs_done", 5), sems("tp_done", 5), sems("ht_done", 5)
    acc_stored = sems("acc_stored", 2)
    hn_stored = [sems(f"hn_stored{n}_", 2) for n in range(5)]
    gains = [a["norm_mix"][0], a["norm_ffn"][0], a["norm_mix"][1], a["norm_ffn"][1], a["final_norm"]]

    def norm_act(act, n, transpose):
        act.sem_inc(sq_done[n], 1)
        if transpose:
            act.sem_inc(ht_done[n], 2)
        with act.Fori(0, NT) as t:
            act.wait_ge(sq_done[n], t + 1)
            act.activation(junk, X[:, ds(t, 1), :].rearrange("p o n -> p (o n)"), ACT.Square,
                           accum_out=ss[:, ds(t, 1)]).then_inc(sq_done[n], 1)
        act.wait_ge(sq_done[n], NT + 1)
        act.activation(rstd, ss, ACT.Ln, scale=1.0 / D, bias=epsb).then_inc(ln_done[n], 1)
        act.wait_ge(ln_done[n], 1)
        act.activation(rstd, rstd, ACT.Exp, scale=-0.5).then_inc(rstd_done[n], 1)
        if transpose:
            with act.Fori(0, NT // 2) as it:
                for u in range(2):
                    t = it * 2 + u
                    act.wait_ge(tp_done[n], t + 3)
                    act.activation(HT[:, :, ds(t * P, P)], pair(2 * u).rearrange("p (k n) -> p k n", k=KT),
                                   ACT.Copy).then_inc(ht_done[n], 1)

    def norm_dve(dve, n, transpose):
        dve.wait_ge(gain_loaded, 16 * (n + 1))
        dve.wait_ge(rstd_done[n], 1)
        with dve.Fori(0, NT // 2) as it:
            for u in range(2):
                t = it * 2 + u
                if transpose:
                    dve.wait_ge(tp_done[n], t + 1)
                if n % 2 == 1 or n == 4:
                    dve.wait_ge(hn_stored[n][u], it * 16 + 16)
                dve.scalar_tensor_tensor(xs[:, u, :], X[:, ds(t, 1), :].rearrange("p o n -> p (o n)"),
                                         rstd[:, ds(t, 1)], gain[:, :], ALU.mult, ALU.mult).then_inc(xs_done[n], 1)
        dve.wait_ge(xs_done[n], NT)
        dve.sem_inc(gain_used, 1)

    def norm_pe(pe, n):
        pe.sem_inc(tp_done[n], 2)
        with pe.Fori(0, NT // 2) as it:
            for u in range(2):
                t = it * 2 + u
                pe.wait_ge(xs_done[n], t + 1)
                pe.wait_ge(ht_done[n], t + 1)
                for k in range(KT):
                    last = pe.transpose(pair(2 * u)[:, k * P:(k + 1) * P], xs[:, u, k * P:(k + 1) * P], ident)
                last.then_inc(tp_done[n], 1)

    def norm_store(sp, n, dram):
        for u in range(2):
            sp.sem_inc(hn_stored[n][u], 16)
        with sp.Fori(0, NT // 2) as it:
            for u in range(2):
                t = it * 2 + u
                sp.wait_ge(xs_done[n], t + 1)
                sp.dma_start(dram[ds(t * P, P), :], xs[:, u, :]).then_inc(hn_stored[n][u], 16)

    def load_gain(sp, n):
        if n:
            sp.wait_ge(gain_used, n)
        sp.dma_start(gain[:, :], gains[n].partition_broadcast(P)).then_inc(gain_loaded, 16)

    wq = [part(4 * u, D).rearrange("p (k c) -> p k c", k=KT) for u in range(2)]
    PADW = T + TAPS - 1
    pre = [part(8 + 5 * u, PADW) for u in range(2)]
    cv = [part(18 + 4 * u, T) for u in range(2)]
    sl = [part(26 + 4 * u, T) for u in range(2)]
    nrm = [part(34 + 4 * u, T) for u in range(2)]
    natb = [part(42 + 4 * u, T).rearrange("p (c n) -> p c n", c=NT) for u in range(2)]
    sqb, rnb = part(50, T), part(54, T)
    wg = tiles(58, 2, KT * E)
    cw = part(60, PROJ * TAPS).rearrange("p (m j) -> p m j", m=PROJ)
    nsc, nbi = part(61, PROJ), part(61.25, PROJ)
    abias = part(61.5, 4)
    ga, gn, ge, lg, bs = (part(64 + 4 * i, T)[0:E, :] for i in range(5))
    lgn = part(172, NT * E).rearrange("p (c n) -> p c n", c=NT)
    btn = part(173, NT * E).rearrange("p (c n) -> p c n", c=NT)
    SCN = 6
    SC = part(174, 2 * NT * SCN * H).rearrange("p (d c k h) -> p d c k h", d=2, c=NT, k=SCN)
    tot = part(177, NT * E).rearrange("p (c d h) -> p c d h", c=NT, d=2)
    GCT = part(116, 2 * NT * P)

    uf = part(182, 2 * P)

    b_small, w_loaded = sem("b_small_loaded"), sems("w_loaded", 2)
    gate_mm, gate_steps, gate_acts = sem("gate_products"), sem("gate_dve_steps"), sem("gate_act_steps")
    b_zero = sem("b_tables_set")
    proj_done, evac_done, conv_steps, conv_done = sem("proj_done"), sem("evac_done"), sem("conv_steps"), sem("conv_done")
    silu_done, sqb_done, sqmm_done, lnr_done, rn_done = (sem("silu_done"), sem("sqb_done"), sem("sqmm_done"),
                                                         sem("lnr_done"), sem("rn_done"))
    mul_done, tpq_done, nat_done = sem("mul_done"), sem("tpq_done"), sem("nat_done")
    t_stored, n_stored = sems("t_stored", 2), sems("n_stored", 2)
    b2_pe, b2_act, b2_dve = sem("scan_tables_pe"), sem("scan_tables_act"), sem("scan_tables_dve")

    def b_loop(eng, step):
        for m in range(2):
            step(m, m, True, m >= 1, False)
        with eng.Fori(1, PROJ // 2) as it:
            for u in range(2):
                step(it * 2 + u, u, True, True, True)
        step(PROJ, 0, False, True, True)
        step(PROJ + 1, 1, False, False, True)

    loads = [[[tiles(32 * u + 16 * d + 4 * n, H, P) for n in range(4)] for d in range(2)] for u in range(2)]
    dec = [tiles(64 + 26 * d, H, P) for d in range(2)]
    MT = [tiles(68 + 26 * d, H, P) for d in range(2)]
    intra = [tiles(72 + 26 * d, H, P) for d in range(2)]
    XM = [tiles(76 + 26 * d, H, P) for d in range(2)]
    XT = [tiles(80 + 26 * d, H, P) for d in range(2)]
    PN = [tiles(84 + 26 * d, H, P // 2) for d in range(2)]
    VN = [tiles(86 + 26 * d, H, P) for d in range(2)]
    ST = [tiles(160, H, P), tiles(164, H, P)]
    OB = [tiles(168, H, P), tiles(178, H, P)]
    sc = [part(172 + 0.25 * d, SCN * H).rearrange("p (k h) -> p k h", k=SCN) for d in range(2)]
    gmask, gsel = part(188, C_SEL - C_NEGF), part(124, H * P)

    def g(col, n=P):
        return gmask[:, col - C_NEGF:col - C_NEGF + n]

    PE, VE, AE, PL = sems("c_pe", 2), sems("c_dve", 2), sems("c_act", 2), sems("c_pool", 2)
    c_ld = [sems(f"c_loaded{d}_", 2) for d in range(2)]
    o_stored = sems("o_stored", 2)
    s_gcst = sem("masks_loaded")

    def at(steps, name, i, before=0):
        return (i + 1 - before) * len(steps) + steps.index(name) + 1

    def blocks(ap, d, j):
        b = 2 << j
        v = ap.rearrange("p h (n two b) -> p h n two b", two=2, b=b)
        return v[:, :, :, d, :]

    def half(ap, j):
        return ap.rearrange("p h (n b) -> p h n b", b=2 << j)

    wo = tiles(0, KT, D)
    of, ob, sz, og = (tiles(32 + 8 * i, 2, D) for i in range(4))
    ot = [tiles(64 + 4 * u, KT, P) for u in range(2)]
    sqd = part(72, D)
    nw = part(76, P)
    ssd = small[:, 24:40].rearrange("p (u h) -> p u h", u=2)
    wo_loaded, d_loaded = sem("wo_loaded"), sems("d_loaded", 2)
    d_sum, d_sq, d_ss, d_ln, d_ro, d_og = (sem("d_sum"), sem("d_sq"), sem("d_ss"), sem("d_ln"), sem("d_ro"), sem("d_og"))
    d_chain, d_tp, d_ot, d_mm, d_add = sem("d_chain"), sem("d_tp"), sem("d_ot"), sem("d_mm"), sem("d_add")

    def skewed(eng, step):
        step(0, 0, True, False)
        step(1, 1, True, True)
        with eng.Fori(1, NT // 2) as it:
            for u in range(2):
                step(it * 2 + u, u, True, True)
        step(NT, 0, False, True)

    EPAD = T + CF_TAPS - 1
    wag = [[part(8 * u + 4 * n, D).rearrange("p (k c) -> p k c", k=KT) for n in range(2)] for u in range(2)]
    pre_e = [part(16 + 5 * u, EPAD) for u in range(2)]
    sg_e = [part(26, T), part(182, T)]
    acc_e = part(160, T)
    U = tiles(32, KT, T)
    w2 = tiles(64, KT, D)
    sq_e = part(164, T)
    mb, rb = part(168, T), part(172, T)
    dww = part(176, KT * CF_TAPS).rearrange("p (m j) -> p m j", m=KT)
    ccol = part(177, 5 * KT)
    b2b = part(178, D)
    e_small, e_w, w2_loaded = sem("e_small_loaded"), sems("e_w_loaded", 2), sem("w2_loaded")
    e_mm, e_sig, e_pre, e_chain, e_conv, e_zero = (sem("e_mm"), sem("e_sig"), sem("e_pre"), sem("e_chain"),
                                                   sem("e_conv"), sem("e_zero"))
    e_mean, e_mb, e_xc, e_sq, e_sqmm, e_ln, e_rb, e_xn, e_u = (
        sem("e_mean"), sem("e_mb"), sem("e_centred"), sem("e_sq"), sem("e_sqmm"), sem("e_ln"), sem("e_rb"),
        sem("e_normed"), sem("e_u"))
    e_pw2, e_add, e_bias = sem("e_pw2"), sem("e_add"), sem("e_bias_added")

    WG = [tiles(0, KT, D), tiles(64, KT, D)]
    WU = [tiles(32, KT, D), tiles(96, KT, D)]
    WD = tiles(128, KT, D)
    xin = [part(160 + 4 * u, D) for u in range(2)]
    xT = tiles(168, KT, P)
    SG, HD, hT, YS = part(172, D), part(176, D), tiles(180, KT, P), [part(184 + 4 * u, D) for u in range(2)]
    PT = [part(172, T)[0:E, :], part(176, T)[0:E, :]]
    top = ctx.enter_context(nc.sbuf_tensor("top", [P, 5 * P], F32))
    wr = top[:, 0:P].rearrange("p (k e) -> p k e", k=KT)
    pr = top[:, P:2 * P].rearrange("p (t e) -> p t e", t=NT)
    vals, idxf = top[0:E, 2 * P:3 * P], top[0:E, 3 * P:4 * P]
    aff = top[:, 4 * P:4 * P + E]
    mx, sm, rs = small[:, 40:48], small[:, 48:56], small[:, 56:64]
    idxT, idx8 = idxu[:, 0:E], idxu[0:E, E:E + CAP]
    idg, ids = [idxu[:, E + CAP + u:E + CAP + u + 1] for u in range(2)], [idxu[:, E + CAP + 2:E + CAP + 3]] * 2

    wr_loaded, passed = sem("wr_loaded"), sem("passed")
    LAYER = {"logits": 1, "soft": 5, "exp": 1, "pt_mm": 1, "pt": 1, "top": 3 * (CAP // 8) + 1, "top_mm": 1, "idx": 2,
             "wu0": 8 * E, "wu1": 8 * E, "wg0": 8 * E, "wg1": 8 * E, "wd": 16 * E, "gath0": 8 * E, "gath1": 8 * E,
             "idg": 2 * E, "scat": 16 * E, "scat_ok": E + 2, "tpx": E, "xt": E, "gate": E, "up": E, "silu": E,
             "hid": E + 1, "tph": E, "ht": E, "down": E + 1, "y": E + 1}
    ms = {n: sem(f"m_{n}") for n in LAYER}

    def first_layers(l):
        return {n: l * v for n, v in LAYER.items()}

    block = ctx.enter_context(nc.Block())
    stop = dbg.get("stop", 99)

    @block.sync
    def _(sp):
        for n in range(2):
            sp.dma_start(cst[:, n * P:(n + 1) * P], a["consts"][:, n * P:(n + 1) * P]).then_inc(s_cst, 16)
        sp.dma_start(X, a["x"].rearrange("(t p) d -> p t d", p=P)).then_inc(s_x, 16)
        load_gain(sp, 0)
        sp.dma_start(wg, a["w_gates"]).then_inc(b_small, 16)
        sp.dma_start(cw[:, 0:3 * H, :], a["conv_w"]).then_inc(b_small, 16)
        sp.dma_start(abias[0:E, 0:2], a["gate_bias"]).then_inc(b_small, 16)
        sp.dma_start(gmask, a["consts"][:, C_NEGF:C_SEL]).then_inc(s_gcst, 16)
        sp.dma_start(uf, a["consts"][:, C_UF:C_UF + 2 * P]).then_inc(s_gcst, 16)
        for u in range(2):
            sp.sem_inc(t_stored[u], 16)
            sp.sem_inc(n_stored[u], 16)
        for m in range(2):
            sp.dma_start(wq[m], a["w_in"][m]).then_inc(w_loaded[m], 16)

        def b_step(m, u, now, prev, prev2):
            if now:
                if not isinstance(m, int) or m + 2 < PROJ:
                    sp.wait_ge(proj_done, m + 1)
                    sp.dma_start(wq[u], a["w_in"][ds(m + 2, 1)].rearrange("o p k c -> (o p) k c")).then_inc(w_loaded[u], 16)

        def b_stores(m, u, is_t, is_n):
            sp.wait_ge(mul_done, m + 1)
            if is_t:
                sp.dma_start(qk_t[ds(m, 1)].rearrange("o p t -> (o p) t"), nrm[u]).then_inc(t_stored[u], 16)
            else:
                sp.wait_ge(t_stored[u], (m - u) * 8 + 16)
                sp.sem_inc(t_stored[u], 16)
            sp.wait_ge(nat_done, m + 1)
            if is_n:
                sp.dma_start(nat[:, :, ds(m, 1), :].rearrange("c p o n -> p c (o n)"), natb[u]).then_inc(n_stored[u], 16)
            else:
                sp.wait_ge(n_stored[u], (m - u) * 8 + 16)
                sp.sem_inc(n_stored[u], 16)

        def b_range(lo, hi, is_t, is_n, load):
            with sp.Fori(lo // 2, hi // 2) as it:
                for u in range(2):
                    if load:
                        sp.wait_ge(proj_done, it * 2 + u + 1)
                        sp.dma_start(wq[u], a["w_in"][ds(it * 2 + u + 2, 1)].rearrange("o p k c -> (o p) k c")
                                     ).then_inc(w_loaded[u], 16)
                    b_stores(it * 2 + u - 2, u, is_t, is_n)

        for m in range(2):
            b_step(m, m, True, False, False)
        b_range(2, H + 2, True, False, True)
        b_range(H + 2, 2 * H + 2, True, True, True)
        b_range(2 * H + 2, PROJ - 2, False, True, True)
        b_range(PROJ - 2, PROJ + 2, False, True, False)
        for u in range(2):
            sp.wait_ge(t_stored[u], 8 * PROJ + 16)
            sp.wait_ge(n_stored[u], 8 * PROJ + 16)
        if stop <= 1:
            return
        sp.wait_ge(stage_done, 4 * 1)
        sp.dma_start(gsel, a["consts"][:, C_SEL:C_END]).then_inc(s_gcst, 16)
        with sp.Fori(0, NT // 2) as it:
            for u in range(2):
                i = it * 2 + u
                for d in range(2):
                    c = i if d == 0 else i * -1 + (NT - 1)
                    sp.wait_ge(VE[d], at(DVE_STEPS, "s", i, 2) + len(DVE_STEPS))
                    for n, src in enumerate((qk_t[0:H, :, ds(c * P, P)].rearrange("h p t -> p h t"),
                                             qk_t[H:2 * H, :, ds(c * P, P)].rearrange("h p t -> p h t"),
                                             nat[ds(c, 1), :, H:2 * H, :].rearrange("o p h n -> (o p) h n"),
                                             nat[ds(c, 1), :, 2 * H:3 * H, :].rearrange("o p h n -> (o p) h n"))):
                        sp.dma_start(loads[u][d][n], src).then_inc(c_ld[d][u], 16)
        for d in range(2):
            sp.wait_ge(o_stored[d], 16 * (NT + 1))
        if stop <= 2:
            return
        sp.wait_ge(stage_done, 4 * 2)
        sp.dma_start(wo, a["dn_w_out"].rearrange("(k p) n -> p k n", p=P)).then_inc(wo_loaded, 16)
        sp.dma_start(nw, a["dn_norm_w"].partition_broadcast(P)).then_inc(wo_loaded, 16)
        with sp.Fori(0, NT // 2) as it:
            for u in range(2):
                c = it * 2 + u
                sp.wait_ge(d_og, c + 1)
                for dst, src in ((of, o_dir[0][ds(c, 1)]), (ob, o_dir[1][ds(c, 1)]),
                                 (sz, nat[ds(c, 1), :, 3 * H:PROJ, :].rearrange("o p h n -> o p (h n)"))):
                    sp.dma_start(dst[:, u, :], src.rearrange("o p n -> (o p) n")).then_inc(d_loaded[u], 16)

        def moe_sp(l, n, x_done):
            base = first_layers(l)
            load_gain(sp, n)
            sp.dma_start(wr, a["w_router"][l]).then_inc(wr_loaded, 16)
            x_done(sp)
            sp.dma_start(acc_d[l].rearrange("(t p) d -> p t d", p=P), X).then_inc(acc_stored[l], 16)

            def load(w, e, dst, s):
                sp.dma_start(dst, a[w][l][ds(e, 1)].rearrange("o (k p) f -> p (o k) f", p=P)).then_inc(ms[s], 16)

            norm_store(sp, n, hn_d[l])
            load("w_gate", 0, WG[0], "wg0")
            load("w_up", 0, WU[0], "wu0")
            load("w_gate", 1, WG[1], "wg1")
            sp.wait_ge(ms["logits"], 1 + base["logits"])
            load("w_up", 1, WU[1], "wu1")
            sp.wait_ge(xs_done[n], NT)
            sp.wait_ge(acc_stored[l], 16)
            with sp.Fori(0, E // 2 - 1) as it:
                for u in range(2):
                    e = it * 2 + u
                    sp.wait_ge(ms["down"], e + 1 + base["down"])
                    load("w_down", e, WD, "wd")
                    sp.wait_ge(ms["up"], e + 1 + base["up"])
                    load("w_gate", e + 2, WG[u], f"wg{u}")
                    load("w_up", e + 2, WU[u], f"wu{u}")
            for e in (E - 2, E - 1):
                sp.wait_ge(ms["down"], e + 1 + base["down"])
                load("w_down", e, WD, "wd")
            sp.wait_ge(ms["scat_ok"], E + 2 + base["scat_ok"])
            sp.wait_ge(ms["down"], E + 1 + base["down"])
            sp.dma_start(X, acc_d[l].rearrange("(t p) d -> p t d", p=P)).then_inc(s_x, 16)

        moe_sp(0, 1, lambda sp: sp.wait_ge(d_add, NT + 1))
        if stop <= 4:
            sp.wait_ge(s_x, 32)
            return
        sp.wait_ge(stage_done, 4 * 3)
        load_gain(sp, 2)
        for m in range(2):
            for n in range(2):
                sp.dma_start(wag[m][n], a["w_pw1"][m + KT * n]).then_inc(e_w[m], 16)
        sp.dma_start(dww, a["cf_dw_w"]).then_inc(e_small, 16)
        sp.dma_start(ccol, a["cf_cols"]).then_inc(e_small, 16)
        sp.dma_start(b2b, a["b_pw2"].partition_broadcast(P)).then_inc(e_small, 16)
        sp.dma_start(w2, a["w_pw2"].rearrange("(k p) n -> p k n", p=P)).then_inc(w2_loaded, 16)
        with sp.Fori(0, KT // 2 - 1) as it:
            for u in range(2):
                ch = it * 2 + u
                sp.wait_ge(e_mm, ch + 1)
                for n in range(2):
                    sp.dma_start(wag[u][n], a["w_pw1"][ds(ch + 2 + KT * n, 1)].rearrange("o p k c -> (o p) k c")
                                 ).then_inc(e_w[u], 16)
        moe_sp(1, 3, lambda sp: sp.wait_ge(e_add, NT))
        sp.wait_ge(stage_done, 4 * 4)
        load_gain(sp, 4)
        norm_store(sp, 4, out[0])
        for u in range(2):
            sp.wait_ge(hn_stored[4][u], 16 * (NT // 2 + 1))

    @block.gpsimd
    def _(pool):
        pool.memset(epsb, EPS).then_inc(s_eps, 1)
        pool.memset(cw[:, 3 * H:PROJ, :], 0.0).then_inc(b_zero, 1)
        pool.wait_ge(b_zero, 1)
        pool.memset(cw[:, 3 * H:PROJ, TAPS // 2:TAPS // 2 + 1], 1.0).then_inc(b_zero, 1)
        pool.memset(nsc[:, 0:2 * H], -0.5).then_inc(b_zero, 1)
        pool.memset(nsc[:, 2 * H:PROJ], 0.0).then_inc(b_zero, 1)
        pool.memset(nbi[:, 0:H], -0.5 * float(np.log(P))).then_inc(b_zero, 1)
        pool.memset(nbi[:, H:PROJ], 0.0).then_inc(b_zero, 1)
        for u in range(2):
            pool.memset(pre[u][:, 0:TAPS // 2], 0.0).then_inc(b_zero, 1)
            pool.memset(pre[u][:, T + TAPS // 2:PADW], 0.0).then_inc(b_zero, 1)
        if stop <= 1:
            return
        stage_end(pool, 1)
        for d in range(2):
            pool.sem_inc(PL[d], 1)
        with pool.Fori(0, NT) as i:
            for d in range(2):
                pool.wait_ge(AE[d], at(ACT_STEPS, "vn", i))
                pool.tensor_tensor(XM[d], VN[d], sc[d][:, 2, :].unsqueeze(2).to_broadcast([P, H, P]), ALU.mult
                                   ).then_inc(PL[d], 1)
        if stop <= 2:
            return
        stage_end(pool, 2)

        def moe_pool_run(l, n):
            base = first_layers(l)
            pool.wait_ge(ms["idx"], 2 + base["idx"])
            for u in range(2):
                pool.wait_ge(hn_stored[n][u], 16 * (NT // 2 + 1))
            pool.wait_ge(acc_stored[l], 16)
            pool.sem_inc(ms["scat_ok"], 2)
            for u in range(2):
                pool.tensor_copy(idg[u], idxT[:, u:u + 1]).then_inc(ms["idg"], 1)
            pool.wait_ge(ms["idg"], 2 + base["idg"])
            for u in range(2):
                pool.indirect_dma_start(xin[u], None, hn_d[l], bass.IndirectOffsetOnAxis(ap=idg[u], axis=0)
                                        ).then_inc(ms[f"gath{u}"], 16)
            def gather(e, u, n_idg):
                pool.wait_ge(ms["tpx"], e - 1 + base["tpx"])
                pool.tensor_copy(idg[u], idxT[:, ds(e, 1)]).then_inc(ms["idg"], 1)
                pool.wait_ge(ms["idg"], n_idg + base["idg"])
                pool.sem_inc(passed, 1)
                pool.indirect_dma_start(xin[u], None, hn_d[l], bass.IndirectOffsetOnAxis(ap=idg[u], axis=0)
                                        ).then_inc(ms[f"gath{u}"], 16)

            def scatter(e, u, n_idg, first=False):
                if not first:
                    pool.wait_ge(ms["scat"], e * 16 + base["scat"])
                    pool.sem_inc(ms["scat_ok"], 1)
                pool.wait_ge(ms["y"], e + 2 + base["y"])
                pool.tensor_copy(ids[0], idxT[:, ds(e, 1)]).then_inc(ms["idg"], 1)
                pool.wait_ge(ms["idg"], n_idg + base["idg"])
                pool.sem_inc(passed, 1)
                pool.indirect_dma_start(acc_d[l], bass.IndirectOffsetOnAxis(ap=ids[0], axis=0), YS[u], None,
                                        compute_op=ALU.add).then_inc(ms["scat"], 16)

            for e in (2, 3):
                gather(e, e % 2, e + 1)
            for e in range(2):
                gather(e + 4, e, 2 * e + 5)
                scatter(e, e, 2 * e + 6, e == 0)
            with pool.Fori(1, E // 2 - 2) as it:
                for u in range(2):
                    e = it * 2 + u
                    gather(e + 4, u, e * 2 + 5)
                    scatter(e, u, e * 2 + 6)
            for e in range(E - 4, E):
                scatter(e, e % 2, E + e + 1)
            pool.wait_ge(ms["scat"], 16 * E + base["scat"])
            pool.sem_inc(ms["scat_ok"], 1)

        moe_pool_run(0, 1)
        if stop <= 4:
            return
        stage_end(pool, 3)
        for u in range(2):
            pool.memset(pre_e[u][:, 0:CF_TAPS // 2], 0.0).then_inc(e_zero, 1)
            pool.memset(pre_e[u][:, T + CF_TAPS // 2:EPAD], 0.0).then_inc(e_zero, 1)
        pool.wait_ge(e_small, 48)
        pool.wait_ge(xs_done[2], NT)
        for t in range(NT):
            pool.tensor_tensor(X[:, t, :], X[:, t, :], b2b, ALU.add).then_inc(e_bias, 1)
        moe_pool_run(1, 3)
        stage_end(pool, 4)

    @block.scalar
    def _(act):
        act.wait_ge(s_eps, 1)
        act.wait_ge(s_x, 16)
        norm_act(act, 0, True)
        act.wait_ge(b_small, 48)
        act.activation(abias[0:E, 2:3], abias[0:E, 0:1], ACT.Exp).then_inc(gate_acts, 1)
        act.wait_ge(gate_steps, 2)
        act.activation(ge, gn, ACT.Exp).then_inc(gate_acts, 1)
        act.wait_ge(gate_acts, 2)
        act.activation(ge, ge, ACT.Ln, bias=1.0).then_inc(gate_acts, 1)
        act.wait_ge(gate_mm, 2)
        act.activation(bs, pair(6)[0:E, :], ACT.Sigmoid).then_inc(gate_acts, 1)
        act.wait_ge(b_zero, 10)

        def b_step(m, u, now, prev, prev2):
            if now:
                act.wait_ge(proj_done, m + 1)
                if prev2:
                    act.wait_ge(conv_done, m - 1)
                act.activation(pre[u][:, TAPS // 2:TAPS // 2 + T], pair(2 * u), ACT.Copy).then_inc(evac_done, 1)
            if prev:
                p = m - 1
                act.wait_ge(sqmm_done, p + 1)
                act.wait_ge(mul_done, p)
                act.activation(rnb, pair(4), ACT.Ln, bias=epsb).then_inc(lnr_done, 1)
                act.wait_ge(lnr_done, p + 1)
                act.activation(rnb, rnb, ACT.Exp, scale=nsc[:, ds(p, 1)], bias=nbi[:, ds(p, 1)]).then_inc(rn_done, 1)
            if now:
                act.wait_ge(conv_done, m + 1)
                if prev2:
                    act.wait_ge(mul_done, m - 1)
                act.activation(sl[u], cv[u], ACT.Silu).then_inc(silu_done, 1)
                act.wait_ge(silu_done, m + 1)
                if prev:
                    act.wait_ge(sqmm_done, m)
                act.activation(sqb, sl[u], ACT.Square).then_inc(sqb_done, 1)
            if prev2:
                p = m - 2
                act.wait_ge(tpq_done, p + 3)
                act.wait_ge(n_stored[u], (p - u) * 8 + 16)
                act.activation(natb[u], pair(6).rearrange("p (c n) -> p c n", c=NT), ACT.Copy).then_inc(nat_done, 1)

        b_loop(act, b_step)
        act.wait_ge(b2_pe, 1)
        act.activation(lgn, ps[:, 0, 0:NT * E].rearrange("p (c n) -> p c n", c=NT), ACT.Copy).then_inc(b2_act, 1)
        act.activation(btn, ps[:, 1, 0:NT * E].rearrange("p (c n) -> p c n", c=NT), ACT.Copy).then_inc(b2_act, 1)
        act.wait_ge(b2_pe, 2)
        act.activation(tot.rearrange("p c d h -> p (c d h)"), ps[:, 4, 0:NT * E], ACT.Copy).then_inc(b2_act, 1)
        for d in range(2):
            act.activation(SC[:, d, :, 0, :], ps[:, 2 + d, 0:NT * H].rearrange("p (c h) -> p c h", c=NT), ACT.Copy
                           ).then_inc(b2_act, 1)
        act.wait_ge(b2_act, 5)
        for d in range(2):
            act.activation(SC[:, d, :, 1, :], SC[:, d, :, 0, :], ACT.Exp).then_inc(b2_act, 1)
            act.activation(SC[:, d, :, 3, :], tot[:, :, d, :], ACT.Exp).then_inc(b2_act, 1)
            act.activation(SC[:, d, :, 4, :], btn[:, :, d * H:(d + 1) * H], ACT.Copy).then_inc(b2_act, 1)
        act.wait_ge(b2_act, 11)
        act.wait_ge(b2_dve, 2)
        for d in range(2):
            act.activation(SC[:, d, :, 5, :], SC[:, d, :, 1, :], ACT.Copy, scale=-1.0).then_inc(b2_act, 1)
            act.activation(SC[:, d, :, 2, :], SC[:, d, :, 2, :], ACT.Exp).then_inc(b2_act, 1)
        act.wait_ge(b2_pe, 3)
        act.activation(GCT[0:H, :], ps[0:H, 4:8, :].rearrange("p b n -> p (b n)"), ACT.Copy).then_inc(b2_act, 1)
        if stop <= 1:
            return
        stage_end(act, 1)
        for d in range(2):
            act.sem_inc(AE[d], len(ACT_STEPS))
            act.sem_inc(o_stored[d], 16)

        with act.Fori(0, NT) as i:
            for d in range(2):
                act.wait_ge(VE[d], at(DVE_STEPS, "arg", i))
                act.activation(dec[d], dec[d], ACT.Exp).then_inc(AE[d], 1)
            for d in range(2):
                act.wait_ge(PE[d], at(PE_STEPS, "x0", i))
                act.activation(XM[d], heads(pair(4 * d + 2)), ACT.Copy).then_inc(AE[d], 1)
            for j in range(LEVELS):
                for d in range(2):
                    act.wait_ge(PE[d], at(PE_STEPS, f"t{j}", i))
                    act.activation(XT[d], heads(pair(4 * d + 2)), ACT.Copy).then_inc(AE[d], 1)
            for d in range(2):
                act.wait_ge(PE[d], at(PE_STEPS, "qs", i))
                act.wait_ge(o_stored[d], i * 16 + 16)
                for h in range(H):
                    last = act.activation(OB[d][:, h, :], pair(4 * d + 2)[:, h * P:(h + 1) * P], ACT.Copy,
                                          scale=sc[d][:, 1, h:h + 1])
                last.then_inc(AE[d], 1)
            for d in range(2):
                act.wait_ge(PE[d], at(PE_STEPS, "xr", i))
                for h in range(H):
                    last = act.activation(VN[d][:, h, :], pair(4 * d)[:, h * P:(h + 1) * P], ACT.Copy,
                                          scale=sc[d][:, 4, h:h + 1])
                last.then_inc(AE[d], 1)
            for d in range(2):
                c = i if d == 0 else i * -1 + (NT - 1)
                act.wait_ge(VE[d], at(DVE_STEPS, "o", i))
                act.dma_start(o_dir[d][ds(c, 1)].rearrange("o p n -> (o p) n"),
                              OB[d].rearrange("p h n -> p (h n)")).then_inc(o_stored[d], 16)
        if stop <= 2:
            return
        stage_end(act, 2)

        act.sem_inc(d_ot, 1)

        def d_step(c, u, now, prev):
            if now:
                act.wait_ge(d_sum, c + 1)
                act.wait_ge(d_ss, c + 1)
                act.activation(sqd, of[:, u, :], ACT.Square).then_inc(d_sq, 1)
                act.wait_ge(d_ss, c + 2)
                act.activation(ssd[:, u, :], ssd[:, u, :], ACT.Ln, scale=1.0 / P, bias=epsb).then_inc(d_ln, 1)
                act.wait_ge(d_ln, c + 1)
                act.activation(ssd[:, u, :], ssd[:, u, :], ACT.Exp, scale=-0.5).then_inc(d_ro, 1)
                act.wait_ge(d_tp, c + 3)
                act.wait_ge(d_mm, c + 1)
                act.activation(ot[u], pair(0).rearrange("p (k n) -> p k n", k=KT), ACT.Copy).then_inc(d_ot, 1)

        skewed(act, d_step)

        def moe_act(l, n):
            base = first_layers(l)
            norm_act(act, n, True)
            act.wait_ge(ms["soft"], 2 + base["soft"])
            act.activation(pr, pr, ACT.Exp).then_inc(ms["exp"], 1)
            act.wait_ge(ms["pt_mm"], 1 + base["pt_mm"])
            act.activation(PT[0], ps[0:E, 2:4, :].rearrange("p b n -> p (b n)"), ACT.Copy).then_inc(ms["pt"], 1)

            def x_evac(e):
                act.wait_ge(ms["tpx"], e + 1 + base["tpx"])
                act.activation(xT, pair(6).rearrange("p (k n) -> p k n", k=KT), ACT.Copy).then_inc(ms["xt"], 1)

            def silu(e):
                act.wait_ge(ms["gate"], e + 1 + base["gate"])
                act.wait_ge(ms["hid"], e + 1 + base["hid"])
                act.activation(SG, pair(0), ACT.Silu).then_inc(ms["silu"], 1)

            def h_evac(e):
                act.wait_ge(ms["tph"], e + 1 + base["tph"])
                act.activation(hT, pair(6).rearrange("p (k n) -> p k n", k=KT), ACT.Copy).then_inc(ms["ht"], 1)

            x_evac(0)
            silu(0)
            act.wait_ge(ms["up"], 1 + base["up"])
            x_evac(1)
            with act.Fori(0, E - 2) as e:
                silu(e + 1)
                h_evac(e)
                act.wait_ge(ms["up"], e + 2 + base["up"])
                x_evac(e + 2)
            silu(E - 1)
            h_evac(E - 2)
            h_evac(E - 1)

        act.wait_ge(d_add, NT + 1)
        moe_act(0, 1)
        if stop <= 4:
            return
        stage_end(act, 3)
        act.wait_ge(s_x, 32)
        norm_act(act, 2, True)
        act.wait_ge(e_small, 48)
        with act.Fori(0, KT // 2) as it:
            for u in range(2):
                ch = it * 2 + u
                act.wait_ge(e_mm, ch + 1)
                act.wait_ge(e_pre, ch + 1)
                act.activation(sg_e[u], pair(4 * u + 2), ACT.Sigmoid, bias=ccol[:, ds(ch + KT, 1)]
                               ).then_inc(e_sig, 1)
        for k in range(KT):
            act.wait_ge(e_xc, k + 1)
            if k:
                act.wait_ge(e_sqmm, k)
            act.activation(sq_e, U[:, k, :], ACT.Square).then_inc(e_sq, 1)
        act.wait_ge(e_sqmm, KT)
        act.activation(rb, pair(2), ACT.Ln, scale=1.0 / D, bias=epsb).then_inc(e_ln, 1)
        act.wait_ge(e_ln, 1)
        act.activation(rb, rb, ACT.Exp, scale=-0.5).then_inc(e_rb, 1)
        for k in range(KT):
            act.wait_ge(e_xn, k + 1)
            act.activation(U[:, k, :], U[:, k, :], ACT.Silu, scale=ccol[:, 3 * KT + k:3 * KT + k + 1],
                           bias=ccol[:, 4 * KT + k:4 * KT + k + 1]).then_inc(e_u, 1)
        act.wait_ge(e_add, NT)
        moe_act(1, 3)
        stage_end(act, 4)
        act.wait_ge(s_x, 48)
        norm_act(act, 4, False)

    @block.vector
    def _(dve):
        norm_dve(dve, 0, True)
        dve.wait_ge(gate_mm, 1)
        dve.wait_ge(b_small, 48)
        dve.tensor_scalar(ga, pair(4)[0:E, :], abias[0:E, 1:2], None, ALU.add).then_inc(gate_steps, 1)
        dve.wait_ge(gate_steps, 1)
        dve.scalar_tensor_tensor(gn, ga, -1.0, ga, ALU.mult, ALU.min).then_inc(gate_steps, 1)
        dve.wait_ge(gate_acts, 3)
        dve.scalar_tensor_tensor(lg, ga, 0.0, ge, ALU.max, ALU.add).then_inc(gate_steps, 1)
        dve.wait_ge(gate_steps, 3)
        dve.tensor_scalar(lg, lg, abias[0:E, 2:3], -1.0, ALU.mult, ALU.mult).then_inc(gate_steps, 1)
        dve.wait_ge(b_zero, 10)

        def b_step(m, u, now, prev, prev2):
            if now:
                dve.wait_ge(evac_done, m + 1)
                if prev2:
                    dve.wait_ge(silu_done, m - 1)
                for j in range(TAPS):
                    tap = cw[:, ds(m, 1), j:j + 1].rearrange("p o j -> p (o j)")
                    if j == 0:
                        ins = dve.tensor_scalar(cv[u], pre[u][:, 0:T], tap, None, ALU.mult)
                    else:
                        ins = dve.scalar_tensor_tensor(cv[u], pre[u][:, j:j + T], tap, cv[u], ALU.mult, ALU.add)
                    if j < TAPS - 1:
                        ins.then_inc(conv_steps, 1)
                        dve.wait_ge(conv_steps, m * (TAPS - 1) + j + 1)
                    else:
                        ins.then_inc(conv_done, 1)
            if prev:
                p = m - 1
                dve.wait_ge(rn_done, p + 1)
                dve.wait_ge(tpq_done, p + 1)
                dve.wait_ge(t_stored[1 - u], (p - (1 - u)) * 8 + 16)
                dve.tensor_tensor(nrm[1 - u], sl[1 - u], rnb, ALU.mult).then_inc(mul_done, 1)

        b_loop(dve, b_step)
        dve.wait_ge(b2_act, 5)
        for d in range(2):
            dve.tensor_tensor(SC[:, d, :, 2, :], tot[:, :, d, :], SC[:, d, :, 0, :], ALU.subtract).then_inc(b2_dve, 1)
        if stop <= 1:
            return
        stage_end(dve, 1)
        for d in range(2):
            dve.sem_inc(VE[d], len(DVE_STEPS) - 1)
            dve.memset(ST[d], 0.0).then_inc(VE[d], 1)
        dve.wait_ge(s_gcst, 32)
        negm = [g(C_NEGF), g(C_NEGB)]
        m0 = [g(C_M0F), g(C_M0B)]

        with dve.Fori(0, NT // 2) as it:
            for u in range(2):
                i = it * 2 + u
                for d in range(2):
                    c = i if d == 0 else i * -1 + (NT - 1)
                    dve.wait_ge(AE[d], at(ACT_STEPS, "vn", i, 1))
                    dve.wait_ge(VE[d], at(DVE_STEPS, "s", i, 1))
                    dve.wait_ge(PL[d], i + 1)
                    dve.tensor_copy(sc[d], SC[:, d, ds(c, 1), :, :].rearrange("p o k h -> p (o k) h")).then_inc(VE[d], 1)
                for d in range(2):
                    dve.wait_ge(VE[d], at(DVE_STEPS, "sc", i))
                    dve.wait_ge(PE[d], at(PE_STEPS, "dec", i))
                    for h in range(H):
                        last = dve.scalar_tensor_tensor(dec[d][:, h, :], pair(4 * d)[:, h * P:(h + 1) * P],
                                                        sc[d][:, 0, h:h + 1], negm[d], ALU.subtract, ALU.min)
                    last.then_inc(VE[d], 1)
                for d in range(2):
                    dve.wait_ge(PE[d], at(PE_STEPS, "kk", i))
                    dve.wait_ge(AE[d], at(ACT_STEPS, "dec", i))
                    for h in range(H):
                        last = dve.scalar_tensor_tensor(MT[d][:, h, :], pair(4 * d + 2)[:, h * P:(h + 1) * P],
                                                        sc[d][:, 4, h:h + 1], dec[d][:, h, :], ALU.mult, ALU.mult)
                    last.then_inc(VE[d], 1)
                    dve.wait_ge(PE[d], at(PE_STEPS, "qk", i))
                    dve.tensor_tensor(intra[d], heads(pair(4 * d)), dec[d], ALU.mult).then_inc(VE[d], 1)
                for d in range(2):
                    dve.wait_ge(VE[d], at(DVE_STEPS, "mt", i))
                    dve.tensor_tensor(XT[d], MT[d], m0[d].unsqueeze(1).to_broadcast([P, H, P]), ALU.mult
                                      ).then_inc(VE[d], 1)
                    dve.wait_ge(VE[d], at(DVE_STEPS, "xa", i))
                    dve.tensor_tensor(XT[d], XT[d], ident.unsqueeze(1).to_broadcast([P, H, P]), ALU.add
                                      ).then_inc(VE[d], 1)
                for j in range(LEVELS):
                    for d in range(2):
                        lm = C_LM + (d * LEVELS + j) * (P // 2)
                        dve.wait_ge(PE[d], at(PE_STEPS, f"p{j}", i))
                        dve.tensor_tensor(PN[d], ps[:, 4 * d, :].rearrange("p (h n) -> p h n", h=H),
                                          g(lm, P // 2).unsqueeze(1).to_broadcast([P, H, P // 2]), ALU.mult
                                          ).then_inc(VE[d], 1)
                    for d in range(2):
                        dve.wait_ge(PE[d], at(PE_STEPS, f"xp{j}", i))
                        dve.tensor_tensor(blocks(XM[d], d, j), blocks(XM[d], d, j),
                                          half(ps[:, 4 * d + 1, :].rearrange("p (h n) -> p h n", h=H), j),
                                          ALU.add).then_inc(VE[d], 1)
                for d in range(2):
                    dve.wait_ge(PE[d], at(PE_STEPS, "ks", i))
                    for h in range(H):
                        last = dve.scalar_tensor_tensor(dec[d][:, h, :], pair(4 * d)[:, h * P:(h + 1) * P],
                                                        sc[d][:, 5, h:h + 1], loads[u][d][3][:, h, :],
                                                        ALU.mult, ALU.add)
                    last.then_inc(VE[d], 1)
                for d in range(2):
                    dve.wait_ge(PE[d], at(PE_STEPS, "iv", i))
                    dve.tensor_tensor(OB[d], OB[d], heads(pair(4 * d)), ALU.add).then_inc(VE[d], 1)
                for d in range(2):
                    dve.wait_ge(PE[d], at(PE_STEPS, "kv", i))
                    for h in range(H):
                        last = dve.scalar_tensor_tensor(ST[d][:, h, :], ST[d][:, h, :], sc[d][:, 3, h:h + 1],
                                                        pair(4 * d + 2)[:, h * P:(h + 1) * P], ALU.mult, ALU.add)
                    last.then_inc(VE[d], 1)
        if stop <= 2:
            return
        stage_end(dve, 2)

        dve.sem_inc(d_og, 2)
        dve.sem_inc(d_ss, 1)
        dve.sem_inc(d_add, 1)
        dve.wait_ge(wo_loaded, 32)

        def d_step(c, u, now, prev):
            if now:
                it2 = (c - u) * 24 + 48
                dve.wait_ge(d_loaded[u], it2)
                dve.tensor_tensor(of[:, u, :], of[:, u, :], ob[:, u, :], ALU.add).then_inc(d_sum, 1)
                dve.wait_ge(d_sq, c + 1)
                dve.tensor_reduce(ssd[:, u, :], heads(sqd), AX.X, ALU.add).then_inc(d_ss, 1)
                dve.wait_ge(d_ro, c + 1)
                dve.tensor_tensor(heads(of[:, u, :]), heads(of[:, u, :]),
                                  ssd[:, u, :].unsqueeze(2).to_broadcast([P, H, P]), ALU.mult).then_inc(d_chain, 1)
                dve.wait_ge(d_chain, c * 2 + 1)
                dve.tensor_tensor(heads(of[:, u, :]), heads(of[:, u, :]),
                                  nw.unsqueeze(1).to_broadcast([P, H, P]), ALU.mult).then_inc(d_chain, 1)
                dve.wait_ge(d_chain, c * 2 + 2)
                dve.wait_ge(d_tp, c + 1)
                dve.tensor_tensor(og[:, u, :], of[:, u, :], sz[:, u, :], ALU.mult).then_inc(d_og, 1)
            if prev:
                p = c - 1
                dve.wait_ge(d_mm, p + 3)
                xt = X[:, ds(p, 1), :].rearrange("p o n -> p (o n)")
                dve.tensor_tensor(xt, xt, pair(4 + 2 * (1 - u)), ALU.add).then_inc(d_add, 1)

        skewed(dve, d_step)

        def moe_dve(l, n):
            base = first_layers(l)
            norm_dve(dve, n, True)
            dve.wait_ge(ms["logits"], 1 + base["logits"])
            lgt = ps[:, 0, 0:P].rearrange("p (t e) -> p t e", t=NT)
            dve.tensor_reduce(mx, lgt, AX.X, ALU.max).then_inc(ms["soft"], 1)
            dve.wait_ge(ms["soft"], 1 + base["soft"])
            dve.tensor_tensor(pr, lgt, mx.unsqueeze(2).to_broadcast([P, NT, E]), ALU.subtract).then_inc(ms["soft"], 1)
            dve.wait_ge(ms["exp"], 1 + base["exp"])
            dve.tensor_reduce(sm, pr, AX.X, ALU.add).then_inc(ms["soft"], 1)
            dve.wait_ge(ms["soft"], 3 + base["soft"])
            dve.reciprocal(rs, sm).then_inc(ms["soft"], 1)
            dve.wait_ge(ms["soft"], 4 + base["soft"])
            dve.tensor_tensor(pr, pr, rs.unsqueeze(2).to_broadcast([P, NT, E]), ALU.mult).then_inc(ms["soft"], 1)
            dve.wait_ge(ms["pt"], 1 + base["pt"])
            for r in range(CAP // 8):
                v8, i8 = vals[:, r * 8:r * 8 + 8], idx8[:, r * 8:r * 8 + 8]
                dve.max(v8, PT[r % 2]).then_inc(ms["top"], 1)
                dve.wait_ge(ms["top"], 3 * r + 1 + base["top"])
                dve.max_index(i8, v8, PT[r % 2]).then_inc(ms["top"], 1)
                dve.match_replace(PT[1 - r % 2], v8, PT[r % 2], -1.0).then_inc(ms["top"], 1)
                dve.wait_ge(ms["top"], 3 * r + 3 + base["top"])
            dve.tensor_copy(idxf, idx8).then_inc(ms["top"], 1)
            dve.wait_ge(ms["top_mm"], 1 + base["top_mm"])
            dve.tensor_copy(idxT, ps[:, 4, 0:E]).then_inc(ms["idx"], 1)
            dve.tensor_copy(aff, ps[:, 5, 0:E]).then_inc(ms["idx"], 1)
            dve.wait_ge(ms["idx"], 2 + base["idx"])
            dve.sem_inc(ms["hid"], 1)
            dve.sem_inc(ms["y"], 1)

            def hid(e):
                dve.wait_ge(ms["up"], e + 1 + base["up"])
                dve.wait_ge(ms["silu"], e + 1 + base["silu"])
                dve.wait_ge(ms["tph"], e + base["tph"]) if not isinstance(e, int) or e else None
                dve.tensor_tensor(HD, SG, pair(2), ALU.mult).then_inc(ms["hid"], 1)

            def y(e, u):
                dve.wait_ge(ms["down"], e + 2 + base["down"])
                dve.wait_ge(ms["scat_ok"], e + 1 + base["scat_ok"])
                dve.tensor_scalar(YS[u], pair(4), aff[:, ds(e, 1)], None, ALU.mult).then_inc(ms["y"], 1)

            hid(0)
            with dve.Fori(0, E // 2 - 1) as it:
                for u in range(2):
                    hid(it * 2 + u + 1)
                    y(it * 2 + u, u)
            hid(E - 1)
            y(E - 2, 0)
            y(E - 1, 1)

        moe_dve(0, 1)
        if stop <= 4:
            return
        stage_end(dve, 3)
        norm_dve(dve, 2, True)
        dve.sem_inc(e_pre, 2)
        dve.wait_ge(e_small, 48)
        dve.wait_ge(e_zero, 4)
        with dve.Fori(0, KT // 2) as it:
            for u in range(2):
                ch = it * 2 + u
                dve.wait_ge(e_sig, ch + 1)
                dve.scalar_tensor_tensor(pre_e[u][:, CF_TAPS // 2:CF_TAPS // 2 + T], pair(4 * u), ccol[:, ds(ch, 1)],
                                         sg_e[u], ALU.add, ALU.mult).then_inc(e_pre, 1)
                dve.wait_ge(e_pre, ch + 3)
                for j in range(CF_TAPS):
                    tap = dww[:, ds(ch, 1), j:j + 1].rearrange("p o j -> p (o j)")
                    last = U[:, ds(ch, 1), :].rearrange("p o n -> p (o n)") if j == CF_TAPS - 1 else acc_e
                    if j == 0:
                        ins = dve.tensor_scalar(last, pre_e[u][:, 0:T], tap, ccol[:, ds(ch + 2 * KT, 1)],
                                                ALU.mult, ALU.add)
                    else:
                        ins = dve.scalar_tensor_tensor(last, pre_e[u][:, j:j + T], tap, acc_e, ALU.mult, ALU.add)
                    ins.then_inc(e_chain, 1)
                    dve.wait_ge(e_chain, ch * CF_TAPS + j + 1)
                dve.sem_inc(e_conv, 1)
        dve.wait_ge(e_mean, 1)
        dve.tensor_scalar(mb, pair(0), 1.0 / D, None, ALU.mult).then_inc(e_mb, 1)
        dve.wait_ge(e_mb, 1)
        for k in range(KT):
            dve.tensor_tensor(U[:, k, :], U[:, k, :], mb, ALU.subtract).then_inc(e_xc, 1)
        dve.wait_ge(e_rb, 1)
        for k in range(KT):
            dve.tensor_tensor(U[:, k, :], U[:, k, :], rb, ALU.mult).then_inc(e_xn, 1)
        dve.wait_ge(e_bias, NT)
        for t in range(NT):
            dve.wait_ge(e_pw2, t + 1)
            dve.tensor_tensor(X[:, t, :], X[:, t, :], pair(4 + 2 * (t % 2)), ALU.add).then_inc(e_add, 1)
        moe_dve(1, 3)
        stage_end(dve, 4)
        norm_dve(dve, 4, False)

    @block.tensor
    def _(pe):
        pe.wait_ge(s_cst, 32)
        norm_pe(pe, 0)
        pe.wait_ge(b_small, 48)
        pe.wait_ge(ht_done[0], NT + 2)
        for n in range(2):
            for half_ in range(2):
                for k in range(KT):
                    last = pe.matmul(ps[0:E, 4 + 2 * n + half_, :], wg[:, n, k * E:(k + 1) * E],
                                     HT[:, k, half_ * HALF:(half_ + 1) * HALF], start=(k == 0), stop=(k == KT - 1))
            last.then_inc(gate_mm, 1)

        def b_step(m, u, now, prev, prev2):
            if now:
                pe.wait_ge(w_loaded[u], m // 2 * 16 + 16 if isinstance(m, int) else (m - u) * 8 + 16)
                if prev2:
                    pe.wait_ge(evac_done, m - 1)
                for half_ in range(2):
                    for k in range(KT):
                        last = pe.matmul(ps[:, 2 * u + half_, :], wq[u][:, k, :],
                                         HT[:, k, half_ * HALF:(half_ + 1) * HALF], start=(k == 0), stop=(k == KT - 1))
                last.then_inc(proj_done, 1)
            if prev:
                p = m - 1
                pe.wait_ge(sqb_done, p + 1)
                if prev2:
                    pe.wait_ge(lnr_done, p)
                else:
                    pe.wait_ge(gate_steps, 1)
                for half_ in range(2):
                    last = pe.matmul(ps[:, 4 + half_, :], ones, sqb[:, half_ * HALF:(half_ + 1) * HALF],
                                     start=True, stop=True)
                last.then_inc(sqmm_done, 1)
            if prev2:
                p = m - 2
                pe.wait_ge(mul_done, p + 1)
                pe.wait_ge(nat_done, p)
                for c in range(NT):
                    last = pe.transpose(pair(6)[:, c * P:(c + 1) * P], nrm[u][:, c * P:(c + 1) * P], ident)
                last.then_inc(tpq_done, 1)

        pe.sem_inc(tpq_done, 2)
        b_loop(pe, b_step)
        pe.wait_ge(evac_done, PROJ)
        pe.wait_ge(gate_steps, 4)
        for c in range(NT):
            pe.transpose(ps[:, 0, c * E:(c + 1) * E], lg[:, c * P:(c + 1) * P], ident[0:E, 0:E])
        for c in range(NT):
            last = pe.transpose(ps[:, 1, c * E:(c + 1) * E], bs[:, c * P:(c + 1) * P], ident[0:E, 0:E])
        last.then_inc(b2_pe, 1)
        pe.wait_ge(b2_act, 1)
        pe.wait_ge(s_gcst, 32)
        pe.wait_ge(nat_done, PROJ)
        pe.wait_ge(lnr_done, PROJ)
        for d in range(2):
            pe.matmul(ps[:, 2 + d, 0:NT * H].rearrange("p (c h) -> p c h", c=NT), uf[:, d * P:(d + 1) * P], lgn[:, :, d * H:(d + 1) * H],
                      start=True, stop=True)
        pe.matmul(ps[:, 4, 0:NT * E], ones, lgn.rearrange("p c n -> p (c n)"), start=True, stop=True).then_inc(b2_pe, 1)
        pe.wait_ge(b2_act, 5)
        for d in range(2):
            for c in range(NT):
                n = (d * NT + c) * P
                last = pe.transpose(ps[0:H, 4 + n // HALF, n % HALF:n % HALF + P], SC[:, d, c, 0, :], ident)
        last.then_inc(b2_pe, 1)
        if stop <= 1:
            return
        stage_end(pe, 1)
        for d in range(2):
            pe.sem_inc(PE[d], len(PE_STEPS))
        sel = gsel[0:H, :]
        pe.wait_ge(s_gcst, 48)

        with pe.Fori(0, NT // 2) as it:
            for u in range(2):
                i = it * 2 + u

                def decay(d):
                    c = i if d == 0 else i * -1 + (NT - 1)
                    pe.wait_ge(VE[d], at(DVE_STEPS, "o", i, 1))
                    for h in range(H):
                        last = pe.matmul(pair(4 * d)[:, h * P:(h + 1) * P], sel[:, h * P:(h + 1) * P],
                                         GCT[0:H, ds((c + d * NT) * P, P)], start=(h % 4 == 0), stop=(h % 4 == 3),
                                         skip_group_check=True)
                    last.then_inc(PE[d], 1)

                def products(d, name, lhs, rhs, base, n=P, off=0):
                    per = HALF // n
                    for h in range(H):
                        last = pe.matmul(pair(base)[:, h * n:(h + 1) * n] if off == 0 else
                                         pair(base)[:, off + h * n:off + (h + 1) * n],
                                         lhs[:, h, :], rhs[:, h], start=True, stop=True, skip_group_check=True)
                    last.then_inc(PE[d], 1)

                for d in range(2):
                    decay(d)
                for d in range(2):
                    q_t, k_t, k_n, v_n = loads[u][d]
                    pe.wait_ge(c_ld[d][u], it * 64 + 64)
                    pe.wait_ge(VE[d], at(DVE_STEPS, "s", i, 1))
                    products(d, "kk", k_t, k_t, 4 * d + 2)
                    pe.wait_ge(VE[d], at(DVE_STEPS, "arg", i))
                    products(d, "qk", k_t, q_t, 4 * d)
                for d in range(2):
                    pe.wait_ge(VE[d], at(DVE_STEPS, "xt0", i))
                    for h in range(H):
                        last = pe.transpose(pair(4 * d + 2)[:, h * P:(h + 1) * P], XT[d][:, h, :], ident)
                    last.then_inc(PE[d], 1)

                def p_step(d, j):
                    if j == 0:
                        pe.wait_ge(AE[d], at(ACT_STEPS, "x0", i))
                    else:
                        pe.wait_ge(VE[d], at(DVE_STEPS, f"x{j - 1}", i))
                    products(d, "p", MT[d], blocks(XM[d], d, j), 4 * d, P // 2)

                for d in range(2):
                    p_step(d, 0)
                for j in range(LEVELS):
                    for d in range(2):
                        pe.wait_ge(VE[d], at(DVE_STEPS, f"pn{j}", i))
                        if j:
                            pe.wait_ge(AE[d], at(ACT_STEPS, f"t{j - 1}", i))
                        products(d, "xp", XT[d], PN[d], 4 * d, P // 2, HALF)
                    for d in range(2):
                        if j < LEVELS - 1:
                            p_step(d, j + 1)
                        else:
                            pe.wait_ge(VE[d], at(DVE_STEPS, f"x{j}", i))
                        for h in range(H):
                            last = pe.transpose(pair(4 * d + 2)[:, h * P:(h + 1) * P], XM[d][:, h, :], ident)
                        last.then_inc(PE[d], 1)
                for d in range(2):
                    q_t, k_t, k_n, v_n = loads[u][d]
                    products(d, "ks", k_t, ST[d], 4 * d)
                    pe.wait_ge(AE[d], at(ACT_STEPS, f"t{LEVELS - 1}", i))
                    products(d, "qs", q_t, ST[d], 4 * d + 2)
                for d in range(2):
                    pe.wait_ge(VE[d], at(DVE_STEPS, "r", i))
                    products(d, "xr", XT[d], dec[d], 4 * d)
                for d in range(2):
                    pe.wait_ge(AE[d], at(ACT_STEPS, "vn", i))
                    products(d, "iv", intra[d], VN[d], 4 * d)
                for d in range(2):
                    q_t, k_t, k_n, v_n = loads[u][d]
                    pe.wait_ge(AE[d], at(ACT_STEPS, "oq", i))
                    pe.wait_ge(PL[d], i + 2)
                    products(d, "kv", k_n, XM[d], 4 * d + 2)
        if stop <= 2:
            return
        stage_end(pe, 2)

        pe.sem_inc(d_tp, 2)
        pe.sem_inc(d_mm, 2)
        pe.wait_ge(wo_loaded, 32)

        def d_step(c, u, now, prev):
            if now:
                pe.wait_ge(d_og, c + 3)
                pe.wait_ge(d_ot, c + 1)
                for k in range(KT):
                    last = pe.transpose(pair(0)[:, k * P:(k + 1) * P], og[:, u, k * P:(k + 1) * P], ident)
                last.then_inc(d_tp, 1)
            if prev:
                p, w = c - 1, 1 - u
                pe.wait_ge(d_ot, p + 2)
                pe.wait_ge(d_add, p) if not isinstance(p, int) or p else None
                for half_ in range(2):
                    for k in range(KT):
                        last = pe.matmul(ps[:, 4 + 2 * w + half_, :], ot[w][:, k, :],
                                         wo[:, k, half_ * HALF:(half_ + 1) * HALF], start=(k == 0), stop=(k == KT - 1))
                last.then_inc(d_mm, 1)

        skewed(pe, d_step)

        def moe_pe(l, n):
            base = first_layers(l)
            norm_pe(pe, n)
            pe.wait_ge(ht_done[n], NT + 2)
            pe.wait_ge(wr_loaded, 16 * (l + 1))
            for t in range(NT):
                for k in range(KT):
                    last = pe.matmul(ps[:, 0, t * E:(t + 1) * E], HT[:, k, t * P:(t + 1) * P], wr[:, k, :],
                                     start=(k == 0), stop=(k == KT - 1))
            last.then_inc(ms["logits"], 1)
            pe.wait_ge(ms["soft"], 5 + base["soft"])
            for t in range(NT):
                last = pe.transpose(ps[0:E, 2 + t // 4, t % 4 * P:(t % 4 + 1) * P], pr[:, t, :], ident)
            last.then_inc(ms["pt_mm"], 1)
            pe.wait_ge(ms["top"], 3 * (CAP // 8) + 1 + base["top"])
            pe.transpose(ps[:, 4, 0:E], idxf, ident[0:E, 0:E])
            pe.transpose(ps[:, 5, 0:E], vals, ident[0:E, 0:E]).then_inc(ms["top_mm"], 1)
            pe.sem_inc(ms["down"], 1)

            def tpx(e, u, slot_count):
                pe.wait_ge(ms[f"gath{u}"], slot_count + base[f"gath{u}"])
                for k in range(KT):
                    last = pe.transpose(pair(6)[:, k * P:(k + 1) * P], xin[u][:, k * P:(k + 1) * P], ident)
                last.then_inc(ms["tpx"], 1)

            def product(bank, lhs, w, half_):
                for k in range(KT):
                    last = pe.matmul(ps[:, bank + half_, :], lhs[:, k, :], w[:, k, half_ * HALF:(half_ + 1) * HALF],
                                     start=(k == 0), stop=(k == KT - 1))
                return last

            def gate(e, u, slot_count):
                pe.wait_ge(ms["xt"], e + 1 + base["xt"])
                pe.wait_ge(ms[f"wg{u}"], slot_count + base[f"wg{u}"])
                pe.wait_ge(ms["silu"], e + base["silu"]) if not isinstance(e, int) or e else None
                product(0, xT, WG[u], 0)
                product(0, xT, WG[u], 1).then_inc(ms["gate"], 1)

            def up(e, u, slot_count):
                pe.wait_ge(ms[f"wu{u}"], slot_count + base[f"wu{u}"])
                pe.wait_ge(ms["hid"], e + 1 + base["hid"])
                product(2, xT, WU[u], 0)
                product(2, xT, WU[u], 1).then_inc(ms["up"], 1)

            def tph(e):
                pe.wait_ge(ms["hid"], e + 2 + base["hid"])
                pe.wait_ge(ms["xt"], e + 2 + base["xt"])
                for k in range(KT):
                    last = pe.transpose(pair(6)[:, k * P:(k + 1) * P], HD[:, k * P:(k + 1) * P], ident)
                last.then_inc(ms["tph"], 1)

            def down(e, between):
                pe.wait_ge(ms["ht"], e + 1 + base["ht"])
                pe.wait_ge(ms["wd"], e * 16 + 16 + base["wd"])
                pe.wait_ge(ms["y"], e + 1 + base["y"])
                product(4, hT, WD, 0)
                between()
                product(4, hT, WD, 1).then_inc(ms["down"], 1)

            pe.wait_ge(ms["idx"], 2 + base["idx"])
            tpx(0, 0, 16)
            gate(0, 0, 16)
            up(0, 0, 16)
            tpx(1, 1, 16)
            with pe.Fori(0, E // 2 - 1) as it:
                for u in range(2):
                    e = it * 2 + u
                    nxt = it * 16 + 16 * (1 + u)
                    gate(e + 1, 1 - u, nxt)
                    tph(e)
                    up(e + 1, 1 - u, nxt)

                    def next_x():
                        pe.wait_ge(ms["ht"], e + 1 + base["ht"])
                        tpx(e + 2, u, it * 16 + 32)
                    down(e, next_x)
            gate(E - 1, 1, 8 * E)
            tph(E - 2)
            up(E - 1, 1, 8 * E)
            down(E - 2, lambda: None)
            pe.wait_ge(ms["hid"], E + 1 + base["hid"])
            pe.wait_ge(ms["ht"], E - 1 + base["ht"])
            for k in range(KT):
                last = pe.transpose(pair(6)[:, k * P:(k + 1) * P], HD[:, k * P:(k + 1) * P], ident)
            last.then_inc(ms["tph"], 1)
            down(E - 1, lambda: None)

        moe_pe(0, 1)
        if stop <= 4:
            return
        stage_end(pe, 3)
        norm_pe(pe, 2)
        pe.wait_ge(ht_done[2], NT + 2)
        with pe.Fori(0, KT // 2) as it:
            for u in range(2):
                ch = it * 2 + u
                pe.wait_ge(e_w[u], it * 32 + 32)
                pe.wait_ge(e_pre, ch + 1)
                for n in range(2):
                    for half_ in range(2):
                        for k in range(KT):
                            last = pe.matmul(ps[:, 4 * u + 2 * n + half_, :], wag[u][n][:, k, :],
                                             HT[:, k, half_ * HALF:(half_ + 1) * HALF],
                                             start=(k == 0), stop=(k == KT - 1))
                last.then_inc(e_mm, 1)
        pe.wait_ge(e_conv, KT)
        for half_ in range(2):
            for k in range(KT):
                last = pe.matmul(ps[:, half_, :], ones, U[:, k, half_ * HALF:(half_ + 1) * HALF],
                                 start=(k == 0), stop=(k == KT - 1))
        last.then_inc(e_mean, 1)
        for k in range(KT):
            pe.wait_ge(e_sq, k + 1)
            for half_ in range(2):
                last = pe.matmul(ps[:, 2 + half_, :], ones, sq_e[:, half_ * HALF:(half_ + 1) * HALF],
                                 start=(k == 0), stop=(k == KT - 1))
            last.then_inc(e_sqmm, 1)
        pe.wait_ge(w2_loaded, 16)
        pe.wait_ge(e_u, KT)
        for t in range(NT):
            if t >= 2:
                pe.wait_ge(e_add, t - 1)
            for half_ in range(2):
                for k in range(KT):
                    last = pe.matmul(ps[:, 4 + 2 * (t % 2) + half_, :], U[:, k, t * P:(t + 1) * P],
                                     w2[:, k, half_ * HALF:(half_ + 1) * HALF], start=(k == 0), stop=(k == KT - 1))
            last.then_inc(e_pw2, 1)
        moe_pe(1, 3)
        stage_end(pe, 4)


def laid_out(inputs):
    x = {k: np.asarray(v) for k, v in inputs.items()}
    w_in = x["dn_w_in"][0]
    gates = w_in[:, 4 * D:].reshape(KT, P, 2, 2, H)
    tiled = lambda w: np.ascontiguousarray(w.reshape(KT, P, -1, P).transpose(2, 1, 0, 3))
    cols = lambda v: np.ascontiguousarray(v.reshape(-1, P).T)
    return {
        "x": x["x"][0],
        "consts": constants(),
        "norm_mix": x["norm_mix"], "norm_ffn": x["norm_ffn"], "final_norm": x["final_norm"],
        "w_in": tiled(w_in[:, :4 * D]),
        "w_gates": np.ascontiguousarray(gates[:, :, :, ::-1].transpose(1, 3, 0, 2, 4)).reshape(P, 2, KT * 2 * H),
        "conv_w": np.ascontiguousarray(x["dn_conv_w"][0].reshape(TAPS, 3 * H, P).transpose(2, 1, 0)),
        "gate_bias": np.stack([x["dn_a_log"][0].reshape(-1), x["dn_dt_bias"][0].reshape(-1)], 1),
        "dn_norm_w": x["dn_norm_w"][0],
        "dn_w_out": x["dn_w_out"][0],
        "w_pw1": tiled(x["cf_w_pw1"][0]),
        "cf_cols": np.concatenate([cols(x["cf_b_pw1"][0]), cols(x["cf_dw_b"][0]), cols(x["cf_ln_g"][0]),
                                   cols(x["cf_ln_b"][0])], 1),
        "cf_dw_w": np.ascontiguousarray(x["cf_dw_w"][0].reshape(CF_TAPS, KT, P).transpose(2, 1, 0)),
        "w_pw2": x["cf_w_pw2"][0],
        "b_pw2": x["cf_b_pw2"][0],
        "w_router": np.ascontiguousarray(x["moe_w_router"].reshape(2, KT, P, E).transpose(0, 2, 1, 3)),
        "w_gate": x["moe_w_gate"], "w_up": x["moe_w_up"], "w_down": x["moe_w_down"],
    }


def kernel(**inputs):
    import concourse.bacc as bacc
    from concourse.bass_utils import run_bass_kernel_spmd

    nc = bacc.Bacc("TRN2", target_bir_lowering=False, num_devices=1)
    arrays = laid_out(inputs)
    aps = {n: nc.dram_tensor(f"in_{n}", v.shape, mybir.dt.from_np(v.dtype), kind="ExternalInput").ap()
           for n, v in arrays.items()}
    out = nc.dram_tensor("out", (1, T, D), F32, kind="ExternalOutput").ap()
    build(nc, aps, out)
    r = run_bass_kernel_spmd(nc, [{f"in_{n}": v for n, v in arrays.items()}], core_ids=[0])
    return r.results[0]["out"]
```

```python
from contextlib import ExitStack

import numpy as np
import concourse.bass as bass
from concourse import mybir

P = 128
T = 1024
D = 1024
NT = T // P
KT = D // P
H = 8
TAPS = 5
CF_TAPS = 31
E = 16
CAP = 2 * T // E
EPS = 1e-6
HALF = 512
LEVELS = 6
PROJ = 4 * H
NEG = -1e30

ALU = mybir.AluOpType
ACT = mybir.ActivationFunctionType
AX = mybir.AxisListType
F32 = mybir.dt.float32
F32R = mybir.dt.float32r
U32 = mybir.dt.uint32
ds = bass.ds

C_IDENT, C_ONES, C_UF, C_UB, C_NEGF, C_NEGB, C_M0F, C_M0B = (P * n for n in range(8))
C_LM = 8 * P
C_END = C_LM + 2 * LEVELS * (P // 2)


def constants():
    c = np.zeros((P, C_END), np.float32)
    r, t = np.arange(P)[:, None], np.arange(P)[None, :]
    c[:, C_IDENT:C_IDENT + P] = r == t
    c[:, C_ONES:C_ONES + P] = 1.0
    c[:, C_UF:C_UF + P] = r <= t
    c[:, C_UB:C_UB + P] = r >= t
    c[:, C_NEGF:C_NEGF + P] = np.where(t >= r, 0.0, NEG)
    c[:, C_NEGB:C_NEGB + P] = np.where(t <= r, 0.0, NEG)
    c[:, C_M0F:C_M0F + P] = -1.0 * ((t == r + 1) & (r % 2 == 0))
    c[:, C_M0B:C_M0B + P] = -1.0 * ((t == r - 1) & (r % 2 == 1))
    for d in range(2):
        for j in range(LEVELS):
            b = 2 << j
            cols = (t[0] // b) % 2 == d
            block = t[0][cols] // b
            partner = block + 1 if d == 0 else block - 1
            a = C_LM + (d * LEVELS + j) * (P // 2)
            c[:, a:a + P // 2] = -1.0 * ((r // b) == partner[None, :])
    return c


MERGES = range(LEVELS)
PE_INV = ["kk", "qk", "x0", "p0"] + [s for j in MERGES for s in
         ((f"xp{j}", f"p{j + 1}", f"t{j}") if j < LEVELS - 1 else (f"xp{j}", f"t{j}"))]
DVE_INV = ["mt", "xa", "xt0"] + [s for j in MERGES for s in (f"pn{j}", f"x{j}")]
ACT_INV = ["qk", "x0"] + [f"t{j}" for j in MERGES]
PE_SCAN = ["qs", "ks", "xr", "iv", "kv"]
DVE_SCAN = ["r", "o", "s"]
ACT_SCAN = ["oq", "vn"]
AHEAD = 2


def chunk_schedule():
    scan = [(s, d) for s in PE_SCAN for d in range(2)]
    order = [("kk", 0), ("kk", 1), scan.pop(0), ("qk", 0), scan.pop(0), ("x0", 0), ("qk", 1), ("p0", 0), ("x0", 1),
             ("xp0", 0), ("p0", 1), scan.pop(0), ("xp0", 1)]
    for j in MERGES:
        if j:
            order += [("arg", 0)] if j == LEVELS - 1 else []
            order += [(f"xp{j}", d) for d in range(2)]
            order += [scan.pop(0)] if scan else []
        for d in range(2):
            order += [(f"p{j + 1}", d)] if j < LEVELS - 1 else []
            order += [(f"t{j}", d)]
        order += [scan.pop(0)] if scan else []
    order += [("arg", 1)]
    return order


SCHEDULE = chunk_schedule()


def at(steps, name, i, before=0):
    return (i + AHEAD - before) * len(steps) + steps.index(name) + 1


def build(nc, a, out, dbg=None):
    ctx = ExitStack()
    with ctx:
        _build(nc, ctx, a, out, dbg or {})


def _build(nc, ctx, a, out, dbg):
    def sem(name):
        return ctx.enter_context(nc.semaphore(name))

    def sems(name, n):
        return [sem(f"{name}{i}") for i in range(n)]

    qk_t = nc.dram_tensor("qk_t", (2 * H, P, T), F32, kind="Internal").ap()
    nat = nc.dram_tensor("nat", (NT, P, PROJ, P), F32, kind="Internal").ap()
    gc_d = nc.dram_tensor("gc_d", (2, NT, H, P), F32, kind="Internal").ap()
    o_dir = nc.dram_tensor("o_dir", (2, NT, P, D), F32, kind="Internal").ap()
    hn_d = [nc.dram_tensor(f"hn_d{l}", (T, D), F32, kind="Internal").ap() for l in range(2)]
    acc_d = [nc.dram_tensor(f"acc_d{l}", (T, D), F32, kind="Internal").ap() for l in range(2)]

    K = 256
    with ExitStack() as below:
        below.enter_context(nc.sbuf_tensor("below", [P, 64 * K], F32))
        HR = below.enter_context(nc.sbuf_tensor("stream_parts", [P, 2, KT, T], F32R))
        WR = below.enter_context(nc.sbuf_tensor("weight_parts", [P, 2, 2, KT, P], F32R))
        GR = below.enter_context(nc.sbuf_tensor("gate_parts", [P, 2, KT, P], F32R))
    arena = ctx.enter_context(nc.sbuf_tensor("arena", [P, 196 * K], F32))
    cst = ctx.enter_context(nc.sbuf_tensor("cst", [P, 2 * P], F32))
    gain = ctx.enter_context(nc.sbuf_tensor("gain", [P, D], F32))
    small = ctx.enter_context(nc.sbuf_tensor("small", [P, 256], F32))
    idxu = ctx.enter_context(nc.sbuf_tensor("idxu", [P, E + CAP + 4], U32))
    ps = ctx.enter_context(nc.psum_tensor("ps", [P, 8, HALF], F32))

    def part(kib, n):
        at = int(kib * K)
        assert at + n <= 196 * K
        return arena[:, at:at + n]

    def tiles(kib, n, w):
        return part(kib, n * w).rearrange("p (n w) -> p n w", n=n)

    def pair(b):
        return ps[:, b:b + 2, :].rearrange("p b n -> p (b n)")

    def heads(ap):
        return ap.rearrange("p (h n) -> p h n", h=H)

    ident, ones = cst[:, 0:P], cst[:, P:2 * P]
    X = tiles(128, NT, D)
    HT = tiles(96, KT, T)
    xs = tiles(160, 2, D)
    junk = part(168, D)

    ss, rstd = small[:, 0:8], small[:, 8:16]
    epsb = small[:, 16:17]
    lnq = small[:, 17:19]

    def in_parts(pe, out, lhs, rhs):
        parts = ((0, 0), (0, 1), (1, 0))
        for k in range(KT):
            for n, (a_, b_) in enumerate(parts):
                last = pe.matmul(out, lhs[:, a_, k, :], rhs(b_, k), start=(k == 0 and n == 0),
                                 stop=(k == KT - 1 and n == len(parts) - 1))
        return last

    s_cst, s_x, s_eps = sem("constants_loaded"), sem("x_loaded"), sem("eps_set")
    gain_loaded, gain_used = sem("gain_loaded"), sem("gain_used")
    stage_done = sem("stage_done")

    def stage_end(eng, n):
        eng.drain().then_inc(stage_done, 1)
        eng.wait_ge(stage_done, 4 * n)

    sq_done, ln_done, rstd_done = sem("sq_done"), sem("ln_done"), sem("rstd_done")
    xs_done, tp_done, ht_done = sem("xs_done"), sem("tp_done"), sem("ht_done")
    hi_done = sem("high_parts_done")
    acc_stored = sems("acc_stored", 2)
    hn_stored = sems("hn_stored", 2)

    def before(n, what):
        if what == "hn_stored":
            return (16 * (NT // 2) + 16) * (0, 0, 1, 1, 2)[n]
        return n * {"sq_done": NT + 1, "ln_done": 1, "rstd_done": 1, "xs_done": NT, "tp_done": NT + 2,
                    "ht_done": NT + 2}[what]

    gains = [a["norm_mix"][0], a["norm_ffn"][0], a["norm_mix"][1], a["norm_ffn"][1], a["final_norm"]]

    def norm_act(act, n, transpose, parts=False):
        act.sem_inc(sq_done, 1)
        if transpose and not parts:
            act.sem_inc(ht_done, 2)
        with act.Fori(0, NT) as t:
            act.wait_ge(sq_done, t + 1 + before(n, "sq_done"))
            act.activation(junk, X[:, ds(t, 1), :].rearrange("p o n -> p (o n)"), ACT.Square,
                           accum_out=ss[:, ds(t, 1)]).then_inc(sq_done, 1)
        act.wait_ge(sq_done, NT + 1 + before(n, "sq_done"))
        act.activation(rstd, ss, ACT.Ln, scale=1.0 / D, bias=epsb).then_inc(ln_done, 1)
        act.wait_ge(ln_done, 1 + before(n, "ln_done"))
        act.activation(rstd, rstd, ACT.Exp, scale=-0.5).then_inc(rstd_done, 1)
        if transpose:
            with act.Fori(0, NT // 2) as it:
                for u in range(2):
                    t = it * 2 + u
                    act.wait_ge(tp_done, t + 3 + before(n, "tp_done"))
                    dst = HR[:, 0, :, ds(t * P, P)] if parts else HT[:, :, ds(t * P, P)]
                    act.activation(dst, pair(2 * u).rearrange("p (k n) -> p k n", k=KT), ACT.Copy
                                   ).then_inc(hi_done if parts else ht_done, 1)

    def norm_dve_parts(dve, n):
        dve.wait_ge(gain_loaded, 16 * (n + 1))
        dve.wait_ge(rstd_done, 1 + before(n, "rstd_done"))
        dve.sem_inc(ht_done, 2)

        def scaled(t, u):
            dve.wait_ge(tp_done, t + 1 + before(n, "tp_done"))
            dve.scalar_tensor_tensor(xs[:, u, :], X[:, ds(t, 1), :].rearrange("p o n -> p (o n)"),
                                     rstd[:, ds(t, 1)], gain[:, :], ALU.mult, ALU.mult).then_inc(xs_done, 1)

        def low(t, u):
            dve.wait_ge(hi_done, t + 1)
            dve.tensor_tensor(HR[:, 1, :, ds(t * P, P)], pair(2 * u).rearrange("p (k n) -> p k n", k=KT),
                              HR[:, 0, :, ds(t * P, P)], ALU.subtract).then_inc(ht_done, 1)

        scaled(0, 0)
        with dve.Fori(0, NT // 2 - 1) as it:
            for u in range(2):
                scaled(it * 2 + u + 1, 1 - u)
                low(it * 2 + u, u)
        scaled(NT - 1, 1)
        low(NT - 2, 0)
        low(NT - 1, 1)
        dve.sem_inc(gain_used, 1)

    def norm_dve(dve, n, transpose):
        dve.wait_ge(gain_loaded, 16 * (n + 1))
        dve.wait_ge(rstd_done, 1 + before(n, "rstd_done"))
        with dve.Fori(0, NT // 2) as it:
            for u in range(2):
                t = it * 2 + u
                if transpose:
                    dve.wait_ge(tp_done, t + 1 + before(n, "tp_done"))
                if n % 2 == 1 or n == 4:
                    dve.wait_ge(hn_stored[u], it * 16 + 16 + before(n, "hn_stored"))
                dve.scalar_tensor_tensor(xs[:, u, :], X[:, ds(t, 1), :].rearrange("p o n -> p (o n)"),
                                         rstd[:, ds(t, 1)], gain[:, :], ALU.mult, ALU.mult).then_inc(xs_done, 1)
        dve.wait_ge(xs_done, NT + before(n, "xs_done"))
        dve.sem_inc(gain_used, 1)

    def norm_pe(pe, n):
        pe.sem_inc(tp_done, 2)
        with pe.Fori(0, NT // 2) as it:
            for u in range(2):
                t = it * 2 + u
                pe.wait_ge(xs_done, t + 1 + before(n, "xs_done"))
                pe.wait_ge(ht_done, t + 1 + before(n, "ht_done"))
                for k in range(KT):
                    last = pe.transpose(pair(2 * u)[:, k * P:(k + 1) * P], xs[:, u, k * P:(k + 1) * P], ident)
                last.then_inc(tp_done, 1)

    def norm_store(sp, n, dram):
        for u in range(2):
            sp.sem_inc(hn_stored[u], 16)
        with sp.Fori(0, NT // 2) as it:
            for u in range(2):
                t = it * 2 + u
                sp.wait_ge(xs_done, t + 1 + before(n, "xs_done"))
                sp.dma_start(dram[ds(t * P, P), :], xs[:, u, :]).then_inc(hn_stored[u], 16)

    def load_gain(sp, n):
        if n:
            sp.wait_ge(gain_used, n)
        sp.dma_start(gain[:, :], gains[n].partition_broadcast(P)).then_inc(gain_loaded, 16)

    wq = [part(4 * u, D).rearrange("p (k c) -> p k c", k=KT) for u in range(2)]
    PADW = T + TAPS - 1
    pre = [part(8 + 5 * u, PADW) for u in range(2)]
    cv = [part(18 + 4 * u, T) for u in range(2)]
    sl = [part(26 + 4 * u, T) for u in range(2)]
    nrm = [part(34 + 4 * u, T) for u in range(2)]
    natb = [part(42 + 4 * u, T).rearrange("p (c n) -> p c n", c=NT) for u in range(2)]
    sqb, rnb = part(50, T), part(54, T)
    wg = tiles(184, KT, P)
    cw = part(60, PROJ * TAPS).rearrange("p (m j) -> p m j", m=PROJ)
    nsc, nbi = part(61, PROJ), part(61.25, PROJ)
    abias = part(61.5, 4)
    ga, gn, ge, lg, bs = (part(at_, T)[0:E, :] for at_ in (160, 164, 168, 152, 156))
    lgn = part(172, NT * E).rearrange("p (c n) -> p c n", c=NT)
    btn = part(173, NT * E).rearrange("p (c n) -> p c n", c=NT)
    SCN = 6
    SC = part(174, 2 * NT * SCN * H).rearrange("p (d c k h) -> p d c k h", d=2, c=NT, k=SCN)
    tot = part(177, NT * E).rearrange("p (c d h) -> p c d h", c=NT, d=2)
    GCT = part(144, 2 * NT * P)

    uf = part(182, 2 * P)

    b_small, w_loaded = sem("b_small_loaded"), sems("w_loaded", 2)
    gate_mm, gate_steps, gate_acts = sem("gate_products"), sem("gate_dve_steps"), sem("gate_act_steps")
    b_zero, w_split, w_high, g_split = sem("b_tables_set"), sem("w_split"), sem("w_high"), sem("gate_w_split")
    proj_done, evac_done, conv_steps, conv_done = sem("proj_done"), sem("evac_done"), sem("conv_steps"), sem("conv_done")
    silu_done, sqb_done, sqmm_done, lnr_done, rn_done = (sem("silu_done"), sem("sqb_done"), sem("sqmm_done"),
                                                         sem("lnr_done"), sem("rn_done"))
    mul_done, tpq_done, nat_done = sem("mul_done"), sem("tpq_done"), sem("nat_done")
    t_stored, n_stored = sems("t_stored", 2), sems("n_stored", 2)
    b2_pe, b2_act, b2_dve = sem("scan_tables_pe"), sem("scan_tables_act"), sem("scan_tables_dve")

    NORMED = 2 * H

    def b_loop(eng, step):
        for m in range(2):
            step(m, m, True, m >= 1, False, (True, True, True))
        with eng.Fori(1, NORMED // 2) as it:
            for u in range(2):
                step(it * 2 + u, u, True, True, True, (True, True, True))
        step(NORMED, 0, True, True, True, (False, True, True))
        step(NORMED + 1, 1, True, True, True, (False, False, True))
        with eng.Fori(NORMED // 2 + 1, PROJ // 2 - 1) as it:
            for u in range(2):
                step(it * 2 + u, u, True, True, True, (False, False, False))
        for m in range(PROJ - 2, PROJ + 2):
            step(m, m % 2, m < PROJ, m < PROJ + 1, True, (False, False, False))

    loads = [[[tiles(32 * u + 16 * d + 4 * n, H, P) for n in range(4)] for d in range(2)] for u in range(2)]
    dec, MT, XM, VN, R, VS = ([tiles(64 + 42 * d + 4 * n, H, P) for d in range(2)] for n in range(6))
    intra, XT = ([[tiles(88 + 42 * d + 8 * n + 4 * u, H, P) for d in range(2)] for u in range(2)] for n in range(2))
    PN = [tiles(104 + 42 * d, H, P // 2) for d in range(2)]
    ST = [tiles(160, H, P), tiles(164, H, P)]
    OB = [tiles(168, H, P), tiles(178, H, P)]
    sc = [[part(172 + 0.5 * u + 0.25 * d, SCN * H).rearrange("p (k h) -> p k h", k=SCN) for d in range(2)]
          for u in range(2)]
    gmask = part(188, C_END - C_NEGF)

    def g(col, n=P):
        return gmask[:, col - C_NEGF:col - C_NEGF + n]

    PI, VI, AI = sems("inv_pe", 2), sems("inv_dve", 2), sems("inv_act", 2)
    PS, VC, AS, PL = sems("scan_pe", 2), sems("scan_dve", 2), sems("scan_act", 2), sems("scan_pool", 2)
    DG, EG = sems("decay_dve", 2), sems("decay_act", 2)
    GI, g_loaded = sems("intra_pool", 2), sems("decay_loaded", 2)
    c_ld = [sems(f"c_loaded{d}_", 2) for d in range(2)]
    o_stored = sems("o_stored", 2)
    s_gcst = sem("masks_loaded")

    def chunk(i, d):
        return i if d == 0 else i * -1 + (NT - 1)

    def interleaved(eng, inverse, scan):
        def both(i, u, k):
            for name, d in SCHEDULE:
                if name not in PE_SCAN and k is not None:
                    inverse(name, d, k, 1 - u)
                elif name in PE_SCAN and i is not None:
                    scan(name, d, i, u)

        both(None, 1, 0)
        with eng.Fori(0, NT // 2 - 1) as it:
            for u in range(2):
                both(it * 2 + u, u, it * 2 + u + 1)
        both(NT - 2, 0, NT - 1)
        both(NT - 1, 1, None)

    def blocks(ap, d, j):
        b = 2 << j
        v = ap.rearrange("p h (n two b) -> p h n two b", two=2, b=b)
        return v[:, :, :, d, :]

    def half(ap, j):
        return ap.rearrange("p h (n b) -> p h n b", b=2 << j)

    wo = tiles(0, KT, D)
    of, ob, sz, og = (tiles(32 + 8 * i, 2, D) for i in range(4))
    ot = [tiles(64 + 4 * u, KT, P) for u in range(2)]
    sqd = part(72, D)
    nw = part(76, P)
    ssd = small[:, 24:40].rearrange("p (u h) -> p u h", u=2)
    wo_loaded, nw_loaded, d_loaded = sem("wo_loaded"), sem("nw_loaded"), sems("d_loaded", 2)
    d_sum, d_sq, d_ss, d_ln, d_ro, d_og = (sem("d_sum"), sem("d_sq"), sem("d_ss"), sem("d_ln"), sem("d_ro"), sem("d_og"))
    d_chain, d_tp, d_ot, d_mm, d_add = sem("d_chain"), sem("d_tp"), sem("d_ot"), sem("d_mm"), sem("d_add")

    def skewed(eng, step):
        step(0, 0, True, False)
        step(1, 1, True, True)
        with eng.Fori(1, NT // 2) as it:
            for u in range(2):
                step(it * 2 + u, u, True, True)
        step(NT, 0, False, True)

    EPAD = T + CF_TAPS - 1
    wag = [[part(8 * u + 4 * n, D).rearrange("p (k c) -> p k c", k=KT) for n in range(2)] for u in range(2)]
    pre_e = [part(16 + 5 * u, EPAD) for u in range(2)]
    sg_e = [part(26, T), part(182, T)]
    POOL_TAPS = 11
    CHAIN = CF_TAPS - POOL_TAPS
    prod_e, sum_e = [part(172, T), part(186, T)], [part(168, T), part(190, T)]
    acc_e = [part(160, T), part(164, T)]
    U = tiles(32, KT, T)
    w2 = tiles(64, KT, D)
    sq_e = part(164, T)
    mb, rb = part(168, T), part(172, T)
    dww = part(176, KT * CF_TAPS).rearrange("p (m j) -> p m j", m=KT)
    ccol = part(177, 5 * KT)
    b2b = part(178, D)
    e_small, e_w, w2_loaded = sem("e_small_loaded"), sems("e_w_loaded", 2), sem("w2_loaded")
    e_mm, e_sig, e_pre, e_chain, e_conv, e_zero = (sem("e_mm"), sem("e_sig"), sem("e_pre"), sem("e_chain"),
                                                   sem("e_conv"), sem("e_zero"))
    e_prod, e_padd = sem("e_tap_product"), sem("e_tap_added")
    e_mean, e_mb, e_xc, e_sq, e_sqmm, e_ln, e_rb, e_xn, e_u = (
        sem("e_mean"), sem("e_mb"), sem("e_centred"), sem("e_sq"), sem("e_sqmm"), sem("e_ln"), sem("e_rb"),
        sem("e_normed"), sem("e_u"))
    e_pw2, e_add, e_bias = sem("e_pw2"), sem("e_add"), sem("e_bias_added")

    WG = [tiles(0, KT, D), tiles(64, KT, D)]
    WU = [tiles(32, KT, D), tiles(96, KT, D)]
    WD = tiles(128, KT, D)
    xin = [part(160 + 4 * u, D) for u in range(2)]
    xT = tiles(168, KT, P)
    SG, HD, hT, YS = part(172, D), part(176, D), tiles(180, KT, P), [part(184 + 4 * u, D) for u in range(2)]
    PT = [part(172, T)[0:E, :], part(176, T)[0:E, :]]
    top = ctx.enter_context(nc.sbuf_tensor("top", [P, 5 * P], F32))
    wr = top[:, 0:P].rearrange("p (k e) -> p k e", k=KT)
    pr = top[:, P:2 * P].rearrange("p (t e) -> p t e", t=NT)
    vals, idxf = top[0:E, 2 * P:3 * P], top[0:E, 3 * P:4 * P]
    aff = top[:, 4 * P:4 * P + E]
    mx, sm, rs = small[:, 40:48], small[:, 48:56], small[:, 56:64]
    idxT, idx8 = idxu[:, 0:E], idxu[0:E, E:E + CAP]
    idg, ids = [idxu[:, E + CAP + u:E + CAP + u + 1] for u in range(2)], [idxu[:, E + CAP + 2:E + CAP + 3]] * 2

    wr_loaded, passed = sem("wr_loaded"), sem("passed")
    LAYER = {"logits": 1, "soft": 5, "exp": 1, "pt_mm": 1, "pt": 1, "top": 3 * (CAP // 8) + 1, "top_mm": 1, "idx": 2,
             "wu0": 8 * E, "wu1": 8 * E, "wg0": 8 * E, "wg1": 8 * E, "wd": 16 * E, "gath0": 8 * E, "gath1": 8 * E,
             "idg": 2 * E, "scat": 16 * E, "scat_ok": E + 2, "tpx": E, "xt": E, "gate": E, "up": E, "silu": E,
             "hid": E + 1, "tph": E, "ht": E, "down": E + 1, "y": E + 1}
    ms = {n: sem(f"m_{n}") for n in LAYER}

    def first_layers(l):
        return {n: l * v for n, v in LAYER.items()}

    block = ctx.enter_context(nc.Block())
    stop = dbg.get("stop", 99)

    @block.sync
    def _(sp):
        for n in range(2):
            sp.dma_start(cst[:, n * P:(n + 1) * P], a["consts"][:, n * P:(n + 1) * P]).then_inc(s_cst, 16)
        sp.dma_start(X, a["x"].rearrange("(t p) d -> p t d", p=P)).then_inc(s_x, 16)
        load_gain(sp, 0)
        sp.dma_start(wg, a["w_gates"]).then_inc(b_small, 16)
        sp.dma_start(cw[:, 0:3 * H, :], a["conv_w"]).then_inc(b_small, 16)
        sp.dma_start(abias[0:E, 0:2], a["gate_bias"]).then_inc(b_small, 16)
        sp.dma_start(gmask, a["consts"][:, C_NEGF:C_END]).then_inc(s_gcst, 16)
        sp.dma_start(uf, a["consts"][:, C_UF:C_UF + 2 * P]).then_inc(s_gcst, 16)
        for u in range(2):
            sp.sem_inc(t_stored[u], 16)
            sp.sem_inc(n_stored[u], 16)
        for m in range(2):
            sp.dma_start(wq[m], a["w_in"][m]).then_inc(w_loaded[m], 16)

        def b_reload(m, u):
            sp.wait_ge(w_split, m + 1)
            sp.dma_start(wq[u], a["w_in"][ds(m + 2, 1)].rearrange("o p k c -> (o p) k c")).then_inc(w_loaded[u], 16)

        def b_stores(m, u, is_t, is_n):
            sp.wait_ge(mul_done, m + 1)
            if is_t:
                sp.dma_start(qk_t[ds(m, 1)].rearrange("o p t -> (o p) t"), nrm[u]).then_inc(t_stored[u], 16)
            else:
                sp.wait_ge(t_stored[u], (m - u) * 8 + 16)
                sp.sem_inc(t_stored[u], 16)
            sp.wait_ge(nat_done, m + 1)
            if is_n:
                sp.dma_start(nat[:, :, ds(m, 1), :].rearrange("c p o n -> p c (o n)"), natb[u]).then_inc(n_stored[u], 16)
            else:
                sp.wait_ge(n_stored[u], (m - u) * 8 + 16)
                sp.sem_inc(n_stored[u], 16)

        def b_range(lo, hi, is_t, is_n, load):
            with sp.Fori(lo // 2, hi // 2) as it:
                for u in range(2):
                    if load:
                        b_reload(it * 2 + u, u)
                    b_stores(it * 2 + u - 2, u, is_t, is_n)

        for m in range(2):
            b_reload(m, m)
        b_range(2, H + 2, True, False, True)
        b_range(H + 2, 2 * H + 2, True, True, True)
        b_range(2 * H + 2, PROJ - 2, False, True, True)
        b_range(PROJ - 2, PROJ + 2, False, True, False)
        for u in range(2):
            sp.wait_ge(t_stored[u], 8 * PROJ + 16)
            sp.wait_ge(n_stored[u], 8 * PROJ + 16)
        sp.wait_ge(b2_act, 16)
        sp.dma_start(gc_d.rearrange("d c h p -> h (d c) p"), GCT[0:H, :].rearrange("h (n p) -> h n p", p=P)
                     ).then_inc(s_gcst, 16)
        sp.wait_ge(s_gcst, 48)
        if stop <= 1:
            return
        sp.wait_ge(stage_done, 4 * 1)
        def c_decay(i):
            for d in range(2):
                sp.wait_ge(VI[d], at(DVE_INV, "mt", i, 1))
                sp.sem_inc(passed, 1)
                sp.wait_ge(GI[d], i)
                sp.dma_start(dec[d].rearrange("p h n -> p (h n)"),
                             gc_d[d][ds(chunk(i, d), 1)].rearrange("o h n -> (o h n)").partition_broadcast(P)
                             ).then_inc(g_loaded[d], 16)

        def c_load(i, u, d, parts):
            c = chunk(i, d)
            src = (qk_t[0:H, :, ds(c * P, P)].rearrange("h p t -> p h t"),
                   qk_t[H:2 * H, :, ds(c * P, P)].rearrange("h p t -> p h t"),
                   nat[ds(c, 1), :, H:2 * H, :].rearrange("o p h n -> (o p) h n"),
                   nat[ds(c, 1), :, 2 * H:3 * H, :].rearrange("o p h n -> (o p) h n"))
            for n in parts:
                sp.dma_start(loads[u][d][n], src[n]).then_inc(c_ld[d][u], 16)

        def c_store(i, d):
            sp.wait_ge(VC[d], at(DVE_SCAN, "o", i))
            sp.dma_start(o_dir[d][ds(chunk(i, d), 1)].rearrange("o p n -> (o p) n"),
                         OB[d].rearrange("p h n -> p (h n)")).then_inc(o_stored[d], 16)

        for d in range(2):
            sp.sem_inc(o_stored[d], 16)
            sp.dma_start(dec[d].rearrange("p h n -> p (h n)"),
                         gc_d[d][chunk(0, d)].rearrange("h n -> (h n)").partition_broadcast(P)).then_inc(g_loaded[d], 16)
        for d in range(2):
            c_load(0, 0, d, (1, 0, 3, 2))
        c_decay(1)
        for d in range(2):
            c_load(1, 1, d, (1, 0, 3, 2))
        with sp.Fori(0, NT // 2 - 1) as it:
            for u in range(2):
                i = it * 2 + u
                c_decay(i + 2)
                for d in range(2):
                    c_store(i, d)
                    c_load(i + 2, u, d, (1, 0, 3))
                for d in range(2):
                    sp.wait_ge(VC[d], at(DVE_SCAN, "s", i))
                    c_load(i + 2, u, d, (2,))
        for i in (NT - 2, NT - 1):
            for d in range(2):
                c_store(i, d)
        for d in range(2):
            sp.wait_ge(o_stored[d], 16 * (NT + 1))
        if stop <= 2:
            return
        sp.wait_ge(stage_done, 4 * 2)
        def d_load(c, u):
            for dst, src in ((of, o_dir[0][ds(c, 1)]), (ob, o_dir[1][ds(c, 1)]),
                             (sz, nat[ds(c, 1), :, 3 * H:PROJ, :].rearrange("o p h n -> o p (h n)"))):
                sp.dma_start(dst[:, u, :], src.rearrange("o p n -> (o p) n")).then_inc(d_loaded[u], 16)

        sp.dma_start(nw, a["dn_norm_w"].partition_broadcast(P)).then_inc(nw_loaded, 16)
        d_load(0, 0)
        sp.dma_start(wo, a["dn_w_out"].rearrange("(k p) n -> p k n", p=P)).then_inc(wo_loaded, 16)
        d_load(1, 1)
        sp.dma_start(X, a["x"].rearrange("(t p) d -> p t d", p=P)).then_inc(s_x, 16)
        with sp.Fori(1, NT // 2) as it:
            for u in range(2):
                c = it * 2 + u
                sp.wait_ge(d_og, c + 1)
                d_load(c, u)

        def moe_sp(l, n, x_done):
            base = first_layers(l)
            load_gain(sp, n)
            sp.dma_start(wr, a["w_router"][l]).then_inc(wr_loaded, 16)
            x_done(sp)
            sp.dma_start(acc_d[l].rearrange("(t p) d -> p t d", p=P), X).then_inc(acc_stored[l], 16)

            def load(w, e, dst, s):
                sp.dma_start(dst, a[w][l][ds(e, 1)].rearrange("o (k p) f -> p (o k) f", p=P)).then_inc(ms[s], 16)

            norm_store(sp, n, hn_d[l])
            load("w_gate", 0, WG[0], "wg0")
            load("w_up", 0, WU[0], "wu0")
            load("w_gate", 1, WG[1], "wg1")
            sp.wait_ge(ms["logits"], 1 + base["logits"])
            load("w_up", 1, WU[1], "wu1")
            sp.wait_ge(xs_done, NT + before(n, "xs_done"))
            sp.wait_ge(acc_stored[l], 16)
            with sp.Fori(0, E // 2 - 1) as it:
                for u in range(2):
                    e = it * 2 + u
                    sp.wait_ge(ms["down"], e + 1 + base["down"])
                    load("w_down", e, WD, "wd")
                    sp.wait_ge(ms["up"], e + 1 + base["up"])
                    load("w_gate", e + 2, WG[u], f"wg{u}")
                    load("w_up", e + 2, WU[u], f"wu{u}")
            for e in (E - 2, E - 1):
                sp.wait_ge(ms["down"], e + 1 + base["down"])
                load("w_down", e, WD, "wd")
            sp.wait_ge(ms["scat_ok"], E + 2 + base["scat_ok"])
            sp.wait_ge(ms["down"], E + 1 + base["down"])
            sp.dma_start(X, acc_d[l].rearrange("(t p) d -> p t d", p=P)).then_inc(s_x, 16)

        moe_sp(0, 1, lambda sp: sp.wait_ge(d_add, NT + 1))
        if stop <= 4:
            sp.wait_ge(s_x, 48)
            return
        sp.wait_ge(stage_done, 4 * 3)
        load_gain(sp, 2)
        for m in range(2):
            for n in range(2):
                sp.dma_start(wag[m][n], a["w_pw1"][m + KT * n]).then_inc(e_w[m], 16)
        sp.dma_start(dww, a["cf_dw_w"]).then_inc(e_small, 16)
        sp.dma_start(ccol, a["cf_cols"]).then_inc(e_small, 16)
        sp.dma_start(b2b, a["b_pw2"].partition_broadcast(P)).then_inc(e_small, 16)
        sp.dma_start(w2, a["w_pw2"].rearrange("(k p) n -> p k n", p=P)).then_inc(w2_loaded, 16)
        with sp.Fori(0, KT // 2 - 1) as it:
            for u in range(2):
                ch = it * 2 + u
                sp.wait_ge(e_mm, ch + 1)
                for n in range(2):
                    sp.dma_start(wag[u][n], a["w_pw1"][ds(ch + 2 + KT * n, 1)].rearrange("o p k c -> (o p) k c")
                                 ).then_inc(e_w[u], 16)
        moe_sp(1, 3, lambda sp: sp.wait_ge(e_add, NT))
        sp.wait_ge(stage_done, 4 * 4)
        load_gain(sp, 4)
        norm_store(sp, 4, out[0])
        for u in range(2):
            sp.wait_ge(hn_stored[u], 16 * (NT // 2 + 1) + before(4, "hn_stored"))

    @block.gpsimd
    def _(pool):
        pool.memset(epsb, EPS).then_inc(s_eps, 1)
        pool.memset(cw[:, 3 * H:PROJ, :], 0.0).then_inc(b_zero, 1)
        pool.wait_ge(b_zero, 1)
        pool.memset(cw[:, 3 * H:PROJ, TAPS // 2:TAPS // 2 + 1], 1.0).then_inc(b_zero, 1)
        pool.memset(nsc[:, 0:2 * H], -0.5).then_inc(b_zero, 1)
        pool.memset(nbi[:, 0:H], -0.5 * float(np.log(P))).then_inc(b_zero, 1)
        pool.memset(nbi[:, H:2 * H], 0.0).then_inc(b_zero, 1)
        for u in range(2):
            pool.memset(pre[u][:, 0:TAPS // 2], 0.0).then_inc(b_zero, 1)
            pool.memset(pre[u][:, T + TAPS // 2:PADW], 0.0).then_inc(b_zero, 1)
        if stop <= 1:
            return
        stage_end(pool, 1)
        for d in range(2):
            pool.sem_inc(PL[d], 2)

        def c_inverse(name, d, i, u):
            if name == "qk":
                pool.wait_ge(AI[d], at(ACT_INV, "qk", i))
                pool.tensor_tensor(intra[u][d], intra[u][d], dec[d], ALU.mult).then_inc(GI[d], 1)

        def c_scan(name, d, i, u):
            if name == "xr":
                pool.wait_ge(AS[d], at(ACT_SCAN, "vn", i))
                pool.tensor_tensor(VS[d], VN[d], sc[u][d][:, 2, :].unsqueeze(2).to_broadcast([P, H, P]), ALU.mult
                                   ).then_inc(PL[d], 1)

        interleaved(pool, c_inverse, c_scan)
        if stop <= 2:
            return
        stage_end(pool, 2)

        def moe_pool_run(l, n):
            base = first_layers(l)
            pool.wait_ge(ms["idx"], 2 + base["idx"])
            for u in range(2):
                pool.wait_ge(hn_stored[u], 16 * (NT // 2 + 1) + before(n, "hn_stored"))
            pool.wait_ge(acc_stored[l], 16)
            pool.sem_inc(ms["scat_ok"], 2)
            for u in range(2):
                pool.tensor_copy(idg[u], idxT[:, u:u + 1]).then_inc(ms["idg"], 1)
            pool.wait_ge(ms["idg"], 2 + base["idg"])
            for u in range(2):
                pool.indirect_dma_start(xin[u], None, hn_d[l], bass.IndirectOffsetOnAxis(ap=idg[u], axis=0)
                                        ).then_inc(ms[f"gath{u}"], 16)
            def gather(e, u, n_idg):
                pool.wait_ge(ms["tpx"], e - 1 + base["tpx"])
                pool.tensor_copy(idg[u], idxT[:, ds(e, 1)]).then_inc(ms["idg"], 1)
                pool.wait_ge(ms["idg"], n_idg + base["idg"])
                pool.sem_inc(passed, 1)
                pool.indirect_dma_start(xin[u], None, hn_d[l], bass.IndirectOffsetOnAxis(ap=idg[u], axis=0)
                                        ).then_inc(ms[f"gath{u}"], 16)

            def scatter(e, u, n_idg, first=False):
                if not first:
                    pool.wait_ge(ms["scat"], e * 16 + base["scat"])
                    pool.sem_inc(ms["scat_ok"], 1)
                pool.wait_ge(ms["y"], e + 2 + base["y"])
                pool.tensor_copy(ids[0], idxT[:, ds(e, 1)]).then_inc(ms["idg"], 1)
                pool.wait_ge(ms["idg"], n_idg + base["idg"])
                pool.sem_inc(passed, 1)
                pool.indirect_dma_start(acc_d[l], bass.IndirectOffsetOnAxis(ap=ids[0], axis=0), YS[u], None,
                                        compute_op=ALU.add).then_inc(ms["scat"], 16)

            for e in (2, 3):
                gather(e, e % 2, e + 1)
            for e in range(2):
                gather(e + 4, e, 2 * e + 5)
                scatter(e, e, 2 * e + 6, e == 0)
            with pool.Fori(1, E // 2 - 2) as it:
                for u in range(2):
                    e = it * 2 + u
                    gather(e + 4, u, e * 2 + 5)
                    scatter(e, u, e * 2 + 6)
            for e in range(E - 4, E):
                scatter(e, e % 2, E + e + 1)
            pool.wait_ge(ms["scat"], 16 * E + base["scat"])
            pool.sem_inc(ms["scat_ok"], 1)

        moe_pool_run(0, 1)
        if stop <= 4:
            return
        stage_end(pool, 3)
        for u in range(2):
            pool.memset(pre_e[u][:, 0:CF_TAPS // 2], 0.0).then_inc(e_zero, 1)
            pool.memset(pre_e[u][:, T + CF_TAPS // 2:EPAD], 0.0).then_inc(e_zero, 1)
        pool.wait_ge(e_small, 48)
        pool.wait_ge(xs_done, NT + before(2, "xs_done"))
        for t in range(NT):
            pool.tensor_tensor(X[:, t, :], X[:, t, :], b2b, ALU.add).then_inc(e_bias, 1)
        pool.sem_inc(e_padd, 1)
        with pool.Fori(0, KT // 2) as it:
            for u in range(2):
                ch = it * 2 + u
                pool.wait_ge(e_conv, ch + 1)
                for j in range(1, POOL_TAPS):
                    pool.wait_ge(e_prod, (ch + 2) * POOL_TAPS + j + 1)
                    pool.wait_ge(e_padd, ch * (POOL_TAPS - 1) + j)
                    pool.tensor_tensor(sum_e[u], prod_e[0] if j == 1 else sum_e[u], prod_e[j % 2], ALU.add
                                       ).then_inc(e_padd, 1)
        moe_pool_run(1, 3)
        stage_end(pool, 4)

    @block.scalar
    def _(act):
        act.wait_ge(s_eps, 1)
        act.wait_ge(s_x, 16)
        norm_act(act, 0, True, parts=True)
        act.wait_ge(b_small, 48)
        act.activation(abias[0:E, 2:3], abias[0:E, 0:1], ACT.Exp).then_inc(gate_acts, 1)
        act.wait_ge(gate_steps, 2)
        act.activation(ge, gn, ACT.Exp).then_inc(gate_acts, 1)
        act.wait_ge(gate_acts, 2)
        act.activation(ge, ge, ACT.Ln, bias=1.0).then_inc(gate_acts, 1)
        act.activation(bs, pair(4)[32:32 + E, :], ACT.Sigmoid).then_inc(gate_acts, 1)
        act.wait_ge(b_zero, 9)

        def b_step(m, u, now, prev, prev2, normed):
            if now:
                act.wait_ge(proj_done, m + 1)
                if prev2:
                    act.wait_ge(conv_done, m - 1)
                act.activation(pre[u][:, TAPS // 2:TAPS // 2 + T], pair(2 * u), ACT.Copy).then_inc(evac_done, 1)
            if prev and normed[1]:
                p = m - 1
                act.wait_ge(sqmm_done, p + 1)
                act.wait_ge(mul_done, p)
                act.activation(rnb, pair(4), ACT.Ln, bias=epsb).then_inc(lnr_done, 1)
                act.wait_ge(lnr_done, p + 1)
                act.activation(rnb, rnb, ACT.Exp, scale=nsc[:, ds(p, 1)], bias=nbi[:, ds(p, 1)]).then_inc(rn_done, 1)
            if now:
                act.wait_ge(conv_done, m + 1)
                if prev2:
                    act.wait_ge(mul_done, m - 1)
                    if not normed[2]:
                        act.wait_ge(tpq_done, m + 1)
                act.activation(sl[u], cv[u], ACT.Silu).then_inc(silu_done, 1)
                if normed[0]:
                    act.wait_ge(silu_done, m + 1)
                    if prev:
                        act.wait_ge(sqmm_done, m)
                    act.activation(sqb, sl[u], ACT.Square).then_inc(sqb_done, 1)
            if prev2:
                p = m - 2
                act.wait_ge(tpq_done, p + 3)
                act.wait_ge(n_stored[u], (p - u) * 8 + 16)
                act.activation(natb[u], pair(6).rearrange("p (c n) -> p c n", c=NT), ACT.Copy).then_inc(nat_done, 1)

        b_loop(act, b_step)
        act.wait_ge(b2_pe, 1)
        act.activation(lgn, ps[:, 0, 0:NT * E].rearrange("p (c n) -> p c n", c=NT), ACT.Copy).then_inc(b2_act, 1)
        act.activation(btn, ps[:, 1, 0:NT * E].rearrange("p (c n) -> p c n", c=NT), ACT.Copy).then_inc(b2_act, 1)
        act.wait_ge(b2_pe, 2)
        act.activation(tot.rearrange("p c d h -> p (c d h)"), ps[:, 4, 0:NT * E], ACT.Copy).then_inc(b2_act, 1)
        for d in range(2):
            act.activation(SC[:, d, :, 0, :], ps[:, 2 + d, 0:NT * H].rearrange("p (c h) -> p c h", c=NT), ACT.Copy
                           ).then_inc(b2_act, 1)
        act.wait_ge(b2_act, 5)
        for d in range(2):
            act.activation(SC[:, d, :, 1, :], SC[:, d, :, 0, :], ACT.Exp).then_inc(b2_act, 1)
            act.activation(SC[:, d, :, 3, :], tot[:, :, d, :], ACT.Exp).then_inc(b2_act, 1)
            act.activation(SC[:, d, :, 4, :], btn[:, :, d * H:(d + 1) * H], ACT.Copy).then_inc(b2_act, 1)
        act.wait_ge(b2_act, 11)
        act.wait_ge(b2_dve, 2)
        for d in range(2):
            act.activation(SC[:, d, :, 5, :], SC[:, d, :, 1, :], ACT.Copy, scale=-1.0).then_inc(b2_act, 1)
            act.activation(SC[:, d, :, 2, :], SC[:, d, :, 2, :], ACT.Exp).then_inc(b2_act, 1)
        act.wait_ge(b2_pe, 3)
        act.activation(GCT[0:H, :], ps[0:H, 4:8, :].rearrange("p b n -> p (b n)"), ACT.Copy).then_inc(b2_act, 1)
        if stop <= 1:
            return
        stage_end(act, 1)
        for d in range(2):
            act.sem_inc(AS[d], AHEAD * len(ACT_SCAN))
            act.sem_inc(AI[d], AHEAD * len(ACT_INV))

        def decay(i, d):
            act.wait_ge(DG[d], i * 2 + 2)
            act.activation(dec[d], dec[d], ACT.Exp).then_inc(EG[d], 1)

        for d in range(2):
            decay(0, d)

        def c_inverse(name, d, i, u):
            turned = heads(pair(2 + 2 * d))
            if name == "arg":
                if not isinstance(i, int) or i < NT - 1:
                    decay(i + 1, d)
            elif name == "qk":
                act.wait_ge(PI[d], at(PE_INV, "qk", i))
                act.wait_ge(PS[d], at(PE_SCAN, "iv", i, 2))
                act.activation(intra[u][d], turned, ACT.Copy).then_inc(AI[d], 1)
            elif name == "x0":
                act.wait_ge(PI[d], at(PE_INV, "x0", i))
                act.activation(XM[d], turned, ACT.Copy).then_inc(AI[d], 1)
            elif name[0] == "t":
                act.wait_ge(PI[d], at(PE_INV, name, i))
                act.activation(XT[u][d], turned, ACT.Copy).then_inc(AI[d], 1)

        def c_scan(step, d, i, u):
            if step == "qs":
                act.wait_ge(PS[d], at(PE_SCAN, "qs", i))
                act.wait_ge(o_stored[d], i * 16 + 16)
                for h in range(H):
                    last = act.activation(OB[d][:, h, :], pair(6)[:, h * P:(h + 1) * P], ACT.Copy,
                                          scale=sc[u][d][:, 1, h:h + 1])
                last.then_inc(AS[d], 1)
            elif step == "xr":
                act.wait_ge(PS[d], at(PE_SCAN, "xr", i))
                act.wait_ge(PL[d], i + 2)
                for h in range(H):
                    last = act.activation(VN[d][:, h, :], pair(6)[:, h * P:(h + 1) * P], ACT.Copy,
                                          scale=sc[u][d][:, 4, h:h + 1])
                last.then_inc(AS[d], 1)

        interleaved(act, c_inverse, c_scan)
        if stop <= 2:
            return
        stage_end(act, 2)

        act.sem_inc(d_ot, 1)

        def d_step(c, u, now, prev):
            if now:
                act.wait_ge(d_sum, c + 1)
                act.wait_ge(d_ss, c + 1)
                act.activation(sqd, of[:, u, :], ACT.Square).then_inc(d_sq, 1)
                act.wait_ge(d_ss, c + 2)
                act.activation(ssd[:, u, :], ssd[:, u, :], ACT.Ln, scale=1.0 / P, bias=epsb).then_inc(d_ln, 1)
                act.wait_ge(d_ln, c + 1)
                act.activation(ssd[:, u, :], ssd[:, u, :], ACT.Exp, scale=-0.5).then_inc(d_ro, 1)
                act.wait_ge(d_tp, c + 3)
                act.wait_ge(d_mm, c + 1)
                act.activation(ot[u], pair(0).rearrange("p (k n) -> p k n", k=KT), ACT.Copy).then_inc(d_ot, 1)

        skewed(act, d_step)

        def moe_act(l, n):
            base = first_layers(l)
            norm_act(act, n, True)
            act.wait_ge(ms["soft"], 2 + base["soft"])
            act.activation(pr, pr, ACT.Exp).then_inc(ms["exp"], 1)
            act.wait_ge(ms["pt_mm"], 1 + base["pt_mm"])
            act.activation(PT[0], ps[0:E, 2:4, :].rearrange("p b n -> p (b n)"), ACT.Copy).then_inc(ms["pt"], 1)

            def x_evac(e):
                act.wait_ge(ms["tpx"], e + 1 + base["tpx"])
                act.activation(xT, pair(6).rearrange("p (k n) -> p k n", k=KT), ACT.Copy).then_inc(ms["xt"], 1)

            def silu(e):
                act.wait_ge(ms["gate"], e + 1 + base["gate"])
                act.wait_ge(ms["hid"], e + 1 + base["hid"])
                act.activation(SG, pair(0), ACT.Silu).then_inc(ms["silu"], 1)

            def h_evac(e):
                act.wait_ge(ms["tph"], e + 1 + base["tph"])
                act.activation(hT, pair(6).rearrange("p (k n) -> p k n", k=KT), ACT.Copy).then_inc(ms["ht"], 1)

            x_evac(0)
            silu(0)
            act.wait_ge(ms["up"], 1 + base["up"])
            x_evac(1)
            with act.Fori(0, E - 2) as e:
                silu(e + 1)
                h_evac(e)
                act.wait_ge(ms["up"], e + 2 + base["up"])
                x_evac(e + 2)
            silu(E - 1)
            h_evac(E - 2)
            h_evac(E - 1)

        act.wait_ge(d_add, NT + 1)
        moe_act(0, 1)
        if stop <= 4:
            return
        stage_end(act, 3)
        act.wait_ge(s_x, 48)
        norm_act(act, 2, True)
        act.wait_ge(e_small, 48)
        act.sem_inc(e_prod, 2 * POOL_TAPS)
        with act.Fori(0, KT // 2) as it:
            for u in range(2):
                ch = it * 2 + u
                act.wait_ge(e_mm, ch + 1)
                act.wait_ge(e_pre, ch + 1)
                act.activation(sg_e[u], pair(4 * u + 2), ACT.Sigmoid, bias=ccol[:, ds(ch + KT, 1)]
                               ).then_inc(e_sig, 1)
                act.wait_ge(e_pre, ch + 3)
                for j in range(POOL_TAPS):
                    tap = dww[:, ds(ch, 1), j:j + 1].rearrange("p o j -> p (o j)")
                    act.wait_ge(e_padd, ch * (POOL_TAPS - 1) + 1 + (max(j - 3, 0) + 1 if j >= 2 else 0))
                    act.activation(prod_e[j % 2], pre_e[u][:, j:j + T], ACT.Copy, scale=tap).then_inc(e_prod, 1)
        for k in range(KT):
            act.wait_ge(e_xc, k + 1)
            if k:
                act.wait_ge(e_sqmm, k)
            act.activation(sq_e, U[:, k, :], ACT.Square).then_inc(e_sq, 1)
        act.wait_ge(e_sqmm, KT)
        act.activation(rb, pair(2), ACT.Ln, scale=1.0 / D, bias=epsb).then_inc(e_ln, 1)
        act.wait_ge(e_ln, 1)
        act.activation(rb, rb, ACT.Exp, scale=-0.5).then_inc(e_rb, 1)
        for k in range(KT):
            act.wait_ge(e_xn, k + 1)
            act.activation(U[:, k, :], U[:, k, :], ACT.Silu, scale=ccol[:, 3 * KT + k:3 * KT + k + 1],
                           bias=ccol[:, 4 * KT + k:4 * KT + k + 1]).then_inc(e_u, 1)
        act.wait_ge(e_add, NT)
        moe_act(1, 3)
        stage_end(act, 4)
        act.wait_ge(s_x, 64)
        norm_act(act, 4, False)

    @block.vector
    def _(dve):
        norm_dve_parts(dve, 0)

        def split(m, u, loads_done):
            dve.wait_ge(w_loaded[u], loads_done)
            if not isinstance(m, int) or m >= 2:
                dve.wait_ge(proj_done, m - 1)
            dve.tensor_copy(WR[:, u, 0], wq[u]).then_inc(w_high, 1)
            dve.wait_ge(w_high, m + 1)
            dve.tensor_tensor(WR[:, u, 1], wq[u], WR[:, u, 0], ALU.subtract).then_inc(w_split, 1)

        dve.wait_ge(xs_done, NT)
        dve.wait_ge(b_small, 48)
        dve.tensor_copy(GR[:, 0], wg).then_inc(g_split, 1)
        dve.wait_ge(g_split, 1)
        dve.tensor_tensor(GR[:, 1], wg, GR[:, 0], ALU.subtract).then_inc(g_split, 1)
        split(0, 0, 16)
        dve.wait_ge(gate_mm, 1)
        dve.wait_ge(b_small, 48)
        dve.tensor_scalar(ga, pair(4)[0:E, :], abias[0:E, 1:2], None, ALU.add).then_inc(gate_steps, 1)
        dve.wait_ge(gate_steps, 1)
        dve.scalar_tensor_tensor(gn, ga, -1.0, ga, ALU.mult, ALU.min).then_inc(gate_steps, 1)
        dve.wait_ge(gate_acts, 3)
        dve.scalar_tensor_tensor(lg, ga, 0.0, ge, ALU.max, ALU.add).then_inc(gate_steps, 1)
        dve.wait_ge(gate_steps, 3)
        dve.tensor_scalar(lg, lg, abias[0:E, 2:3], -1.0, ALU.mult, ALU.mult).then_inc(gate_steps, 1)
        dve.wait_ge(b_zero, 9)

        def b_step(m, u, now, prev, prev2, normed):
            if now:
                if isinstance(m, int) and m < PROJ - 1:
                    split(m + 1, 1 - u, (m + 1) // 2 * 16 + 16)
                elif not isinstance(m, int):
                    split(m + 1, 1 - u, (m - u) * 8 + 16 * (1 + u))
                dve.wait_ge(evac_done, m + 1)
                if prev2:
                    dve.wait_ge(silu_done, m - 1)
                for j in range(TAPS):
                    tap = cw[:, ds(m, 1), j:j + 1].rearrange("p o j -> p (o j)")
                    if j == 0:
                        ins = dve.tensor_scalar(cv[u], pre[u][:, 0:T], tap, None, ALU.mult)
                    else:
                        ins = dve.scalar_tensor_tensor(cv[u], pre[u][:, j:j + T], tap, cv[u], ALU.mult, ALU.add)
                    if j < TAPS - 1:
                        ins.then_inc(conv_steps, 1)
                        dve.wait_ge(conv_steps, m * (TAPS - 1) + j + 1)
                    else:
                        ins.then_inc(conv_done, 1)
            if prev:
                p = m - 1
                if normed[1]:
                    dve.wait_ge(rn_done, p + 1)
                    dve.wait_ge(tpq_done, p + 1)
                    dve.wait_ge(t_stored[1 - u], (p - (1 - u)) * 8 + 16)
                    dve.tensor_tensor(nrm[1 - u], sl[1 - u], rnb, ALU.mult).then_inc(mul_done, 1)
                else:
                    dve.wait_ge(silu_done, p + 1)
                    dve.sem_inc(mul_done, 1)

        b_loop(dve, b_step)
        dve.wait_ge(b2_act, 5)
        for d in range(2):
            dve.tensor_tensor(SC[:, d, :, 2, :], tot[:, :, d, :], SC[:, d, :, 0, :], ALU.subtract).then_inc(b2_dve, 1)
        if stop <= 1:
            return
        stage_end(dve, 1)
        for d in range(2):
            dve.sem_inc(VI[d], AHEAD * len(DVE_INV))
            dve.sem_inc(VC[d], AHEAD * len(DVE_SCAN) - 1)
            dve.memset(ST[d], 0.0).then_inc(VC[d], 1)
        dve.wait_ge(s_gcst, 32)
        negm = [g(C_NEGF), g(C_NEGB)]
        m0 = [g(C_M0F), g(C_M0B)]

        def decay_arg(i, u, d):
            dve.wait_ge(PL[d], i + 1)
            dve.wait_ge(VC[d], at(DVE_SCAN, "s", i, 2))
            dve.tensor_copy(sc[u][d], SC[:, d, ds(chunk(i, d), 1), :, :].rearrange("p o k h -> p (o k) h")
                            ).then_inc(DG[d], 1)
            dve.wait_ge(DG[d], i * 2 + 1)
            dve.wait_ge(g_loaded[d], i * 16 + 16)
            for h in range(H):
                last = dve.scalar_tensor_tensor(dec[d][:, h, :], dec[d][:, h, :], sc[u][d][:, 0, h:h + 1], negm[d],
                                                ALU.subtract, ALU.min)
            last.then_inc(DG[d], 1)

        for d in range(2):
            decay_arg(0, 0, d)

        def c_inverse(name, d, i, u):
            turned = pair(2 + 2 * d)
            if name == "arg":
                if not isinstance(i, int) or i < NT - 1:
                    decay_arg(i + 1, 1 - u, d)
            elif name == "kk":
                dve.wait_ge(PI[d], at(PE_INV, "kk", i))
                dve.wait_ge(EG[d], i + 1)
                for h in range(H):
                    last = dve.scalar_tensor_tensor(MT[d][:, h, :], turned[:, h * P:(h + 1) * P],
                                                    sc[u][d][:, 4, h:h + 1], dec[d][:, h, :], ALU.mult, ALU.mult)
                last.then_inc(VI[d], 1)
                dve.wait_ge(VI[d], at(DVE_INV, "mt", i))
                dve.wait_ge(PS[d], at(PE_SCAN, "xr", i, 2))
                dve.tensor_tensor(XT[u][d], MT[d], m0[d].unsqueeze(1).to_broadcast([P, H, P]), ALU.mult
                                  ).then_inc(VI[d], 1)
                dve.wait_ge(VI[d], at(DVE_INV, "xa", i))
                dve.tensor_tensor(XT[u][d], XT[u][d], ident.unsqueeze(1).to_broadcast([P, H, P]), ALU.add
                                  ).then_inc(VI[d], 1)
            elif name[0:2] == "xp":
                j = int(name[2:])
                dve.wait_ge(PI[d], at(PE_INV, name, i))
                dve.tensor_tensor(blocks(XM[d], d, j), blocks(XM[d], d, j), half(heads(ps[:, d, :]), j),
                                  ALU.add).then_inc(VI[d], 1)
            elif name[0] == "p":
                j = int(name[1:])
                lm = C_LM + (d * LEVELS + j) * (P // 2)
                dve.wait_ge(PI[d], at(PE_INV, name, i))
                dve.tensor_tensor(PN[d], heads(ps[:, d, :]), g(lm, P // 2).unsqueeze(1).to_broadcast([P, H, P // 2]),
                                  ALU.mult).then_inc(VI[d], 1)

        def c_scan(step, d, i, u):
            if step == "ks":
                dve.wait_ge(PS[d], at(PE_SCAN, "ks", i))
                for h in range(H):
                    last = dve.scalar_tensor_tensor(R[d][:, h, :], pair(6)[:, h * P:(h + 1) * P],
                                                    sc[u][d][:, 5, h:h + 1], loads[u][d][3][:, h, :],
                                                    ALU.mult, ALU.add)
                last.then_inc(VC[d], 1)
            elif step == "iv":
                dve.wait_ge(PS[d], at(PE_SCAN, "iv", i))
                dve.tensor_tensor(OB[d], OB[d], heads(pair(6)), ALU.add).then_inc(VC[d], 1)
            elif step == "kv":
                dve.wait_ge(PS[d], at(PE_SCAN, "kv", i))
                for h in range(H):
                    last = dve.scalar_tensor_tensor(ST[d][:, h, :], ST[d][:, h, :], sc[u][d][:, 3, h:h + 1],
                                                    pair(6)[:, h * P:(h + 1) * P], ALU.mult, ALU.add)
                last.then_inc(VC[d], 1)

        interleaved(dve, c_inverse, c_scan)
        if stop <= 2:
            return
        stage_end(dve, 2)

        dve.sem_inc(d_og, 2)
        dve.sem_inc(d_ss, 1)
        dve.sem_inc(d_add, 1)
        dve.wait_ge(nw_loaded, 16)

        def d_step(c, u, now, prev):
            if now:
                it2 = (c - u) * 24 + 48
                dve.wait_ge(d_loaded[u], it2)
                dve.tensor_tensor(of[:, u, :], of[:, u, :], ob[:, u, :], ALU.add).then_inc(d_sum, 1)
                dve.wait_ge(d_sq, c + 1)
                dve.tensor_reduce(ssd[:, u, :], heads(sqd), AX.X, ALU.add).then_inc(d_ss, 1)
                dve.wait_ge(d_ro, c + 1)
                dve.tensor_tensor(heads(of[:, u, :]), heads(of[:, u, :]),
                                  ssd[:, u, :].unsqueeze(2).to_broadcast([P, H, P]), ALU.mult).then_inc(d_chain, 1)
                dve.wait_ge(d_chain, c * 2 + 1)
                dve.tensor_tensor(heads(of[:, u, :]), heads(of[:, u, :]),
                                  nw.unsqueeze(1).to_broadcast([P, H, P]), ALU.mult).then_inc(d_chain, 1)
                dve.wait_ge(d_chain, c * 2 + 2)
                dve.wait_ge(d_tp, c + 1)
                dve.tensor_tensor(og[:, u, :], of[:, u, :], sz[:, u, :], ALU.mult).then_inc(d_og, 1)
            if prev:
                p = c - 2
                dve.wait_ge(d_mm, p + 3)
                xt = X[:, ds(p, 1), :].rearrange("p o n -> p (o n)")
                dve.tensor_tensor(xt, xt, pair(4 + 2 * u), ALU.add).then_inc(d_add, 1)

        for c in range(2):
            d_step(c, c, True, False)
        dve.wait_ge(s_x, 32)
        with dve.Fori(1, NT // 2) as it:
            for u in range(2):
                d_step(it * 2 + u, u, True, True)
        for c in range(NT, NT + 2):
            d_step(c, c % 2, False, True)

        def moe_dve(l, n):
            base = first_layers(l)
            norm_dve(dve, n, True)
            dve.wait_ge(ms["logits"], 1 + base["logits"])
            lgt = ps[:, 4, 0:P].rearrange("p (t e) -> p t e", t=NT)
            dve.tensor_reduce(mx, lgt, AX.X, ALU.max).then_inc(ms["soft"], 1)
            dve.wait_ge(ms["soft"], 1 + base["soft"])
            dve.tensor_tensor(pr, lgt, mx.unsqueeze(2).to_broadcast([P, NT, E]), ALU.subtract).then_inc(ms["soft"], 1)
            dve.wait_ge(ms["exp"], 1 + base["exp"])
            dve.tensor_reduce(sm, pr, AX.X, ALU.add).then_inc(ms["soft"], 1)
            dve.wait_ge(ms["soft"], 3 + base["soft"])
            dve.reciprocal(rs, sm).then_inc(ms["soft"], 1)
            dve.wait_ge(ms["soft"], 4 + base["soft"])
            dve.tensor_tensor(pr, pr, rs.unsqueeze(2).to_broadcast([P, NT, E]), ALU.mult).then_inc(ms["soft"], 1)
            dve.wait_ge(ms["pt"], 1 + base["pt"])
            for r in range(CAP // 8):
                v8, i8 = vals[:, r * 8:r * 8 + 8], idx8[:, r * 8:r * 8 + 8]
                dve.max(v8, PT[r % 2]).then_inc(ms["top"], 1)
                dve.wait_ge(ms["top"], 3 * r + 1 + base["top"])
                dve.max_index(i8, v8, PT[r % 2]).then_inc(ms["top"], 1)
                dve.match_replace(PT[1 - r % 2], v8, PT[r % 2], -1.0).then_inc(ms["top"], 1)
                dve.wait_ge(ms["top"], 3 * r + 3 + base["top"])
            dve.tensor_copy(idxf, idx8).then_inc(ms["top"], 1)
            dve.wait_ge(ms["top_mm"], 1 + base["top_mm"])
            dve.tensor_copy(idxT, ps[:, 4, 0:E]).then_inc(ms["idx"], 1)
            dve.tensor_copy(aff, ps[:, 5, 0:E]).then_inc(ms["idx"], 1)
            dve.wait_ge(ms["idx"], 2 + base["idx"])
            dve.sem_inc(ms["hid"], 1)
            dve.sem_inc(ms["y"], 1)

            def hid(e):
                dve.wait_ge(ms["up"], e + 1 + base["up"])
                dve.wait_ge(ms["silu"], e + 1 + base["silu"])
                dve.wait_ge(ms["tph"], e + base["tph"]) if not isinstance(e, int) or e else None
                dve.tensor_tensor(HD, SG, pair(2), ALU.mult).then_inc(ms["hid"], 1)

            def y(e, u):
                dve.wait_ge(ms["down"], e + 2 + base["down"])
                dve.wait_ge(ms["scat_ok"], e + 1 + base["scat_ok"])
                dve.tensor_scalar(YS[u], pair(4), aff[:, ds(e, 1)], None, ALU.mult).then_inc(ms["y"], 1)

            hid(0)
            with dve.Fori(0, E // 2 - 1) as it:
                for u in range(2):
                    hid(it * 2 + u + 1)
                    y(it * 2 + u, u)
            hid(E - 1)
            y(E - 2, 0)
            y(E - 1, 1)

        moe_dve(0, 1)
        if stop <= 4:
            return
        stage_end(dve, 3)
        norm_dve(dve, 2, True)
        dve.sem_inc(e_pre, 2)
        dve.sem_inc(e_conv, 2)
        dve.wait_ge(e_small, 48)
        dve.wait_ge(e_zero, 4)
        with dve.Fori(0, KT // 2) as it:
            for u in range(2):
                ch = it * 2 + u
                dve.wait_ge(e_sig, ch + 1)
                dve.wait_ge(e_prod, (ch + 1) * POOL_TAPS)
                dve.scalar_tensor_tensor(pre_e[u][:, CF_TAPS // 2:CF_TAPS // 2 + T], pair(4 * u), ccol[:, ds(ch, 1)],
                                         sg_e[u], ALU.add, ALU.mult).then_inc(e_pre, 1)
                dve.wait_ge(e_pre, ch + 3)
                dve.wait_ge(e_conv, ch + 2)
                for n in range(CHAIN):
                    j = POOL_TAPS + n
                    tap = dww[:, ds(ch, 1), j:j + 1].rearrange("p o j -> p (o j)")
                    acc = acc_e[n % 2]
                    if n == 0:
                        ins = dve.tensor_scalar(acc, pre_e[u][:, j:j + T], tap, ccol[:, ds(ch + 2 * KT, 1)],
                                                ALU.mult, ALU.add)
                    elif n == 1:
                        ins = dve.tensor_scalar(acc, pre_e[u][:, j:j + T], tap, None, ALU.mult)
                    else:
                        dve.wait_ge(e_chain, ch * (CHAIN + 1) + n - 1)
                        ins = dve.scalar_tensor_tensor(acc, pre_e[u][:, j:j + T], tap, acc, ALU.mult, ALU.add)
                    ins.then_inc(e_chain, 1)
                dve.wait_ge(e_chain, ch * (CHAIN + 1) + CHAIN)
                dve.tensor_tensor(acc_e[0], acc_e[0], acc_e[1], ALU.add).then_inc(e_chain, 1)
                dve.wait_ge(e_chain, (ch + 1) * (CHAIN + 1))
                dve.wait_ge(e_padd, (ch + 1) * (POOL_TAPS - 1) + 1)
                dve.tensor_tensor(U[:, ds(ch, 1), :].rearrange("p o n -> p (o n)"), acc_e[0], sum_e[u], ALU.add
                                  ).then_inc(e_conv, 1)
        dve.wait_ge(e_mean, 1)
        dve.tensor_scalar(mb, pair(0), 1.0 / D, None, ALU.mult).then_inc(e_mb, 1)
        dve.wait_ge(e_mb, 1)
        for k in range(KT):
            dve.tensor_tensor(U[:, k, :], U[:, k, :], mb, ALU.subtract).then_inc(e_xc, 1)
        dve.wait_ge(e_rb, 1)
        for k in range(KT):
            dve.tensor_tensor(U[:, k, :], U[:, k, :], rb, ALU.mult).then_inc(e_xn, 1)
        dve.wait_ge(e_bias, NT)
        for t in range(NT):
            dve.wait_ge(e_pw2, t + 1)
            dve.tensor_tensor(X[:, t, :], X[:, t, :], pair(4 + 2 * (t % 2)), ALU.add).then_inc(e_add, 1)
        moe_dve(1, 3)
        stage_end(dve, 4)
        norm_dve(dve, 4, False)

    @block.tensor
    def _(pe):
        pe.wait_ge(s_cst, 32)
        norm_pe(pe, 0)
        pe.wait_ge(g_split, 2)
        pe.wait_ge(ht_done, NT + 2 + before(0, "ht_done"))
        for half_ in range(2):
            last = in_parts(pe, ps[:, 4 + half_, :], GR, lambda b_, k: HR[:, b_, k, half_ * HALF:(half_ + 1) * HALF])
        last.then_inc(gate_mm, 1)

        def b_step(m, u, now, prev, prev2, normed):
            if now:
                pe.wait_ge(w_split, m + 1)
                if prev2:
                    pe.wait_ge(evac_done, m - 1)
                for half_ in range(2):
                    last = in_parts(pe, ps[:, 2 * u + half_, :], WR[:, u],
                                    lambda b_, k: HR[:, b_, k, half_ * HALF:(half_ + 1) * HALF])
                last.then_inc(proj_done, 1)
            if prev and normed[1]:
                p = m - 1
                pe.wait_ge(sqb_done, p + 1)
                if prev2:
                    pe.wait_ge(lnr_done, p)
                else:
                    pe.wait_ge(gate_steps, 1)
                    pe.wait_ge(gate_acts, 4)
                for half_ in range(2):
                    last = pe.matmul(ps[:, 4 + half_, :], ones, sqb[:, half_ * HALF:(half_ + 1) * HALF],
                                     start=True, stop=True)
                last.then_inc(sqmm_done, 1)
            if prev2:
                p = m - 2
                pe.wait_ge(mul_done, p + 1)
                pe.wait_ge(nat_done, p)
                src = nrm[u] if normed[2] else sl[u]
                for c in range(NT):
                    last = pe.transpose(pair(6)[:, c * P:(c + 1) * P], src[:, c * P:(c + 1) * P], ident)
                last.then_inc(tpq_done, 1)

        pe.sem_inc(tpq_done, 2)
        b_loop(pe, b_step)
        pe.wait_ge(evac_done, PROJ)
        pe.wait_ge(gate_steps, 4)
        for c in range(NT):
            pe.transpose(ps[:, 0, c * E:(c + 1) * E], lg[:, c * P:(c + 1) * P], ident[0:E, 0:E])
        for c in range(NT):
            last = pe.transpose(ps[:, 1, c * E:(c + 1) * E], bs[:, c * P:(c + 1) * P], ident[0:E, 0:E])
        last.then_inc(b2_pe, 1)
        pe.wait_ge(b2_act, 1)
        pe.wait_ge(s_gcst, 32)
        pe.wait_ge(nat_done, PROJ)
        pe.wait_ge(lnr_done, NORMED)
        for d in range(2):
            pe.matmul(ps[:, 2 + d, 0:NT * H].rearrange("p (c h) -> p c h", c=NT), uf[:, d * P:(d + 1) * P], lgn[:, :, d * H:(d + 1) * H],
                      start=True, stop=True)
        pe.matmul(ps[:, 4, 0:NT * E], ones, lgn.rearrange("p c n -> p (c n)"), start=True, stop=True).then_inc(b2_pe, 1)
        pe.wait_ge(b2_act, 5)
        for d in range(2):
            for c in range(NT):
                n = (d * NT + c) * P
                last = pe.transpose(ps[0:H, 4 + n // HALF, n % HALF:n % HALF + P], SC[:, d, c, 0, :], ident)
        last.then_inc(b2_pe, 1)
        if stop <= 1:
            return
        stage_end(pe, 1)
        for d in range(2):
            pe.sem_inc(PI[d], AHEAD * len(PE_INV))
            pe.sem_inc(PS[d], AHEAD * len(PE_SCAN))

        def products(s, out, lhs, rhs):
            n = out.shape[1] // H
            for h in range(H):
                last = pe.matmul(out[:, h * n:(h + 1) * n], lhs[:, h, :], rhs[:, h], start=True, stop=True,
                                 skip_group_check=True)
            last.then_inc(s, 1)

        def turn(s, out, src):
            for h in range(H):
                last = pe.transpose(out[:, h * P:(h + 1) * P], src[:, h, :], ident)
            last.then_inc(s, 1)

        def c_inverse(name, d, i, u):
            q_t, k_t = loads[u][d][0:2]
            turned = pair(2 + 2 * d)
            if name == "kk":
                pe.wait_ge(c_ld[d][u], (i - u) * 32 + 64)
                pe.wait_ge(AI[d], at(ACT_INV, f"t{LEVELS - 1}", i, 1))
                products(PI[d], turned, k_t, k_t)
            elif name == "qk":
                pe.wait_ge(VI[d], at(DVE_INV, "mt", i))
                products(PI[d], turned, k_t, q_t)
            elif name == "x0":
                pe.wait_ge(VI[d], at(DVE_INV, "xt0", i))
                pe.wait_ge(AI[d], at(ACT_INV, "qk", i))
                turn(PI[d], turned, XT[u][d])
            elif name == "p0":
                pe.wait_ge(AI[d], at(ACT_INV, "x0", i))
                products(PI[d], ps[:, d, :], MT[d], blocks(XM[d], d, 0))
            elif name[0:2] == "xp":
                j = int(name[2:])
                pe.wait_ge(VI[d], at(DVE_INV, f"pn{j}", i))
                if j:
                    pe.wait_ge(AI[d], at(ACT_INV, f"t{j - 1}", i))
                products(PI[d], ps[:, d, :], XT[u][d], PN[d])
            elif name[0] == "p":
                j = int(name[1:])
                pe.wait_ge(VI[d], at(DVE_INV, f"x{j - 1}", i))
                products(PI[d], ps[:, d, :], MT[d], blocks(XM[d], d, j))
            elif name[0] == "t":
                j = int(name[1:])
                if j == LEVELS - 1:
                    pe.wait_ge(VI[d], at(DVE_INV, f"x{j}", i))
                turn(PI[d], pair(2 + 2 * d), XM[d])

        def c_scan(step, d, i, u):
            q_t, k_t, k_n = loads[u][d][0:3]
            if step == "qs":
                if d == 0:
                    pe.wait_ge(VC[1], at(DVE_SCAN, "s", i, 1))
                else:
                    pe.wait_ge(AS[0], at(ACT_SCAN, "oq", i))
                pe.wait_ge(VC[d], at(DVE_SCAN, "s", i, 1))
                products(PS[d], pair(6), q_t, ST[d])
            elif step == "ks":
                if d == 0:
                    pe.wait_ge(AS[1], at(ACT_SCAN, "oq", i))
                else:
                    pe.wait_ge(VC[0], at(DVE_SCAN, "r", i))
                products(PS[d], pair(6), k_t, ST[d])
            elif step == "xr":
                if d == 0:
                    pe.wait_ge(VC[1], at(DVE_SCAN, "r", i))
                else:
                    pe.wait_ge(AS[0], at(ACT_SCAN, "vn", i))
                pe.wait_ge(VC[d], at(DVE_SCAN, "r", i))
                pe.wait_ge(AI[d], at(ACT_INV, f"t{LEVELS - 1}", i))
                products(PS[d], pair(6), XT[u][d], R[d])
            elif step == "iv":
                if d == 0:
                    pe.wait_ge(AS[1], at(ACT_SCAN, "vn", i))
                else:
                    pe.wait_ge(VC[0], at(DVE_SCAN, "o", i))
                pe.wait_ge(GI[d], i + 1)
                products(PS[d], pair(6), intra[u][d], VN[d])
            else:
                if d == 0:
                    pe.wait_ge(VC[1], at(DVE_SCAN, "o", i))
                else:
                    pe.wait_ge(VC[0], at(DVE_SCAN, "s", i))
                pe.wait_ge(PL[d], i + 3)
                products(PS[d], pair(6), k_n, VS[d])

        interleaved(pe, c_inverse, c_scan)
        if stop <= 2:
            return
        stage_end(pe, 2)

        pe.sem_inc(d_tp, 2)
        pe.sem_inc(d_mm, 2)
        pe.wait_ge(wo_loaded, 16)

        def d_step(c, u, now, prev):
            if now:
                pe.wait_ge(d_og, c + 3)
                pe.wait_ge(d_ot, c + 1)
                for k in range(KT):
                    last = pe.transpose(pair(0)[:, k * P:(k + 1) * P], og[:, u, k * P:(k + 1) * P], ident)
                last.then_inc(d_tp, 1)
            if prev:
                p, w = c - 1, 1 - u
                pe.wait_ge(d_ot, p + 2)
                pe.wait_ge(d_add, p) if not isinstance(p, int) or p else None
                for half_ in range(2):
                    for k in range(KT):
                        last = pe.matmul(ps[:, 4 + 2 * w + half_, :], ot[w][:, k, :],
                                         wo[:, k, half_ * HALF:(half_ + 1) * HALF], start=(k == 0), stop=(k == KT - 1))
                last.then_inc(d_mm, 1)

        skewed(pe, d_step)

        def moe_pe(l, n):
            base = first_layers(l)
            pe.sem_inc(tp_done, 2)
            pe.wait_ge(wr_loaded, 16 * (l + 1))
            for t in range(NT + 1):
                if t < NT:
                    pe.wait_ge(xs_done, t + 1 + before(n, "xs_done"))
                    pe.wait_ge(ht_done, t + 1 + before(n, "ht_done"))
                    for k in range(KT):
                        last = pe.transpose(pair(2 * (t % 2))[:, k * P:(k + 1) * P], xs[:, t % 2, k * P:(k + 1) * P],
                                            ident)
                    last.then_inc(tp_done, 1)
                if t:
                    pe.wait_ge(ht_done, t + 2 + before(n, "ht_done"))
                    for k in range(KT):
                        last = pe.matmul(ps[:, 4, (t - 1) * E:t * E], HT[:, k, (t - 1) * P:t * P], wr[:, k, :],
                                         start=(k == 0), stop=(k == KT - 1))
            last.then_inc(ms["logits"], 1)
            pe.wait_ge(ms["soft"], 5 + base["soft"])
            for t in range(NT):
                last = pe.transpose(ps[0:E, 2 + t // 4, t % 4 * P:(t % 4 + 1) * P], pr[:, t, :], ident)
            last.then_inc(ms["pt_mm"], 1)
            pe.wait_ge(ms["top"], 3 * (CAP // 8) + 1 + base["top"])
            pe.transpose(ps[:, 4, 0:E], idxf, ident[0:E, 0:E])
            pe.transpose(ps[:, 5, 0:E], vals, ident[0:E, 0:E]).then_inc(ms["top_mm"], 1)
            pe.sem_inc(ms["down"], 1)

            def tpx(e, u, slot_count):
                pe.wait_ge(ms[f"gath{u}"], slot_count + base[f"gath{u}"])
                for k in range(KT):
                    last = pe.transpose(pair(6)[:, k * P:(k + 1) * P], xin[u][:, k * P:(k + 1) * P], ident)
                last.then_inc(ms["tpx"], 1)

            def product(bank, lhs, w, half_):
                for k in range(KT):
                    last = pe.matmul(ps[:, bank + half_, :], lhs[:, k, :], w[:, k, half_ * HALF:(half_ + 1) * HALF],
                                     start=(k == 0), stop=(k == KT - 1))
                return last

            def gate(e, u, slot_count):
                pe.wait_ge(ms["xt"], e + 1 + base["xt"])
                pe.wait_ge(ms[f"wg{u}"], slot_count + base[f"wg{u}"])
                pe.wait_ge(ms["silu"], e + base["silu"]) if not isinstance(e, int) or e else None
                product(0, xT, WG[u], 0)
                product(0, xT, WG[u], 1).then_inc(ms["gate"], 1)

            def up(e, u, slot_count):
                pe.wait_ge(ms[f"wu{u}"], slot_count + base[f"wu{u}"])
                pe.wait_ge(ms["hid"], e + 1 + base["hid"])
                product(2, xT, WU[u], 0)
                product(2, xT, WU[u], 1).then_inc(ms["up"], 1)

            def tph(e):
                pe.wait_ge(ms["hid"], e + 2 + base["hid"])
                pe.wait_ge(ms["xt"], e + 2 + base["xt"])
                for k in range(KT):
                    last = pe.transpose(pair(6)[:, k * P:(k + 1) * P], HD[:, k * P:(k + 1) * P], ident)
                last.then_inc(ms["tph"], 1)

            def down(e, between):
                pe.wait_ge(ms["ht"], e + 1 + base["ht"])
                pe.wait_ge(ms["wd"], e * 16 + 16 + base["wd"])
                pe.wait_ge(ms["y"], e + 1 + base["y"])
                product(4, hT, WD, 0)
                between()
                product(4, hT, WD, 1).then_inc(ms["down"], 1)

            pe.wait_ge(ms["idx"], 2 + base["idx"])
            tpx(0, 0, 16)
            gate(0, 0, 16)
            up(0, 0, 16)
            tpx(1, 1, 16)
            with pe.Fori(0, E // 2 - 1) as it:
                for u in range(2):
                    e = it * 2 + u
                    nxt = it * 16 + 16 * (1 + u)
                    gate(e + 1, 1 - u, nxt)
                    tph(e)
                    up(e + 1, 1 - u, nxt)

                    def next_x():
                        pe.wait_ge(ms["ht"], e + 1 + base["ht"])
                        tpx(e + 2, u, it * 16 + 32)
                    down(e, next_x)
            gate(E - 1, 1, 8 * E)
            tph(E - 2)
            up(E - 1, 1, 8 * E)
            down(E - 2, lambda: None)
            pe.wait_ge(ms["hid"], E + 1 + base["hid"])
            pe.wait_ge(ms["ht"], E - 1 + base["ht"])
            for k in range(KT):
                last = pe.transpose(pair(6)[:, k * P:(k + 1) * P], HD[:, k * P:(k + 1) * P], ident)
            last.then_inc(ms["tph"], 1)
            down(E - 1, lambda: None)

        moe_pe(0, 1)
        if stop <= 4:
            return
        stage_end(pe, 3)
        norm_pe(pe, 2)
        pe.wait_ge(ht_done, NT + 2 + before(2, "ht_done"))
        with pe.Fori(0, KT // 2) as it:
            for u in range(2):
                ch = it * 2 + u
                pe.wait_ge(e_w[u], it * 32 + 32)
                pe.wait_ge(e_pre, ch + 1)
                for n in range(2):
                    for half_ in range(2):
                        for k in range(KT):
                            last = pe.matmul(ps[:, 4 * u + 2 * n + half_, :], wag[u][n][:, k, :],
                                             HT[:, k, half_ * HALF:(half_ + 1) * HALF],
                                             start=(k == 0), stop=(k == KT - 1))
                last.then_inc(e_mm, 1)
        pe.wait_ge(e_pre, KT + 2)
        for k in range(KT):
            pe.wait_ge(e_conv, k + 3)
            for half_ in range(2):
                last = pe.matmul(ps[:, half_, :], ones, U[:, k, half_ * HALF:(half_ + 1) * HALF],
                                 start=(k == 0), stop=(k == KT - 1))
        last.then_inc(e_mean, 1)
        for k in range(KT):
            pe.wait_ge(e_sq, k + 1)
            for half_ in range(2):
                last = pe.matmul(ps[:, 2 + half_, :], ones, sq_e[:, half_ * HALF:(half_ + 1) * HALF],
                                 start=(k == 0), stop=(k == KT - 1))
            last.then_inc(e_sqmm, 1)
        pe.wait_ge(w2_loaded, 16)
        pe.wait_ge(e_u, KT)
        for t in range(NT):
            if t >= 2:
                pe.wait_ge(e_add, t - 1)
            for half_ in range(2):
                for k in range(KT):
                    last = pe.matmul(ps[:, 4 + 2 * (t % 2) + half_, :], U[:, k, t * P:(t + 1) * P],
                                     w2[:, k, half_ * HALF:(half_ + 1) * HALF], start=(k == 0), stop=(k == KT - 1))
            last.then_inc(e_pw2, 1)
        moe_pe(1, 3)
        stage_end(pe, 4)


def laid_out(inputs):
    x = {k: np.asarray(v) for k, v in inputs.items()}
    w_in = x["dn_w_in"][0]
    gates = w_in[:, 4 * D:].reshape(KT, P, 2, 2, H)
    gate_columns = np.zeros((P, KT, P), np.float32)
    for n in range(2):
        gate_columns[:, :, 32 * n:32 * n + E] = gates[:, :, :, 1 - n].transpose(1, 0, 2, 3).reshape(P, KT, E)
    tiled = lambda w: np.ascontiguousarray(w.reshape(KT, P, -1, P).transpose(2, 1, 0, 3))
    cols = lambda v: np.ascontiguousarray(v.reshape(-1, P).T)
    return {
        "x": x["x"][0],
        "consts": constants(),
        "norm_mix": x["norm_mix"], "norm_ffn": x["norm_ffn"], "final_norm": x["final_norm"],
        "w_in": tiled(w_in[:, :4 * D]),
        "w_gates": gate_columns,
        "conv_w": np.ascontiguousarray(x["dn_conv_w"][0].reshape(TAPS, 3 * H, P).transpose(2, 1, 0)),
        "gate_bias": np.stack([x["dn_a_log"][0].reshape(-1), x["dn_dt_bias"][0].reshape(-1)], 1),
        "dn_norm_w": x["dn_norm_w"][0],
        "dn_w_out": x["dn_w_out"][0],
        "w_pw1": tiled(x["cf_w_pw1"][0]),
        "cf_cols": np.concatenate([cols(x["cf_b_pw1"][0]), cols(x["cf_dw_b"][0]), cols(x["cf_ln_g"][0]),
                                   cols(x["cf_ln_b"][0])], 1),
        "cf_dw_w": np.ascontiguousarray(x["cf_dw_w"][0].reshape(CF_TAPS, KT, P).transpose(2, 1, 0)),
        "w_pw2": x["cf_w_pw2"][0],
        "b_pw2": x["cf_b_pw2"][0],
        "w_router": np.ascontiguousarray(x["moe_w_router"].reshape(2, KT, P, E).transpose(0, 2, 1, 3)),
        "w_gate": x["moe_w_gate"], "w_up": x["moe_w_up"], "w_down": x["moe_w_down"],
    }


def kernel(**inputs):
    import concourse.bacc as bacc
    from concourse.bass_utils import run_bass_kernel_spmd

    nc = bacc.Bacc("TRN2", target_bir_lowering=False, num_devices=1)
    arrays = laid_out(inputs)
    aps = {n: nc.dram_tensor(f"in_{n}", v.shape, mybir.dt.from_np(v.dtype), kind="ExternalInput").ap()
           for n, v in arrays.items()}
    out = nc.dram_tensor("out", (1, T, D), F32, kind="ExternalOutput").ap()
    build(nc, aps, out)
    r = run_bass_kernel_spmd(nc, [{f"in_{n}": v for n, v in arrays.items()}], core_ids=[0])
    return r.results[0]["out"]
```

```python
from contextlib import ExitStack

import numpy as np
import concourse.bass as bass
from concourse import mybir

P = 128
T = 1024
D = 1024
NT = T // P
KT = D // P
H = 8
TAPS = 5
CF_TAPS = 31
E = 16
CAP = 2 * T // E
EPS = 1e-6
HALF = 512
LEVELS = 6
PROJ = 4 * H
NEG = -1e30

ALU = mybir.AluOpType
ACT = mybir.ActivationFunctionType
AX = mybir.AxisListType
F32 = mybir.dt.float32
F32R = mybir.dt.float32r
U32 = mybir.dt.uint32
ds = bass.ds

C_IDENT, C_ONES, C_UF, C_UB, C_NEGF, C_NEGB, C_M0F, C_M0B = (P * n for n in range(8))
C_LM = 8 * P
C_END = C_LM + 2 * LEVELS * (P // 2)
C_FLIP = C_END
C_ALL = C_FLIP + P


def constants():
    c = np.zeros((P, C_ALL), np.float32)
    r, t = np.arange(P)[:, None], np.arange(P)[None, :]
    c[:, C_IDENT:C_IDENT + P] = r == t
    c[:, C_ONES:C_ONES + P] = 1.0
    c[:, C_FLIP:C_FLIP + P] = r == P - 1 - t
    c[:, C_UF:C_UF + P] = r <= t
    c[:, C_UB:C_UB + P] = r >= t
    c[:, C_NEGF:C_NEGF + P] = np.where(t >= r, 0.0, NEG)
    c[:, C_NEGB:C_NEGB + P] = np.where(t <= r, 0.0, NEG)
    c[:, C_M0F:C_M0F + P] = -1.0 * ((t == r + 1) & (r % 2 == 0))
    c[:, C_M0B:C_M0B + P] = -1.0 * ((t == r - 1) & (r % 2 == 1))
    for d in range(2):
        for j in range(LEVELS):
            b = 2 << j
            cols = (t[0] // b) % 2 == d
            block = t[0][cols] // b
            partner = block + 1 if d == 0 else block - 1
            a = C_LM + (d * LEVELS + j) * (P // 2)
            c[:, a:a + P // 2] = -1.0 * ((r // b) == partner[None, :])
    return c


MERGES = range(LEVELS)
PE_INV = ["kk", "qk", "x0", "p0"] + [s for j in MERGES for s in
         ((f"xp{j}", f"p{j + 1}", f"t{j}") if j < LEVELS - 1 else (f"xp{j}", f"t{j}"))]
DVE_INV = ["mt", "xa", "xt0"] + [s for j in MERGES for s in (f"pn{j}", f"x{j}")]
ACT_INV = ["qk", "x0"] + [f"t{j}" for j in MERGES]
PE_SCAN = ["qs", "ks", "xr", "iv", "kv"]
DVE_SCAN = ["r", "o", "s"]
ACT_SCAN = ["oq", "vn"]
AHEAD = 2


def chunk_schedule():
    scan = [(s, d) for s in PE_SCAN for d in range(2)]
    order = [("kk", 0), ("kk", 1), scan.pop(0), ("qk", 0), scan.pop(0), ("x0", 0), ("qk", 1), ("p0", 0), ("x0", 1),
             ("xp0", 0), ("p0", 1), scan.pop(0), ("xp0", 1)]
    for j in MERGES:
        if j:
            order += [("arg", 0)] if j == LEVELS - 1 else []
            order += [(f"xp{j}", d) for d in range(2)]
            order += [scan.pop(0)] if scan else []
        for d in range(2):
            order += [(f"p{j + 1}", d)] if j < LEVELS - 1 else []
            order += [(f"t{j}", d)]
        order += [scan.pop(0)] if scan else []
    order += [("arg", 1)]
    return order


SCHEDULE = chunk_schedule()


def at(steps, name, i, before=0):
    return (i + AHEAD - before) * len(steps) + steps.index(name) + 1


def later(step, first):
    return not isinstance(step, int) or step >= first


def earlier(step, end):
    return not isinstance(step, int) or step < end


def build(nc, a, out):
    with ExitStack() as ctx:
        _build(nc, ctx, a, out)


def _build(nc, ctx, a, out):
    def sem(name):
        return ctx.enter_context(nc.semaphore(name))

    def sems(name, n):
        return [sem(f"{name}{i}") for i in range(n)]

    qk_t = nc.dram_tensor("qk_t", (2 * H, P, T), F32, kind="Internal").ap()
    nat = nc.dram_tensor("nat", (NT, P, PROJ, P), F32, kind="Internal").ap()
    gc_d = nc.dram_tensor("gc_d", (2, NT, H, P), F32, kind="Internal").ap()
    o_dir = nc.dram_tensor("o_dir", (2, NT, P, D), F32, kind="Internal").ap()
    hn_d = [nc.dram_tensor(f"hn_d{l}", (T, D), F32, kind="Internal").ap() for l in range(2)]
    acc_d = [nc.dram_tensor(f"acc_d{l}", (T, D), F32, kind="Internal").ap() for l in range(2)]

    K = 256
    with ExitStack() as below:
        below.enter_context(nc.sbuf_tensor("below", [P, 64 * K], F32))
        HR = below.enter_context(nc.sbuf_tensor("stream_parts", [P, 2, KT, T], F32R))
        WR = below.enter_context(nc.sbuf_tensor("weight_parts", [P, 2, 2, KT, P], F32R))
        GR = below.enter_context(nc.sbuf_tensor("gate_parts", [P, 2, KT, P], F32R))
    arena = ctx.enter_context(nc.sbuf_tensor("arena", [P, 196 * K], F32))
    cst = ctx.enter_context(nc.sbuf_tensor("cst", [P, 3 * P], F32))
    gain = ctx.enter_context(nc.sbuf_tensor("gain", [P, D], F32))
    small = ctx.enter_context(nc.sbuf_tensor("small", [P, 256], F32))
    idxu = ctx.enter_context(nc.sbuf_tensor("idxu", [P, E + CAP + 4], U32))
    ps = ctx.enter_context(nc.psum_tensor("ps", [P, 8, HALF], F32))

    def part(kib, n):
        at = int(kib * K)
        assert at + n <= 196 * K
        return arena[:, at:at + n]

    def tiles(kib, n, w):
        return part(kib, n * w).rearrange("p (n w) -> p n w", n=n)

    def pair(b):
        return ps[:, b:b + 2, :].rearrange("p b n -> p (b n)")

    def heads(ap):
        return ap.rearrange("p (h n) -> p h n", h=H)

    ident, ones, flip = cst[:, 0:P], cst[:, P:2 * P], cst[:, 2 * P:3 * P]
    X = tiles(128, NT, D)
    HT = tiles(96, KT, T)
    xs = tiles(160, 2, D)
    junk = part(168, D)

    ss, rstd = small[:, 0:8], small[:, 8:16]
    epsb = small[:, 16:17]

    def in_parts(pe, out, lhs, rhs):
        parts = ((0, 0), (0, 1), (1, 0))
        for k in range(KT):
            for n, (a_, b_) in enumerate(parts):
                last = pe.matmul(out, lhs[:, a_, k, :], rhs(b_, k), start=(k == 0 and n == 0),
                                 stop=(k == KT - 1 and n == len(parts) - 1))
        return last

    s_cst, s_eps = sem("constants_loaded"), sem("eps_set")
    s_x = sems("x_loaded", 2)
    gain_loaded, gain_used = sem("gain_loaded"), sem("gain_used")
    stage_done = sem("stage_done")

    def stage_end(eng, n):
        eng.drain().then_inc(stage_done, 1)
        eng.wait_ge(stage_done, 4 * n)

    sq_done, rms_done, rstd_done = sem("sq_done"), sem("rms_done"), sem("rstd_done")
    xs_done, tp_done, ht_done = sem("xs_done"), sem("tp_done"), sem("ht_done")
    hi_done = sem("high_parts_done")
    acc_stored = sems("acc_stored", 2)
    hn_stored = sems("hn_stored", 2)

    def before(n, what):
        if what == "hn_stored":
            return (16 * (NT // 2) + 16) * (0, 0, 1, 1, 2)[n]
        return n * {"sq_done": NT + 1, "rms_done": NT, "rstd_done": NT, "xs_done": NT, "tp_done": NT + 2,
                    "ht_done": NT + 2}[what]

    gains = [a["norm_mix"][0], a["norm_ffn"][0], a["norm_mix"][1], a["norm_ffn"][1], a["final_norm"]]

    FIRST = 3

    def load_x(sp, src):
        for n, (lo, hi) in enumerate(((0, FIRST), (FIRST, NT))):
            sp.dma_start(X[:, lo:hi, :], src[lo * P:hi * P, :].rearrange("(t p) d -> p t d", p=P)).then_inc(s_x[n], 16)

    def norm_tile(act, n, t):
        act.wait_ge(sq_done, t + 1 + before(n, "sq_done"))
        act.activation(junk, X[:, ds(t, 1), :].rearrange("p o n -> p (o n)"), ACT.Square,
                       accum_out=ss[:, ds(t, 1)]).then_inc(sq_done, 1)
        act.wait_ge(sq_done, t + 2 + before(n, "sq_done"))
        act.sem_inc(passed, 1)
        act.activation(ss[:, ds(t, 1)], ss[:, ds(t, 1)], ACT.Sqrt, scale=1.0 / D, bias=epsb).then_inc(rms_done, 1)

    def norm_evac(act, n, t, bank, parts=False):
        act.wait_ge(tp_done, t + 3 + before(n, "tp_done"))
        dst = HR[:, 0, :, ds(t * P, P)] if parts else HT[:, :, ds(t * P, P)]
        act.activation(dst, pair(bank).rearrange("p (k n) -> p k n", k=KT), ACT.Copy
                       ).then_inc(hi_done if parts else ht_done, 1)

    def norm_act(act, n, transpose, parts=False):
        act.sem_inc(sq_done, 1)
        if transpose and not parts:
            act.sem_inc(ht_done, 2)
        x_loads = {0: 1, 2: 3, 4: 4}[n] * 16

        def evac(t, u):
            if transpose:
                norm_evac(act, n, t, 2 * u, parts)

        act.wait_ge(s_x[0], x_loads)
        for t in range(FIRST):
            norm_tile(act, n, t)
        evac(0, 0)
        act.wait_ge(s_x[1], x_loads)
        norm_tile(act, n, FIRST)
        evac(1, 1)
        with act.Fori(2, NT // 2) as it:
            for u in range(2):
                norm_tile(act, n, it * 2 + u)
                evac(it * 2 + u - 2, u)
        for t in (NT - 2, NT - 1):
            evac(t, t % 2)

    def norm_rstd(dve, n, t):
        dve.wait_ge(rms_done, t + 1 + before(n, "rms_done"))
        dve.reciprocal(rstd[:, ds(t, 1)], ss[:, ds(t, 1)]).then_inc(rstd_done, 1)
        dve.wait_ge(rstd_done, t + 1 + before(n, "rstd_done"))

    def norm_dve_parts(dve, n):
        dve.wait_ge(gain_loaded, 16 * (n + 1))
        dve.sem_inc(ht_done, 2)

        def scaled(t, u):
            norm_rstd(dve, n, t)
            dve.wait_ge(tp_done, t + 1 + before(n, "tp_done"))
            dve.scalar_tensor_tensor(xs[:, u, :], X[:, ds(t, 1), :].rearrange("p o n -> p (o n)"),
                                     rstd[:, ds(t, 1)], gain[:, :], ALU.mult, ALU.mult).then_inc(xs_done, 1)

        def low(t, u):
            dve.wait_ge(hi_done, t + 1)
            dve.tensor_tensor(HR[:, 1, :, ds(t * P, P)], pair(2 * u).rearrange("p (k n) -> p k n", k=KT),
                              HR[:, 0, :, ds(t * P, P)], ALU.subtract).then_inc(ht_done, 1)

        scaled(0, 0)
        with dve.Fori(0, NT // 2 - 1) as it:
            for u in range(2):
                scaled(it * 2 + u + 1, 1 - u)
                low(it * 2 + u, u)
        scaled(NT - 1, 1)
        low(NT - 2, 0)
        low(NT - 1, 1)
        dve.wait_ge(xs_done, NT + before(n, "xs_done"))
        dve.sem_inc(gain_used, 1)

    def norm_scaled(dve, n, t, u, transpose, stored):
        norm_rstd(dve, n, t)
        if transpose:
            dve.wait_ge(tp_done, t + 1 + before(n, "tp_done"))
        if stored:
            dve.wait_ge(hn_stored[u], (t - u) * 8 + 16 + before(n, "hn_stored"))
        dve.scalar_tensor_tensor(xs[:, u, :], X[:, ds(t, 1), :].rearrange("p o n -> p (o n)"),
                                 rstd[:, ds(t, 1)], gain[:, :], ALU.mult, ALU.mult).then_inc(xs_done, 1)

    def norm_over(dve, n):
        dve.wait_ge(xs_done, NT + before(n, "xs_done"))
        dve.sem_inc(gain_used, 1)

    def norm_dve(dve, n, transpose):
        dve.wait_ge(gain_loaded, 16 * (n + 1))
        with dve.Fori(0, NT // 2) as it:
            for u in range(2):
                norm_scaled(dve, n, it * 2 + u, u, transpose, n == 4)
        norm_over(dve, n)

    def norm_pe(pe, n):
        pe.sem_inc(tp_done, 2)
        with pe.Fori(0, NT // 2) as it:
            for u in range(2):
                norm_turn(pe, n, it * 2 + u, u, 2 * u, 1)

    def norm_turn(pe, n, t, u, bank, read):
        pe.wait_ge(xs_done, t + 1 + before(n, "xs_done"))
        pe.wait_ge(ht_done, t + read + before(n, "ht_done"))
        for k in range(KT):
            last = pe.transpose(pair(bank)[:, k * P:(k + 1) * P], xs[:, u, k * P:(k + 1) * P], ident)
        last.then_inc(tp_done, 1)

    def norm_store_credits(sp):
        for u in range(2):
            sp.sem_inc(hn_stored[u], 16)

    def norm_store(sp, n, dram, stream=None, stored=None):
        with sp.Fori(0, NT // 2) as it:
            for u in range(2):
                t = it * 2 + u
                sp.wait_ge(xs_done, t + 1 + before(n, "xs_done"))
                sp.dma_start(dram[ds(t * P, P), :], xs[:, u, :]).then_inc(hn_stored[u], 16)
                if stream is not None:
                    sp.dma_start(stream[ds(t * P, P), :], X[:, ds(t, 1), :].rearrange("p o n -> p (o n)")
                                 ).then_inc(stored, 16)

    def load_gain(sp, n):
        if n:
            sp.wait_ge(gain_used, n)
        sp.dma_start(gain[:, :], gains[n].partition_broadcast(P)).then_inc(gain_loaded, 16)

    wq = [part(4 * u, D).rearrange("p (k c) -> p k c", k=KT) for u in range(2)]
    PADW = T + TAPS - 1
    pre = [part(8 + 5 * u, PADW) for u in range(2)]
    cv = [part(18 + 4 * u, T) for u in range(2)]
    sl = [part(26 + 4 * u, T) for u in range(2)]
    nrm = [part(34 + 4 * u, T) for u in range(2)]
    natb = [part(42 + 4 * u, T).rearrange("p (c n) -> p c n", c=NT) for u in range(2)]
    sqb, rnb = part(50, T), part(54, T)
    wg = tiles(184, KT, P)
    cw = part(60, PROJ * TAPS).rearrange("p (m j) -> p m j", m=PROJ)
    nsc, nbi = part(61, PROJ), part(61.25, PROJ)
    abias = part(61.5, 4)
    ga, gn, ge, lg, bs = (part(at_, T)[0:E, :] for at_ in (160, 164, 168, 152, 156))
    lgn = part(172, NT * E).rearrange("p (c n) -> p c n", c=NT)
    btn = part(173, NT * E).rearrange("p (c n) -> p c n", c=NT)
    SCN = 6
    SC = part(174, 2 * NT * SCN * H).rearrange("p (d c k h) -> p d c k h", d=2, c=NT, k=SCN)
    tot = part(177, NT * E).rearrange("p (c d h) -> p c d h", c=NT, d=2)
    GCT = part(144, 2 * NT * P)

    uf = part(182, 2 * P)

    b_small, w_loaded = sem("b_small_loaded"), sems("w_loaded", 2)
    gate_mm, gate_steps, gate_acts = sem("gate_products"), sem("gate_dve_steps"), sem("gate_act_steps")
    b_zero, w_split, w_high, g_split = sem("b_tables_set"), sem("w_split"), sem("w_high"), sem("gate_w_split")
    proj_done, evac_done, conv_steps, conv_done = sem("proj_done"), sem("evac_done"), sem("conv_steps"), sem("conv_done")
    silu_done, sqb_done, sqmm_done, lnr_done, rn_done = (sem("silu_done"), sem("sqb_done"), sem("sqmm_done"),
                                                         sem("lnr_done"), sem("rn_done"))
    mul_done, tpq_done, nat_done = sem("mul_done"), sem("tpq_done"), sem("nat_done")
    t_stored, n_stored = sems("t_stored", 2), sems("n_stored", 2)
    b2_pe, b2_act, b2_dve = sem("scan_tables_pe"), sem("scan_tables_act"), sem("scan_tables_dve")

    NORMED = 2 * H

    def b_loop(eng, step):
        for m in range(2):
            step(m, m, True, m >= 1, False, (True, True, True))
        with eng.Fori(1, NORMED // 2) as it:
            for u in range(2):
                step(it * 2 + u, u, True, True, True, (True, True, True))
        step(NORMED, 0, True, True, True, (False, True, True))
        step(NORMED + 1, 1, True, True, True, (False, False, True))
        with eng.Fori(NORMED // 2 + 1, PROJ // 2 - 1) as it:
            for u in range(2):
                step(it * 2 + u, u, True, True, True, (False, False, False))
        for m in range(PROJ - 2, PROJ + 2):
            step(m, m % 2, m < PROJ, m < PROJ + 1, True, (False, False, False))

    loads = [[[tiles(32 * u + 16 * d + 4 * n, H, P) for n in range(4)] for d in range(2)] for u in range(2)]
    dec, MT, XM, VN, R, VS = ([tiles(64 + 42 * d + 4 * n, H, P) for d in range(2)] for n in range(6))
    intra, XT = ([[tiles(88 + 42 * d + 8 * n + 4 * u, H, P) for d in range(2)] for u in range(2)] for n in range(2))
    PN = [tiles(104 + 42 * d, H, P // 2) for d in range(2)]
    ST = [tiles(160, H, P), tiles(164, H, P)]
    OB = [tiles(168, H, P), tiles(178, H, P)]
    sc = [[part(172 + 0.5 * u + 0.25 * d, SCN * H).rearrange("p (k h) -> p k h", k=SCN) for d in range(2)]
          for u in range(2)]
    gmask = part(188, C_END - C_NEGF)

    def g(col, n=P):
        return gmask[:, col - C_NEGF:col - C_NEGF + n]

    PI, VI, AI = sems("inv_pe", 2), sems("inv_dve", 2), sems("inv_act", 2)
    PS, VC, AS, PL = sems("scan_pe", 2), sems("scan_dve", 2), sems("scan_act", 2), sems("scan_pool", 2)
    DG, EG = sems("decay_dve", 2), sems("decay_act", 2)
    GI, g_loaded = sems("intra_pool", 2), sems("decay_loaded", 2)
    c_ld = [sems(f"c_loaded{d}_", 2) for d in range(2)]
    o_stored = sems("o_stored", 2)
    s_gcst = sem("masks_loaded")

    def chunk(i, d):
        return i if d == 0 else i * -1 + (NT - 1)

    def interleaved(eng, inverse, scan):
        def both(i, u, k):
            for name, d in SCHEDULE:
                if name not in PE_SCAN and k is not None:
                    inverse(name, d, k, 1 - u)
                elif name in PE_SCAN and i is not None and (name != "kv" or earlier(i, NT - 1)):
                    scan(name, d, i, u)

        both(None, 1, 0)
        with eng.Fori(0, NT // 2 - 1) as it:
            for u in range(2):
                both(it * 2 + u, u, it * 2 + u + 1)
        both(NT - 2, 0, NT - 1)
        both(NT - 1, 1, None)

    def scan_bank(i, d):
        return pair(6) if earlier(i, NT - 1) else pair(2 + 2 * d)

    def blocks(ap, d, j):
        b = 2 << j
        v = ap.rearrange("p h (n two b) -> p h n two b", two=2, b=b)
        return v[:, :, :, d, :]

    def half(ap, j):
        return ap.rearrange("p h (n b) -> p h n b", b=2 << j)

    wo = tiles(0, KT, D)
    of, ob, sz, og = (tiles(32 + 8 * i, 2, D) for i in range(4))
    ot = [tiles(64 + 4 * u, KT, P) for u in range(2)]
    sqd = part(72, D)
    nw = part(76, P)
    ssd = small[:, 24:40].rearrange("p (u h) -> p u h", u=2)
    wo_loaded, nw_loaded, d_loaded = sem("wo_loaded"), sem("nw_loaded"), sems("d_loaded", 2)
    d_sum, d_sq, d_ss, d_rms, d_ro, d_og = (sem("d_sum"), sem("d_sq"), sem("d_ss"), sem("d_rms"), sem("d_ro"), sem("d_og"))
    d_chain, d_tp, d_ot, d_mm, d_add = sem("d_chain"), sem("d_tp"), sem("d_ot"), sem("d_mm"), sem("d_add")

    EPAD = T + CF_TAPS - 1
    wag = [[part(8 * u + 4 * n, D).rearrange("p (k c) -> p k c", k=KT) for n in range(2)] for u in range(2)]
    pre_e = [part(16 + 5 * u, EPAD) for u in range(2)]
    sg_e = [part(26, T), part(182, T)]
    POOL_TAPS = 11
    CHAIN = CF_TAPS - POOL_TAPS
    prod_e, sum_e = [part(172, T), part(186, T)], [part(168, T), part(190, T)]
    acc_e = [part(160, T), part(164, T)]
    U = tiles(32, KT, T)
    w2 = tiles(64, KT, D)
    sq_e = acc_e
    mb, rb = part(168, T), part(172, T)
    dww = part(176, KT * CF_TAPS).rearrange("p (m j) -> p m j", m=KT)
    ccol = part(177, 5 * KT)
    b2b = part(178, D)
    e_small, e_w, w2_loaded = sem("e_small_loaded"), sems("e_w_loaded", 2), sem("w2_loaded")
    e_mm, e_sig, e_pre, e_chain, e_conv, e_zero = (sem("e_mm"), sem("e_sig"), sem("e_pre"), sem("e_chain"),
                                                   sem("e_conv"), sem("e_zero"))
    e_prod, e_padd = sem("e_tap_product"), sem("e_tap_added")
    e_mean, e_mb, e_xc, e_sq, e_sqmm, e_ln, e_rb, e_xn, e_u = (
        sem("e_mean"), sem("e_mb"), sem("e_centred"), sem("e_sq"), sem("e_sqmm"), sem("e_ln"), sem("e_rb"),
        sem("e_normed"), sem("e_u"))
    e_pw2, e_add, e_bias = sem("e_pw2"), sem("e_add"), sem("e_bias_added")

    WG = [tiles(0, KT, D), tiles(64, KT, D)]
    WU = [tiles(32, KT, D), tiles(96, KT, D)]
    WD = tiles(128, KT, D)
    xin = [part(160 + 4 * u, D) for u in range(2)]
    xT = tiles(168, KT, P)
    SG, HD, hT, YS = part(172, D), part(176, D), tiles(180, KT, P), [part(184 + 4 * u, D) for u in range(2)]
    ROW = 32
    SEEK = ROW + E
    PT = [part(172, HALF)[0:2 * ROW, :], part(174, HALF)[0:2 * ROW, :]]
    LT = part(176, T)[0:E, :]
    slots = [t % (NT // 2) * 2 + t // (NT // 2) for t in range(NT)]
    top = ctx.enter_context(nc.sbuf_tensor("top", [P, 6 * P], F32))
    wr = top[:, 0:P].rearrange("p (k e) -> p k e", k=KT)
    prow = top[:, P:3 * P]
    pr = prow.rearrange("p (t e) -> p t e", t=NT)[:, :, 0:E]
    vals, idxf = top[0:SEEK, 3 * P:4 * P], top[0:SEEK, 4 * P:5 * P]
    aff = top[:, 5 * P:5 * P + E]
    both = small[:, 64:64 + 2 * SEEK].rearrange("p (n r) -> p n r", n=2)
    keep, gap, step_back, chosen = (small[:, 160 + n * E:160 + (n + 1) * E] for n in range(4))
    mx, sm, rs = small[:, 40:48], small[:, 48:56], small[:, 56:64]
    idxT, idx8 = idxu[:, 0:E], idxu[0:SEEK, E:E + CAP]
    idg, ids = [idxu[:, E + CAP + u:E + CAP + u + 1] for u in range(2)], [idxu[:, E + CAP + 2:E + CAP + 3]] * 2

    wr_loaded, passed = sem("wr_loaded"), sem("passed")
    LAYER = {"lt_mm": 1, "lt": 1, "logits": 1, "soft": 5, "exp": 1, "pt_mm": 1, "pt": 1, "top": 3 * (CAP // 8) + 1, "top_mm": 1, "both": 1, "flip": 1, "pick": 4, "idx": 2,
             "wu0": 8 * E, "wu1": 8 * E, "wg0": 8 * E, "wg1": 8 * E, "wd": 16 * E, "gath0": 8 * E, "gath1": 8 * E,
             "idg": 2 * E, "scat": 16 * E, "scat_ok": E + 2, "tpx": E, "xt": E, "gate": E, "up": E, "silu": E,
             "hid": E + 1, "tph": E, "ht": E, "down": E + 1, "y": E + 1}
    ms = {n: sem(f"m_{n}") for n in LAYER}

    def first_layers(l):
        return {n: l * v for n, v in LAYER.items()}

    block = ctx.enter_context(nc.Block())

    @block.sync
    def _(sp):
        for n, col in enumerate((C_IDENT, C_ONES, C_FLIP)):
            sp.dma_start(cst[:, n * P:(n + 1) * P], a["consts"][:, col:col + P]).then_inc(s_cst, 16)
        load_x(sp, a["x"])
        load_gain(sp, 0)
        sp.dma_start(wg, a["w_gates"]).then_inc(b_small, 16)
        sp.dma_start(cw[:, 0:3 * H, :], a["conv_w"]).then_inc(b_small, 16)
        sp.dma_start(abias[0:E, 0:2], a["gate_bias"]).then_inc(b_small, 16)
        sp.dma_start(gmask, a["consts"][:, C_NEGF:C_END]).then_inc(s_gcst, 16)
        sp.dma_start(uf, a["consts"][:, C_UF:C_UF + 2 * P]).then_inc(s_gcst, 16)
        for u in range(2):
            sp.sem_inc(t_stored[u], 16)
            sp.sem_inc(n_stored[u], 16)
        for m in range(2):
            sp.dma_start(wq[m], a["w_in"][m]).then_inc(w_loaded[m], 16)

        def b_reload(m, u):
            sp.wait_ge(w_split, m + 1)
            sp.dma_start(wq[u], a["w_in"][ds(m + 2, 1)].rearrange("o p k c -> (o p) k c")).then_inc(w_loaded[u], 16)

        def b_stores(m, u, is_t, is_n):
            sp.wait_ge(mul_done, m + 1)
            if is_t:
                sp.dma_start(qk_t[ds(m, 1)].rearrange("o p t -> (o p) t"), nrm[u]).then_inc(t_stored[u], 16)
            else:
                sp.wait_ge(t_stored[u], (m - u) * 8 + 16)
                sp.sem_inc(t_stored[u], 16)
            sp.wait_ge(nat_done, m + 1)
            if is_n:
                sp.dma_start(nat[:, :, ds(m, 1), :].rearrange("c p o n -> p c (o n)"), natb[u]).then_inc(n_stored[u], 16)
            else:
                sp.wait_ge(n_stored[u], (m - u) * 8 + 16)
                sp.sem_inc(n_stored[u], 16)

        def b_range(lo, hi, is_t, is_n, load):
            with sp.Fori(lo // 2, hi // 2) as it:
                for u in range(2):
                    if load:
                        b_reload(it * 2 + u, u)
                    b_stores(it * 2 + u - 2, u, is_t, is_n)

        for m in range(2):
            b_reload(m, m)
        b_range(2, H + 2, True, False, True)
        b_range(H + 2, 2 * H + 2, True, True, True)
        b_range(2 * H + 2, PROJ - 2, False, True, True)
        b_range(PROJ - 2, PROJ + 2, False, True, False)
        for u in range(2):
            sp.wait_ge(t_stored[u], 8 * PROJ + 16)
            sp.wait_ge(n_stored[u], 8 * PROJ + 16)
        sp.wait_ge(b2_act, 16)
        sp.dma_start(gc_d.rearrange("d c h p -> h (d c) p"), GCT[0:H, :].rearrange("h (n p) -> h n p", p=P)
                     ).then_inc(s_gcst, 16)
        sp.wait_ge(s_gcst, 48)
        sp.wait_ge(stage_done, 4 * 1)
        def c_decay(i):
            for d in range(2):
                sp.wait_ge(VI[d], at(DVE_INV, "mt", i, 1))
                sp.sem_inc(passed, 1)
                sp.wait_ge(GI[d], i)
                sp.dma_start(dec[d].rearrange("p h n -> p (h n)"),
                             gc_d[d][ds(chunk(i, d), 1)].rearrange("o h n -> (o h n)").partition_broadcast(P)
                             ).then_inc(g_loaded[d], 16)

        def c_load(i, u, d, parts):
            c = chunk(i, d)
            src = (qk_t[0:H, :, ds(c * P, P)].rearrange("h p t -> p h t"),
                   qk_t[H:2 * H, :, ds(c * P, P)].rearrange("h p t -> p h t"),
                   nat[ds(c, 1), :, H:2 * H, :].rearrange("o p h n -> (o p) h n"),
                   nat[ds(c, 1), :, 2 * H:3 * H, :].rearrange("o p h n -> (o p) h n"))
            for n in parts:
                sp.dma_start(loads[u][d][n], src[n]).then_inc(c_ld[d][u], 16)

        def c_store(i, d):
            sp.wait_ge(VC[d], at(DVE_SCAN, "o", i))
            sp.dma_start(o_dir[d][ds(chunk(i, d), 1)].rearrange("o p n -> (o p) n"),
                         OB[d].rearrange("p h n -> p (h n)")).then_inc(o_stored[d], 16)

        for d in range(2):
            sp.sem_inc(o_stored[d], 16)
            sp.dma_start(dec[d].rearrange("p h n -> p (h n)"),
                         gc_d[d][chunk(0, d)].rearrange("h n -> (h n)").partition_broadcast(P)).then_inc(g_loaded[d], 16)
        for d in range(2):
            c_load(0, 0, d, (1, 0, 3, 2))
        c_decay(1)
        for d in range(2):
            c_load(1, 1, d, (1, 0, 3, 2))
        with sp.Fori(0, NT // 2 - 1) as it:
            for u in range(2):
                i = it * 2 + u
                c_decay(i + 2)
                for d in range(2):
                    c_store(i, d)
                    c_load(i + 2, u, d, (1, 0, 3))
                for d in range(2):
                    sp.wait_ge(VC[d], at(DVE_SCAN, "s", i))
                    c_load(i + 2, u, d, (2,))
        for d in range(2):
            c_store(NT - 2, d)
        for d in range(2):
            sp.wait_ge(VC[d], at(DVE_SCAN, "s", NT - 2))
        sp.dma_start(wo, a["dn_w_out"].rearrange("(k p) n -> p k n", p=P)).then_inc(wo_loaded, 16)
        for d in range(2):
            c_store(NT - 1, d)
        for d in range(2):
            sp.wait_ge(o_stored[d], 16 * (NT + 1))
        sp.wait_ge(stage_done, 4 * 2)
        def d_load(c, u):
            for dst, src in ((of, o_dir[0][ds(c, 1)]), (ob, o_dir[1][ds(c, 1)]),
                             (sz, nat[ds(c, 1), :, 3 * H:PROJ, :].rearrange("o p h n -> o p (h n)"))):
                sp.dma_start(dst[:, u, :], src.rearrange("o p n -> (o p) n")).then_inc(d_loaded[u], 16)

        sp.dma_start(nw, a["dn_norm_w"].partition_broadcast(P)).then_inc(nw_loaded, 16)
        d_load(0, 0)
        d_load(1, 1)
        sp.wait_ge(d_loaded[0], 48)
        load_x(sp, a["x"])
        load_gain(sp, 1)
        norm_store_credits(sp)
        with sp.Fori(1, NT // 2) as it:
            for u in range(2):
                c = it * 2 + u
                sp.wait_ge(d_og, c + 1)
                d_load(c, u)

        def moe_sp(l, n):
            base = first_layers(l)
            sp.dma_start(wr, a["w_router"][l]).then_inc(wr_loaded, 16)

            def load(w, e, dst, s):
                sp.dma_start(dst, a[w][l][ds(e, 1)].rearrange("o (k p) f -> p (o k) f", p=P)).then_inc(ms[s], 16)

            if l == 1:
                sp.wait_ge(e_conv, KT + 2)
                load("w_gate", 0, WG[0], "wg0")
            norm_store(sp, n, hn_d[l], acc_d[l], acc_stored[l])
            if l == 0:
                sp.wait_ge(d_mm, NT + 2)
                load("w_gate", 0, WG[0], "wg0")
            load("w_up", 0, WU[0], "wu0")
            load("w_gate", 1, WG[1], "wg1")
            sp.wait_ge(ms["logits"], 1 + base["logits"])
            load("w_up", 1, WU[1], "wu1")
            sp.wait_ge(xs_done, NT + before(n, "xs_done"))
            sp.wait_ge(acc_stored[l], 16 * NT)
            for u in range(2):
                sp.wait_ge(ms[f"gath{u}"], 16 + base[f"gath{u}"])
            with sp.Fori(0, E // 2 - 1) as it:
                for u in range(2):
                    e = it * 2 + u
                    sp.wait_ge(ms["down"], e + 1 + base["down"])
                    load("w_down", e, WD, "wd")
                    sp.wait_ge(ms["up"], e + 1 + base["up"])
                    load("w_gate", e + 2, WG[u], f"wg{u}")
                    load("w_up", e + 2, WU[u], f"wu{u}")
            for e in (E - 2, E - 1):
                sp.wait_ge(ms["down"], e + 1 + base["down"])
                load("w_down", e, WD, "wd")
            sp.wait_ge(ms["scat_ok"], E + 2 + base["scat_ok"])
            sp.wait_ge(ms["down"], E + 1 + base["down"])
            load_x(sp, acc_d[l])

        moe_sp(0, 1)
        sp.wait_ge(stage_done, 4 * 3)
        load_gain(sp, 2)
        for m in range(2):
            for n in range(2):
                sp.dma_start(wag[m][n], a["w_pw1"][m + KT * n]).then_inc(e_w[m], 16)
        sp.dma_start(dww, a["cf_dw_w"]).then_inc(e_small, 16)
        sp.dma_start(ccol, a["cf_cols"]).then_inc(e_small, 16)
        sp.dma_start(b2b, a["b_pw2"].partition_broadcast(P)).then_inc(e_small, 16)
        sp.dma_start(w2, a["w_pw2"].rearrange("(k p) n -> p k n", p=P)).then_inc(w2_loaded, 16)
        with sp.Fori(0, KT // 2 - 1) as it:
            for u in range(2):
                ch = it * 2 + u
                sp.wait_ge(e_mm, ch + 1)
                for n in range(2):
                    sp.dma_start(wag[u][n], a["w_pw1"][ds(ch + 2 + KT * n, 1)].rearrange("o p k c -> (o p) k c")
                                 ).then_inc(e_w[u], 16)
        load_gain(sp, 3)
        norm_store_credits(sp)
        moe_sp(1, 3)
        sp.wait_ge(stage_done, 4 * 4)
        load_gain(sp, 4)
        norm_store_credits(sp)
        norm_store(sp, 4, out[0])
        for u in range(2):
            sp.wait_ge(hn_stored[u], 16 * (NT // 2 + 1) + before(4, "hn_stored"))

    @block.gpsimd
    def _(pool):
        pool.memset(epsb, EPS).then_inc(s_eps, 1)
        pool.memset(prow, 0.0).then_inc(b_zero, 1)
        pool.memset(cw[:, 3 * H:PROJ, :], 0.0).then_inc(b_zero, 1)
        pool.wait_ge(b_zero, 2)
        pool.memset(cw[:, 3 * H:PROJ, TAPS // 2:TAPS // 2 + 1], 1.0).then_inc(b_zero, 1)
        pool.memset(nsc[:, 0:2 * H], -0.5).then_inc(b_zero, 1)
        pool.memset(nbi[:, 0:H], -0.5 * float(np.log(P))).then_inc(b_zero, 1)
        pool.memset(nbi[:, H:2 * H], 0.0).then_inc(b_zero, 1)
        for u in range(2):
            pool.memset(pre[u][:, 0:TAPS // 2], 0.0).then_inc(b_zero, 1)
            pool.memset(pre[u][:, T + TAPS // 2:PADW], 0.0).then_inc(b_zero, 1)
        stage_end(pool, 1)
        for d in range(2):
            pool.sem_inc(PL[d], 2)

        def c_inverse(name, d, i, u):
            if name == "qk":
                pool.wait_ge(AI[d], at(ACT_INV, "qk", i))
                pool.tensor_tensor(intra[u][d], intra[u][d], dec[d], ALU.mult).then_inc(GI[d], 1)

        def c_scan(name, d, i, u):
            if name == "xr" and earlier(i, NT - 1):
                pool.wait_ge(AS[d], at(ACT_SCAN, "vn", i))
                pool.tensor_tensor(VS[d], VN[d], sc[u][d][:, 2, :].unsqueeze(2).to_broadcast([P, H, P]), ALU.mult
                                   ).then_inc(PL[d], 1)

        interleaved(pool, c_inverse, c_scan)
        stage_end(pool, 2)

        def moe_pool_run(l, n):
            base = first_layers(l)
            pool.wait_ge(ms["idx"], 2 + base["idx"])
            for u in range(2):
                pool.wait_ge(hn_stored[u], 16 * (NT // 2 + 1) + before(n, "hn_stored"))
            pool.wait_ge(acc_stored[l], 16 * NT)
            pool.sem_inc(ms["scat_ok"], 2)
            for u in range(2):
                pool.tensor_copy(idg[u], idxT[:, u:u + 1]).then_inc(ms["idg"], 1)
            pool.wait_ge(ms["idg"], 2 + base["idg"])
            for u in range(2):
                pool.indirect_dma_start(xin[u], None, hn_d[l], bass.IndirectOffsetOnAxis(ap=idg[u], axis=0)
                                        ).then_inc(ms[f"gath{u}"], 16)
            def gather(e, u, n_idg):
                pool.wait_ge(ms["tpx"], e - 1 + base["tpx"])
                pool.tensor_copy(idg[u], idxT[:, ds(e, 1)]).then_inc(ms["idg"], 1)
                pool.wait_ge(ms["idg"], n_idg + base["idg"])
                pool.sem_inc(passed, 1)
                pool.indirect_dma_start(xin[u], None, hn_d[l], bass.IndirectOffsetOnAxis(ap=idg[u], axis=0)
                                        ).then_inc(ms[f"gath{u}"], 16)

            def scatter(e, u, n_idg, first=False):
                if not first:
                    pool.wait_ge(ms["scat"], e * 16 + base["scat"])
                    pool.sem_inc(ms["scat_ok"], 1)
                pool.wait_ge(ms["y"], e + 2 + base["y"])
                pool.tensor_copy(ids[0], idxT[:, ds(e, 1)]).then_inc(ms["idg"], 1)
                pool.wait_ge(ms["idg"], n_idg + base["idg"])
                pool.sem_inc(passed, 1)
                pool.indirect_dma_start(acc_d[l], bass.IndirectOffsetOnAxis(ap=ids[0], axis=0), YS[u], None,
                                        compute_op=ALU.add).then_inc(ms["scat"], 16)

            for e in (2, 3):
                gather(e, e % 2, e + 1)
            for e in range(2):
                gather(e + 4, e, 2 * e + 5)
                scatter(e, e, 2 * e + 6, e == 0)
            with pool.Fori(1, E // 2 - 2) as it:
                for u in range(2):
                    e = it * 2 + u
                    gather(e + 4, u, e * 2 + 5)
                    scatter(e, u, e * 2 + 6)
            for e in range(E - 4, E):
                scatter(e, e % 2, E + e + 1)
            pool.wait_ge(ms["scat"], 16 * E + base["scat"])
            pool.sem_inc(ms["scat_ok"], 1)

        moe_pool_run(0, 1)
        stage_end(pool, 3)
        for u in range(2):
            pool.memset(pre_e[u][:, 0:CF_TAPS // 2], 0.0).then_inc(e_zero, 1)
            pool.memset(pre_e[u][:, T + CF_TAPS // 2:EPAD], 0.0).then_inc(e_zero, 1)
        pool.wait_ge(e_small, 48)
        pool.wait_ge(xs_done, NT + before(2, "xs_done"))
        for t in range(NT):
            pool.tensor_tensor(X[:, t, :], X[:, t, :], b2b, ALU.add).then_inc(e_bias, 1)
        pool.sem_inc(e_padd, 1)
        with pool.Fori(0, KT // 2) as it:
            for u in range(2):
                ch = it * 2 + u
                pool.wait_ge(e_conv, ch + 1)
                for j in range(1, POOL_TAPS):
                    pool.wait_ge(e_prod, (ch + 2) * POOL_TAPS + j + 1)
                    pool.wait_ge(e_padd, ch * (POOL_TAPS - 1) + j)
                    pool.tensor_tensor(sum_e[u], prod_e[0] if j == 1 else sum_e[u], prod_e[j % 2], ALU.add
                                       ).then_inc(e_padd, 1)
        moe_pool_run(1, 3)
        stage_end(pool, 4)

    @block.scalar
    def _(act):
        act.wait_ge(s_eps, 1)
        norm_act(act, 0, True, parts=True)
        act.wait_ge(b_small, 48)
        act.activation(abias[0:E, 2:3], abias[0:E, 0:1], ACT.Exp).then_inc(gate_acts, 1)
        act.wait_ge(gate_steps, 2)
        act.activation(ge, gn, ACT.Exp).then_inc(gate_acts, 1)
        act.wait_ge(gate_acts, 2)
        act.activation(ge, ge, ACT.Ln, bias=1.0).then_inc(gate_acts, 1)
        act.activation(bs, pair(4)[32:32 + E, :], ACT.Sigmoid).then_inc(gate_acts, 1)
        act.wait_ge(b_zero, 10)

        def b_step(m, u, now, prev, prev2, normed):
            if now:
                act.wait_ge(proj_done, m + 1)
                if prev2:
                    act.wait_ge(conv_done, m - 1)
                act.activation(pre[u][:, TAPS // 2:TAPS // 2 + T], pair(2 * u), ACT.Copy).then_inc(evac_done, 1)
            if prev and normed[1]:
                p = m - 1
                act.wait_ge(sqmm_done, p + 1)
                act.wait_ge(mul_done, p)
                act.activation(rnb, pair(4), ACT.Ln, bias=epsb).then_inc(lnr_done, 1)
                act.wait_ge(lnr_done, p + 1)
                act.activation(rnb, rnb, ACT.Exp, scale=nsc[:, ds(p, 1)], bias=nbi[:, ds(p, 1)]).then_inc(rn_done, 1)
            if now:
                act.wait_ge(conv_done, m + 1)
                if prev2:
                    act.wait_ge(mul_done, m - 1)
                    if not normed[2]:
                        act.wait_ge(tpq_done, m + 1)
                act.activation(sl[u], cv[u], ACT.Silu).then_inc(silu_done, 1)
                if normed[0]:
                    act.wait_ge(silu_done, m + 1)
                    if prev:
                        act.wait_ge(sqmm_done, m)
                    act.activation(sqb, sl[u], ACT.Square).then_inc(sqb_done, 1)
            if prev2:
                p = m - 2
                act.wait_ge(tpq_done, p + 3)
                act.wait_ge(n_stored[u], (p - u) * 8 + 16)
                act.activation(natb[u], pair(6).rearrange("p (c n) -> p c n", c=NT), ACT.Copy).then_inc(nat_done, 1)

        b_loop(act, b_step)
        act.wait_ge(b2_pe, 1)
        act.activation(lgn, ps[:, 0, 0:NT * E].rearrange("p (c n) -> p c n", c=NT), ACT.Copy).then_inc(b2_act, 1)
        act.activation(btn, ps[:, 1, 0:NT * E].rearrange("p (c n) -> p c n", c=NT), ACT.Copy).then_inc(b2_act, 1)
        act.wait_ge(b2_pe, 2)
        act.activation(tot.rearrange("p c d h -> p (c d h)"), ps[:, 4, 0:NT * E], ACT.Copy).then_inc(b2_act, 1)
        for d in range(2):
            act.activation(SC[:, d, :, 0, :], ps[:, 2 + d, 0:NT * H].rearrange("p (c h) -> p c h", c=NT), ACT.Copy
                           ).then_inc(b2_act, 1)
        act.wait_ge(b2_act, 5)
        for d in range(2):
            act.activation(SC[:, d, :, 1, :], SC[:, d, :, 0, :], ACT.Exp).then_inc(b2_act, 1)
            act.activation(SC[:, d, :, 3, :], tot[:, :, d, :], ACT.Exp).then_inc(b2_act, 1)
            act.activation(SC[:, d, :, 4, :], btn[:, :, d * H:(d + 1) * H], ACT.Copy).then_inc(b2_act, 1)
        act.wait_ge(b2_act, 11)
        act.wait_ge(b2_dve, 2)
        for d in range(2):
            act.activation(SC[:, d, :, 5, :], SC[:, d, :, 1, :], ACT.Copy, scale=-1.0).then_inc(b2_act, 1)
            act.activation(SC[:, d, :, 2, :], SC[:, d, :, 2, :], ACT.Exp).then_inc(b2_act, 1)
        act.wait_ge(b2_pe, 3)
        act.activation(GCT[0:H, :], ps[0:H, 4:8, :].rearrange("p b n -> p (b n)"), ACT.Copy).then_inc(b2_act, 1)
        stage_end(act, 1)
        for d in range(2):
            act.sem_inc(AS[d], AHEAD * len(ACT_SCAN))
            act.sem_inc(AI[d], AHEAD * len(ACT_INV))

        def decay(i, d):
            act.wait_ge(DG[d], i * 2 + 2)
            act.activation(dec[d], dec[d], ACT.Exp).then_inc(EG[d], 1)

        for d in range(2):
            decay(0, d)

        def c_inverse(name, d, i, u):
            turned = heads(pair(2 + 2 * d))
            if name == "arg":
                if earlier(i, NT - 1):
                    decay(i + 1, d)
            elif name == "qk":
                act.wait_ge(PI[d], at(PE_INV, "qk", i))
                act.wait_ge(PS[d], at(PE_SCAN, "iv", i, 2))
                act.activation(intra[u][d], turned, ACT.Copy).then_inc(AI[d], 1)
            elif name == "x0":
                act.wait_ge(PI[d], at(PE_INV, "x0", i))
                act.activation(XM[d], turned, ACT.Copy).then_inc(AI[d], 1)
            elif name[0] == "t":
                act.wait_ge(PI[d], at(PE_INV, name, i))
                act.activation(XT[u][d], turned, ACT.Copy).then_inc(AI[d], 1)

        def c_scan(step, d, i, u):
            if step == "qs":
                act.wait_ge(PS[d], at(PE_SCAN, "qs", i))
                act.wait_ge(o_stored[d], i * 16 + 16)
                for h in range(H):
                    last = act.activation(OB[d][:, h, :], scan_bank(i, d)[:, h * P:(h + 1) * P], ACT.Copy,
                                          scale=sc[u][d][:, 1, h:h + 1])
                last.then_inc(AS[d], 1)
            elif step == "xr":
                act.wait_ge(PS[d], at(PE_SCAN, "xr", i))
                act.wait_ge(PL[d], i + 2)
                for h in range(H):
                    last = act.activation(VN[d][:, h, :], scan_bank(i, d)[:, h * P:(h + 1) * P], ACT.Copy,
                                          scale=sc[u][d][:, 4, h:h + 1])
                last.then_inc(AS[d], 1)

        interleaved(act, c_inverse, c_scan)
        stage_end(act, 2)

        act.sem_inc(d_ot, 1)

        def d_step(c, u, now, prev):
            if now:
                act.wait_ge(d_sum, c + 1)
                act.wait_ge(d_ss, c + 1)
                act.activation(sqd, of[:, u, :], ACT.Square).then_inc(d_sq, 1)
                act.wait_ge(d_ss, c + 2)
                act.activation(ssd[:, u, :], ssd[:, u, :], ACT.Sqrt, scale=1.0 / P, bias=epsb).then_inc(d_rms, 1)
                act.wait_ge(d_tp, c + 3)
                act.wait_ge(d_mm, c + 1)
                act.activation(ot[u], pair(0).rearrange("p (k n) -> p k n", k=KT), ACT.Copy).then_inc(d_ot, 1)

        act.sem_inc(sq_done, 1)
        act.sem_inc(ht_done, 2)

        def d_norm(c, u):
            if earlier(c, NT):
                d_step(c, u, True, False)
            if later(c, 2) and earlier(c, NT + 2):
                act.wait_ge(d_add, c)
                norm_tile(act, 1, c - 2)
            if later(c, 4):
                norm_evac(act, 1, c - 4, 2)

        for c in range(4):
            d_norm(c, c % 2)
        with act.Fori(2, NT // 2) as it:
            for u in range(2):
                d_norm(it * 2 + u, u)
        for c in range(NT, NT + 4):
            d_norm(c, c % 2)

        def moe_act(l, n):
            base = first_layers(l)
            act.wait_ge(ms["lt_mm"], 1 + base["lt_mm"])
            act.activation(LT, pair(0)[0:E, :], ACT.Copy).then_inc(ms["lt"], 1)
            act.wait_ge(ms["soft"], 2 + base["soft"])
            act.activation(pr, pr, ACT.Exp).then_inc(ms["exp"], 1)
            act.wait_ge(ms["pt_mm"], 1 + base["pt_mm"])
            act.activation(PT[0], ps[0:2 * ROW, 2, :], ACT.Copy).then_inc(ms["pt"], 1)

            def x_evac(e):
                act.wait_ge(ms["tpx"], e + 1 + base["tpx"])
                act.activation(xT, pair(6).rearrange("p (k n) -> p k n", k=KT), ACT.Copy).then_inc(ms["xt"], 1)

            def silu(e):
                act.wait_ge(ms["gate"], e + 1 + base["gate"])
                act.wait_ge(ms["hid"], e + 1 + base["hid"])
                act.activation(SG, pair(0), ACT.Silu).then_inc(ms["silu"], 1)

            def h_evac(e):
                act.wait_ge(ms["tph"], e + 1 + base["tph"])
                act.activation(hT, pair(6).rearrange("p (k n) -> p k n", k=KT), ACT.Copy).then_inc(ms["ht"], 1)

            x_evac(0)
            silu(0)
            act.wait_ge(ms["up"], 1 + base["up"])
            x_evac(1)
            with act.Fori(0, E - 2) as e:
                silu(e + 1)
                h_evac(e)
                act.wait_ge(ms["up"], e + 2 + base["up"])
                x_evac(e + 2)
            silu(E - 1)
            h_evac(E - 2)
            h_evac(E - 1)

        moe_act(0, 1)
        stage_end(act, 3)
        norm_act(act, 2, True)
        act.wait_ge(e_small, 48)
        act.sem_inc(e_prod, 2 * POOL_TAPS)
        with act.Fori(0, KT // 2) as it:
            for u in range(2):
                ch = it * 2 + u
                act.wait_ge(e_mm, ch + 1)
                act.wait_ge(e_pre, ch + 1)
                act.activation(sg_e[u], pair(4 * u + 2), ACT.Sigmoid, bias=ccol[:, ds(ch + KT, 1)]
                               ).then_inc(e_sig, 1)
                act.wait_ge(e_pre, ch + 3)
                for j in range(POOL_TAPS):
                    tap = dww[:, ds(ch, 1), j:j + 1].rearrange("p o j -> p (o j)")
                    act.wait_ge(e_padd, ch * (POOL_TAPS - 1) + 1 + (max(j - 3, 0) + 1 if j >= 2 else 0))
                    act.activation(prod_e[j % 2], pre_e[u][:, j:j + T], ACT.Copy, scale=tap).then_inc(e_prod, 1)
        for k in range(KT):
            act.wait_ge(e_xc, k + 1)
            if k >= 2:
                act.wait_ge(e_sqmm, k - 1)
            act.activation(sq_e[k % 2], U[:, k, :], ACT.Square).then_inc(e_sq, 1)
        act.wait_ge(e_sqmm, KT)
        act.activation(rb, pair(2), ACT.Ln, scale=1.0 / D, bias=epsb).then_inc(e_ln, 1)
        act.wait_ge(e_ln, 1)
        act.activation(rb, rb, ACT.Exp, scale=-0.5).then_inc(e_rb, 1)
        for half_ in range(2):
            for k in range(KT):
                cols = U[:, k, half_ * HALF:(half_ + 1) * HALF]
                act.wait_ge(e_xn, half_ * KT + k + 1)
                act.activation(cols, cols, ACT.Silu, scale=ccol[:, 3 * KT + k:3 * KT + k + 1],
                               bias=ccol[:, 4 * KT + k:4 * KT + k + 1]).then_inc(e_u, 1)
        act.sem_inc(sq_done, 1)
        act.sem_inc(ht_done, 2)
        for t in range(NT + 2):
            if t < NT:
                act.wait_ge(e_add, t + 1)
                norm_tile(act, 3, t)
            if t >= 2:
                norm_evac(act, 3, t - 2, 2)
        moe_act(1, 3)
        stage_end(act, 4)
        norm_act(act, 4, False)

    @block.vector
    def _(dve):
        norm_dve_parts(dve, 0)

        def split(m, u, loads_done):
            dve.wait_ge(w_loaded[u], loads_done)
            if later(m, 2):
                dve.wait_ge(proj_done, m - 1)
            dve.tensor_copy(WR[:, u, 0], wq[u]).then_inc(w_high, 1)
            dve.wait_ge(w_high, m + 1)
            dve.tensor_tensor(WR[:, u, 1], wq[u], WR[:, u, 0], ALU.subtract).then_inc(w_split, 1)

        dve.wait_ge(xs_done, NT)
        dve.wait_ge(b_small, 48)
        dve.tensor_copy(GR[:, 0], wg).then_inc(g_split, 1)
        dve.wait_ge(g_split, 1)
        dve.tensor_tensor(GR[:, 1], wg, GR[:, 0], ALU.subtract).then_inc(g_split, 1)
        split(0, 0, 16)
        dve.wait_ge(gate_mm, 1)
        dve.wait_ge(b_small, 48)
        dve.tensor_scalar(ga, pair(4)[0:E, :], abias[0:E, 1:2], None, ALU.add).then_inc(gate_steps, 1)
        dve.wait_ge(gate_steps, 1)
        dve.scalar_tensor_tensor(gn, ga, -1.0, ga, ALU.mult, ALU.min).then_inc(gate_steps, 1)
        dve.wait_ge(gate_acts, 3)
        dve.scalar_tensor_tensor(lg, ga, 0.0, ge, ALU.max, ALU.add).then_inc(gate_steps, 1)
        dve.wait_ge(gate_steps, 3)
        dve.tensor_scalar(lg, lg, abias[0:E, 2:3], -1.0, ALU.mult, ALU.mult).then_inc(gate_steps, 1)
        dve.wait_ge(b_zero, 10)

        def b_step(m, u, now, prev, prev2, normed):
            if now:
                if earlier(m, PROJ - 1):
                    split(m + 1, 1 - u, (m - u) * 8 + 16 * (1 + u))
                dve.wait_ge(evac_done, m + 1)
                if prev2:
                    dve.wait_ge(silu_done, m - 1)
                for j in range(TAPS):
                    tap = cw[:, ds(m, 1), j:j + 1].rearrange("p o j -> p (o j)")
                    if j == 0:
                        ins = dve.tensor_scalar(cv[u], pre[u][:, 0:T], tap, None, ALU.mult)
                    else:
                        ins = dve.scalar_tensor_tensor(cv[u], pre[u][:, j:j + T], tap, cv[u], ALU.mult, ALU.add)
                    if j < TAPS - 1:
                        ins.then_inc(conv_steps, 1)
                        dve.wait_ge(conv_steps, m * (TAPS - 1) + j + 1)
                    else:
                        ins.then_inc(conv_done, 1)
            if prev:
                p = m - 1
                if normed[1]:
                    dve.wait_ge(rn_done, p + 1)
                    dve.wait_ge(tpq_done, p + 1)
                    dve.wait_ge(t_stored[1 - u], (p - (1 - u)) * 8 + 16)
                    dve.tensor_tensor(nrm[1 - u], sl[1 - u], rnb, ALU.mult).then_inc(mul_done, 1)
                else:
                    dve.wait_ge(silu_done, p + 1)
                    dve.sem_inc(mul_done, 1)

        b_loop(dve, b_step)
        dve.wait_ge(b2_act, 5)
        for d in range(2):
            dve.tensor_tensor(SC[:, d, :, 2, :], tot[:, :, d, :], SC[:, d, :, 0, :], ALU.subtract).then_inc(b2_dve, 1)
        stage_end(dve, 1)
        for d in range(2):
            dve.sem_inc(VI[d], AHEAD * len(DVE_INV))
            dve.sem_inc(VC[d], AHEAD * len(DVE_SCAN) - 1)
            dve.memset(ST[d], 0.0).then_inc(VC[d], 1)
        dve.wait_ge(s_gcst, 32)
        negm = [g(C_NEGF), g(C_NEGB)]
        m0 = [g(C_M0F), g(C_M0B)]

        def decay_arg(i, u, d):
            dve.wait_ge(PL[d], i + 1)
            dve.wait_ge(VC[d], at(DVE_SCAN, "s", i, 2))
            dve.tensor_copy(sc[u][d], SC[:, d, ds(chunk(i, d), 1), :, :].rearrange("p o k h -> p (o k) h")
                            ).then_inc(DG[d], 1)
            dve.wait_ge(DG[d], i * 2 + 1)
            dve.wait_ge(g_loaded[d], i * 16 + 16)
            for h in range(H):
                last = dve.scalar_tensor_tensor(dec[d][:, h, :], dec[d][:, h, :], sc[u][d][:, 0, h:h + 1], negm[d],
                                                ALU.subtract, ALU.min)
            last.then_inc(DG[d], 1)

        for d in range(2):
            decay_arg(0, 0, d)

        def c_inverse(name, d, i, u):
            turned = pair(2 + 2 * d)
            if name == "arg":
                if earlier(i, NT - 1):
                    decay_arg(i + 1, 1 - u, d)
            elif name == "kk":
                dve.wait_ge(PI[d], at(PE_INV, "kk", i))
                dve.wait_ge(EG[d], i + 1)
                for h in range(H):
                    last = dve.scalar_tensor_tensor(MT[d][:, h, :], turned[:, h * P:(h + 1) * P],
                                                    sc[u][d][:, 4, h:h + 1], dec[d][:, h, :], ALU.mult, ALU.mult)
                last.then_inc(VI[d], 1)
                dve.wait_ge(VI[d], at(DVE_INV, "mt", i))
                dve.wait_ge(PS[d], at(PE_SCAN, "xr", i, 2))
                dve.tensor_tensor(XT[u][d], MT[d], m0[d].unsqueeze(1).to_broadcast([P, H, P]), ALU.mult
                                  ).then_inc(VI[d], 1)
                dve.wait_ge(VI[d], at(DVE_INV, "xa", i))
                dve.tensor_tensor(XT[u][d], XT[u][d], ident.unsqueeze(1).to_broadcast([P, H, P]), ALU.add
                                  ).then_inc(VI[d], 1)
            elif name[0:2] == "xp":
                j = int(name[2:])
                dve.wait_ge(PI[d], at(PE_INV, name, i))
                dve.tensor_tensor(blocks(XM[d], d, j), blocks(XM[d], d, j), half(heads(ps[:, d, :]), j),
                                  ALU.add).then_inc(VI[d], 1)
            elif name[0] == "p":
                j = int(name[1:])
                lm = C_LM + (d * LEVELS + j) * (P // 2)
                dve.wait_ge(PI[d], at(PE_INV, name, i))
                dve.tensor_tensor(PN[d], heads(ps[:, d, :]), g(lm, P // 2).unsqueeze(1).to_broadcast([P, H, P // 2]),
                                  ALU.mult).then_inc(VI[d], 1)

        def c_scan(step, d, i, u):
            if step == "ks":
                dve.wait_ge(PS[d], at(PE_SCAN, "ks", i))
                for h in range(H):
                    last = dve.scalar_tensor_tensor(R[d][:, h, :], scan_bank(i, d)[:, h * P:(h + 1) * P],
                                                    sc[u][d][:, 5, h:h + 1], loads[u][d][3][:, h, :],
                                                    ALU.mult, ALU.add)
                last.then_inc(VC[d], 1)
            elif step == "iv":
                dve.wait_ge(PS[d], at(PE_SCAN, "iv", i))
                dve.tensor_tensor(OB[d], OB[d], heads(scan_bank(i, d)), ALU.add).then_inc(VC[d], 1)
            elif step == "kv":
                dve.wait_ge(PS[d], at(PE_SCAN, "kv", i))
                for h in range(H):
                    last = dve.scalar_tensor_tensor(ST[d][:, h, :], ST[d][:, h, :], sc[u][d][:, 3, h:h + 1],
                                                    scan_bank(i, d)[:, h * P:(h + 1) * P], ALU.mult, ALU.add)
                last.then_inc(VC[d], 1)

        interleaved(dve, c_inverse, c_scan)
        stage_end(dve, 2)

        dve.sem_inc(d_og, 2)
        dve.sem_inc(d_ss, 1)
        dve.sem_inc(d_add, 1)
        dve.wait_ge(nw_loaded, 16)

        def d_step(c, u, now, prev):
            if now:
                it2 = (c - u) * 24 + 48
                dve.wait_ge(d_loaded[u], it2)
                dve.tensor_tensor(of[:, u, :], of[:, u, :], ob[:, u, :], ALU.add).then_inc(d_sum, 1)
                dve.wait_ge(d_sq, c + 1)
                dve.tensor_reduce(ssd[:, u, :], heads(sqd), AX.X, ALU.add).then_inc(d_ss, 1)
                dve.wait_ge(d_rms, c + 1)
                dve.reciprocal(ssd[:, u, :], ssd[:, u, :]).then_inc(d_ro, 1)
                dve.wait_ge(d_ro, c + 1)
                dve.tensor_tensor(heads(of[:, u, :]), heads(of[:, u, :]),
                                  ssd[:, u, :].unsqueeze(2).to_broadcast([P, H, P]), ALU.mult).then_inc(d_chain, 1)
                dve.wait_ge(d_chain, c * 2 + 1)
                dve.tensor_tensor(heads(of[:, u, :]), heads(of[:, u, :]),
                                  nw.unsqueeze(1).to_broadcast([P, H, P]), ALU.mult).then_inc(d_chain, 1)
                dve.wait_ge(d_chain, c * 2 + 2)
                dve.wait_ge(d_tp, c + 1)
                dve.tensor_tensor(og[:, u, :], of[:, u, :], sz[:, u, :], ALU.mult).then_inc(d_og, 1)
            if prev:
                p = c - 2
                dve.wait_ge(d_mm, p + 3)
                xt = X[:, ds(p, 1), :].rearrange("p o n -> p (o n)")
                dve.tensor_tensor(xt, xt, pair(4 + 2 * u), ALU.add).then_inc(d_add, 1)

        def d_norm(c, u):
            if earlier(c, NT):
                d_step(c, u, True, later(c, 2))
            elif c < NT + 2:
                d_step(c, u, False, True)
            if later(c, 3):
                norm_scaled(dve, 1, c - 3, 1 - u, True, True)

        for c in range(2):
            d_norm(c, c)
        dve.wait_ge(gain_loaded, 32)
        for n in range(2):
            dve.wait_ge(s_x[n], 32)
        for c in range(2, 4):
            d_norm(c, c % 2)
        with dve.Fori(2, NT // 2) as it:
            for u in range(2):
                d_norm(it * 2 + u, u)
        for c in range(NT, NT + 3):
            d_norm(c, c % 2)
        norm_over(dve, 1)

        def moe_dve(l, n):
            base = first_layers(l)
            dve.wait_ge(ms["logits"], 1 + base["logits"])
            lgt = ps[:, 4, 0:NT * ROW].rearrange("p (t e) -> p t e", t=NT)[:, :, 0:E]
            dve.tensor_reduce(mx, lgt, AX.X, ALU.max).then_inc(ms["soft"], 1)
            dve.wait_ge(ms["soft"], 1 + base["soft"])
            dve.tensor_tensor(pr, lgt, mx.unsqueeze(2).to_broadcast([P, NT, E]), ALU.subtract).then_inc(ms["soft"], 1)
            dve.wait_ge(ms["exp"], 1 + base["exp"])
            dve.tensor_reduce(sm, pr, AX.X, ALU.add).then_inc(ms["soft"], 1)
            dve.wait_ge(ms["soft"], 3 + base["soft"])
            dve.reciprocal(rs, sm).then_inc(ms["soft"], 1)
            dve.wait_ge(ms["soft"], 4 + base["soft"])
            dve.tensor_tensor(pr, pr, rs.unsqueeze(2).to_broadcast([P, NT, E]), ALU.mult).then_inc(ms["soft"], 1)
            pt = [b[0:SEEK, :] for b in PT]
            dve.wait_ge(ms["pt"], 1 + base["pt"])
            for r in range(CAP // 8):
                v8, i8 = vals[:, r * 8:r * 8 + 8], idx8[:, r * 8:r * 8 + 8]
                dve.max(v8, pt[r % 2]).then_inc(ms["top"], 1)
                dve.wait_ge(ms["top"], 3 * r + 1 + base["top"])
                dve.max_index(i8, v8, pt[r % 2]).then_inc(ms["top"], 1)
                dve.match_replace(pt[1 - r % 2], v8, pt[r % 2], -1.0).then_inc(ms["top"], 1)
                dve.wait_ge(ms["top"], 3 * r + 3 + base["top"])
            dve.tensor_copy(idxf, idx8).then_inc(ms["top"], 1)
            dve.wait_ge(ms["top_mm"], 1 + base["top_mm"])
            dve.tensor_copy(both, ps[:, 4:6, 0:SEEK]).then_inc(ms["both"], 1)
            dve.wait_ge(ms["flip"], 1 + base["flip"])
            v0, t0, v1, t1 = both[:, 0, 0:E], both[:, 1, 0:E], ps[:, 6, 0:E], ps[:, 6, E:2 * E]
            dve.tensor_tensor(keep, v0, v1, ALU.is_ge).then_inc(ms["pick"], 1)
            dve.scalar_tensor_tensor(gap, t1, float(HALF), t0, ALU.add, ALU.subtract).then_inc(ms["pick"], 1)
            dve.tensor_tensor(aff, v0, v1, ALU.max).then_inc(ms["idx"], 1)
            dve.wait_ge(ms["pick"], 2 + base["pick"])
            dve.tensor_tensor(step_back, keep, gap, ALU.mult).then_inc(ms["pick"], 1)
            dve.wait_ge(ms["pick"], 3 + base["pick"])
            dve.scalar_tensor_tensor(chosen, t1, float(HALF), step_back, ALU.add, ALU.subtract).then_inc(ms["pick"], 1)
            dve.wait_ge(ms["pick"], 4 + base["pick"])
            dve.tensor_copy(idxT, chosen).then_inc(ms["idx"], 1)
            dve.wait_ge(ms["idx"], 2 + base["idx"])
            dve.sem_inc(ms["hid"], 1)
            dve.sem_inc(ms["y"], 1)

            def hid(e):
                dve.wait_ge(ms["up"], e + 1 + base["up"])
                dve.wait_ge(ms["silu"], e + 1 + base["silu"])
                if later(e, 1):
                    dve.wait_ge(ms["tph"], e + base["tph"])
                dve.tensor_tensor(HD, SG, pair(2), ALU.mult).then_inc(ms["hid"], 1)

            def y(e, u):
                dve.wait_ge(ms["down"], e + 2 + base["down"])
                dve.wait_ge(ms["scat_ok"], e + 1 + base["scat_ok"])
                dve.tensor_scalar(YS[u], pair(4), aff[:, ds(e, 1)], None, ALU.mult).then_inc(ms["y"], 1)

            hid(0)
            with dve.Fori(0, E // 2 - 1) as it:
                for u in range(2):
                    hid(it * 2 + u + 1)
                    y(it * 2 + u, u)
            hid(E - 1)
            y(E - 2, 0)
            y(E - 1, 1)

        moe_dve(0, 1)
        stage_end(dve, 3)
        norm_dve(dve, 2, True)
        dve.sem_inc(e_pre, 2)
        dve.sem_inc(e_conv, 2)
        dve.wait_ge(e_small, 48)
        dve.wait_ge(e_zero, 4)
        with dve.Fori(0, KT // 2) as it:
            for u in range(2):
                ch = it * 2 + u
                dve.wait_ge(e_sig, ch + 1)
                dve.wait_ge(e_prod, (ch + 1) * POOL_TAPS)
                dve.scalar_tensor_tensor(pre_e[u][:, CF_TAPS // 2:CF_TAPS // 2 + T], pair(4 * u), ccol[:, ds(ch, 1)],
                                         sg_e[u], ALU.add, ALU.mult).then_inc(e_pre, 1)
                dve.wait_ge(e_pre, ch + 3)
                dve.wait_ge(e_conv, ch + 2)
                for n in range(CHAIN):
                    j = POOL_TAPS + n
                    tap = dww[:, ds(ch, 1), j:j + 1].rearrange("p o j -> p (o j)")
                    acc = acc_e[n % 2]
                    if n == 0:
                        ins = dve.tensor_scalar(acc, pre_e[u][:, j:j + T], tap, ccol[:, ds(ch + 2 * KT, 1)],
                                                ALU.mult, ALU.add)
                    elif n == 1:
                        ins = dve.tensor_scalar(acc, pre_e[u][:, j:j + T], tap, None, ALU.mult)
                    else:
                        dve.wait_ge(e_chain, ch * (CHAIN + 1) + n - 1)
                        ins = dve.scalar_tensor_tensor(acc, pre_e[u][:, j:j + T], tap, acc, ALU.mult, ALU.add)
                    ins.then_inc(e_chain, 1)
                dve.wait_ge(e_chain, ch * (CHAIN + 1) + CHAIN)
                dve.tensor_tensor(acc_e[0], acc_e[0], acc_e[1], ALU.add).then_inc(e_chain, 1)
                dve.wait_ge(e_chain, (ch + 1) * (CHAIN + 1))
                dve.wait_ge(e_padd, (ch + 1) * (POOL_TAPS - 1) + 1)
                dve.tensor_tensor(U[:, ds(ch, 1), :].rearrange("p o n -> p (o n)"), acc_e[0], sum_e[u], ALU.add
                                  ).then_inc(e_conv, 1)
        dve.wait_ge(e_mean, 1)
        dve.tensor_scalar(mb, pair(0), 1.0 / D, None, ALU.mult).then_inc(e_mb, 1)
        dve.wait_ge(e_mb, 1)
        for k in range(KT):
            dve.tensor_tensor(U[:, k, :], U[:, k, :], mb, ALU.subtract).then_inc(e_xc, 1)
        dve.wait_ge(e_rb, 1)
        for half_ in range(2):
            for k in range(KT):
                cols = U[:, k, half_ * HALF:(half_ + 1) * HALF]
                dve.tensor_tensor(cols, cols, rb[:, half_ * HALF:(half_ + 1) * HALF], ALU.mult).then_inc(e_xn, 1)
        dve.wait_ge(e_bias, NT)
        for t in range(NT):
            dve.wait_ge(e_pw2, t + 1)
            dve.tensor_tensor(X[:, t, :], X[:, t, :], pair(4 + 2 * (t % 2)), ALU.add).then_inc(e_add, 1)
            if t == 0:
                dve.wait_ge(gain_loaded, 64)
            else:
                norm_scaled(dve, 3, t - 1, (t - 1) % 2, True, True)
        norm_scaled(dve, 3, NT - 1, (NT - 1) % 2, True, True)
        norm_over(dve, 3)
        moe_dve(1, 3)
        stage_end(dve, 4)
        norm_dve(dve, 4, False)

    @block.tensor
    def _(pe):
        pe.wait_ge(s_cst, 48)
        norm_pe(pe, 0)
        pe.wait_ge(g_split, 2)
        pe.wait_ge(ht_done, NT + 2 + before(0, "ht_done"))
        for half_ in range(2):
            last = in_parts(pe, ps[:, 4 + half_, :], GR, lambda b_, k: HR[:, b_, k, half_ * HALF:(half_ + 1) * HALF])
        last.then_inc(gate_mm, 1)

        def b_step(m, u, now, prev, prev2, normed):
            if now:
                pe.wait_ge(w_split, m + 1)
                if prev2:
                    pe.wait_ge(evac_done, m - 1)
                for half_ in range(2):
                    last = in_parts(pe, ps[:, 2 * u + half_, :], WR[:, u],
                                    lambda b_, k: HR[:, b_, k, half_ * HALF:(half_ + 1) * HALF])
                last.then_inc(proj_done, 1)
            if prev and normed[1]:
                p = m - 1
                pe.wait_ge(sqb_done, p + 1)
                if prev2:
                    pe.wait_ge(lnr_done, p)
                else:
                    pe.wait_ge(gate_steps, 1)
                    pe.wait_ge(gate_acts, 4)
                for half_ in range(2):
                    last = pe.matmul(ps[:, 4 + half_, :], ones, sqb[:, half_ * HALF:(half_ + 1) * HALF],
                                     start=True, stop=True)
                last.then_inc(sqmm_done, 1)
            if prev2:
                p = m - 2
                pe.wait_ge(mul_done, p + 1)
                pe.wait_ge(nat_done, p)
                src = nrm[u] if normed[2] else sl[u]
                for c in range(NT):
                    last = pe.transpose(pair(6)[:, c * P:(c + 1) * P], src[:, c * P:(c + 1) * P], ident)
                last.then_inc(tpq_done, 1)

        pe.sem_inc(tpq_done, 2)
        b_loop(pe, b_step)
        pe.wait_ge(evac_done, PROJ)
        pe.wait_ge(gate_steps, 4)
        for c in range(NT):
            pe.transpose(ps[:, 0, c * E:(c + 1) * E], lg[:, c * P:(c + 1) * P], ident[0:E, 0:E])
        for c in range(NT):
            last = pe.transpose(ps[:, 1, c * E:(c + 1) * E], bs[:, c * P:(c + 1) * P], ident[0:E, 0:E])
        last.then_inc(b2_pe, 1)
        pe.wait_ge(b2_act, 1)
        pe.wait_ge(s_gcst, 32)
        pe.wait_ge(nat_done, PROJ)
        pe.wait_ge(lnr_done, NORMED)
        for d in range(2):
            pe.matmul(ps[:, 2 + d, 0:NT * H].rearrange("p (c h) -> p c h", c=NT), uf[:, d * P:(d + 1) * P], lgn[:, :, d * H:(d + 1) * H],
                      start=True, stop=True)
        pe.matmul(ps[:, 4, 0:NT * E], ones, lgn.rearrange("p c n -> p (c n)"), start=True, stop=True).then_inc(b2_pe, 1)
        pe.wait_ge(b2_act, 5)
        for d in range(2):
            for c in range(NT):
                n = (d * NT + c) * P
                last = pe.transpose(ps[0:H, 4 + n // HALF, n % HALF:n % HALF + P], SC[:, d, c, 0, :], ident)
        last.then_inc(b2_pe, 1)
        stage_end(pe, 1)
        for d in range(2):
            pe.sem_inc(PI[d], AHEAD * len(PE_INV))
            pe.sem_inc(PS[d], AHEAD * len(PE_SCAN))

        def products(s, out, lhs, rhs):
            n = out.shape[1] // H
            for h in range(H):
                last = pe.matmul(out[:, h * n:(h + 1) * n], lhs[:, h, :], rhs[:, h], start=True, stop=True,
                                 skip_group_check=True)
            last.then_inc(s, 1)

        def turn(s, out, src):
            for h in range(H):
                last = pe.transpose(out[:, h * P:(h + 1) * P], src[:, h, :], ident)
            last.then_inc(s, 1)

        def c_inverse(name, d, i, u):
            q_t, k_t = loads[u][d][0:2]
            turned = pair(2 + 2 * d)
            if name == "kk":
                pe.wait_ge(c_ld[d][u], (i - u) * 32 + 64)
                pe.wait_ge(AI[d], at(ACT_INV, f"t{LEVELS - 1}", i, 1))
                products(PI[d], turned, k_t, k_t)
            elif name == "qk":
                pe.wait_ge(VI[d], at(DVE_INV, "mt", i))
                products(PI[d], turned, k_t, q_t)
            elif name == "x0":
                pe.wait_ge(VI[d], at(DVE_INV, "xt0", i))
                pe.wait_ge(AI[d], at(ACT_INV, "qk", i))
                turn(PI[d], turned, XT[u][d])
            elif name == "p0":
                pe.wait_ge(AI[d], at(ACT_INV, "x0", i))
                products(PI[d], ps[:, d, :], MT[d], blocks(XM[d], d, 0))
            elif name[0:2] == "xp":
                j = int(name[2:])
                pe.wait_ge(VI[d], at(DVE_INV, f"pn{j}", i))
                if j:
                    pe.wait_ge(AI[d], at(ACT_INV, f"t{j - 1}", i))
                products(PI[d], ps[:, d, :], XT[u][d], PN[d])
            elif name[0] == "p":
                j = int(name[1:])
                pe.wait_ge(VI[d], at(DVE_INV, f"x{j - 1}", i))
                products(PI[d], ps[:, d, :], MT[d], blocks(XM[d], d, j))
            elif name[0] == "t":
                j = int(name[1:])
                if j == LEVELS - 1:
                    pe.wait_ge(VI[d], at(DVE_INV, f"x{j}", i))
                turn(PI[d], pair(2 + 2 * d), XM[d])

        def c_scan(step, d, i, u):
            q_t, k_t, k_n = loads[u][d][0:3]
            if earlier(i, NT - 1):
                read_by = {("qs", 0): (VC[1], DVE_SCAN, "s", 1), ("qs", 1): (AS[0], ACT_SCAN, "oq", 0),
                           ("ks", 0): (AS[1], ACT_SCAN, "oq", 0), ("ks", 1): (VC[0], DVE_SCAN, "r", 0),
                           ("xr", 0): (VC[1], DVE_SCAN, "r", 0), ("xr", 1): (AS[0], ACT_SCAN, "vn", 0),
                           ("iv", 0): (AS[1], ACT_SCAN, "vn", 0), ("iv", 1): (VC[0], DVE_SCAN, "o", 0),
                           ("kv", 0): (VC[1], DVE_SCAN, "o", 0), ("kv", 1): (VC[0], DVE_SCAN, "s", 0)}[step, d]
                pe.wait_ge(read_by[0], at(read_by[1], read_by[2], i, read_by[3]))
            elif step == "qs":
                pe.wait_ge(AI[d], at(ACT_INV, f"t{LEVELS - 1}", i))
            elif step == "ks":
                pe.wait_ge(AS[d], at(ACT_SCAN, "oq", i))
            out = scan_bank(i, d)
            if step == "qs":
                pe.wait_ge(VC[d], at(DVE_SCAN, "s", i, 1))
                products(PS[d], out, q_t, ST[d])
            elif step == "ks":
                products(PS[d], out, k_t, ST[d])
            elif step == "xr":
                pe.wait_ge(VC[d], at(DVE_SCAN, "r", i))
                pe.wait_ge(AI[d], at(ACT_INV, f"t{LEVELS - 1}", i))
                products(PS[d], out, XT[u][d], R[d])
            elif step == "iv":
                pe.wait_ge(AS[d], at(ACT_SCAN, "vn", i))
                pe.wait_ge(GI[d], i + 1)
                products(PS[d], out, intra[u][d], VN[d])
            else:
                pe.wait_ge(PL[d], i + 3)
                products(PS[d], out, k_n, VS[d])

        interleaved(pe, c_inverse, c_scan)
        stage_end(pe, 2)

        pe.sem_inc(d_tp, 2)
        pe.sem_inc(d_mm, 2)
        pe.wait_ge(wo_loaded, 16)

        def d_step(c, u, now, prev):
            if now:
                pe.wait_ge(d_og, c + 3)
                pe.wait_ge(d_ot, c + 1)
                for k in range(KT):
                    last = pe.transpose(pair(0)[:, k * P:(k + 1) * P], og[:, u, k * P:(k + 1) * P], ident)
                last.then_inc(d_tp, 1)
            if prev:
                p, w = c - 1, 1 - u
                pe.wait_ge(d_ot, p + 2)
                if later(p, 1):
                    pe.wait_ge(d_add, p)
                for half_ in range(2):
                    for k in range(KT):
                        last = pe.matmul(ps[:, 4 + 2 * w + half_, :], ot[w][:, k, :],
                                         wo[:, k, half_ * HALF:(half_ + 1) * HALF], start=(k == 0), stop=(k == KT - 1))
                last.then_inc(d_mm, 1)

        pe.sem_inc(tp_done, 2)

        def d_norm(c, u):
            d_step(c, u, earlier(c, NT), later(c, 1))
            if later(c, 3):
                norm_turn(pe, 1, c - 3, 1 - u, 2, 2)

        for c in range(4):
            d_norm(c, c % 2)
        with pe.Fori(2, NT // 2) as it:
            for u in range(2):
                d_norm(it * 2 + u, u)
        d_norm(NT, 0)

        def moe_pe(l, n):
            base = first_layers(l)
            pe.wait_ge(wr_loaded, 16 * (l + 1))
            for half_ in range(2):
                pe.wait_ge(ht_done, (NT // 2 if half_ == 0 else NT) + 2 + before(n, "ht_done"))
                for k in range(KT):
                    last = pe.matmul(ps[0:E, half_, :], wr[:, k, :], HT[:, k, half_ * HALF:(half_ + 1) * HALF],
                                     start=(k == 0), stop=(k == KT - 1))
                if half_ == 0:
                    for t in (NT - 2, NT - 1):
                        norm_turn(pe, n, t, t % 2, 2, 2)
            last.then_inc(ms["lt_mm"], 1)
            pe.wait_ge(ms["lt"], 1 + base["lt"])
            for t in range(NT):
                last = pe.transpose(ps[:, 4, slots[t] * ROW:slots[t] * ROW + E], LT[:, t * P:(t + 1) * P],
                                    ident[0:E, 0:E])
            last.then_inc(ms["logits"], 1)
            pe.wait_ge(ms["soft"], 5 + base["soft"])
            for t in range(NT // 2):
                last = pe.transpose(ps[0:2 * ROW, 2, t * P:(t + 1) * P], prow[:, t * 2 * ROW:(t + 1) * 2 * ROW], ident)
            last.then_inc(ms["pt_mm"], 1)
            pe.wait_ge(ms["top"], 3 * (CAP // 8) + 1 + base["top"])
            pe.transpose(ps[:, 4, 0:SEEK], vals, ident[0:SEEK, 0:SEEK])
            pe.transpose(ps[:, 5, 0:SEEK], idxf, ident[0:SEEK, 0:SEEK]).then_inc(ms["top_mm"], 1)
            pe.wait_ge(ms["both"], 1 + base["both"])
            pe.matmul(ps[:, 6, 0:2 * E].rearrange("p (n e) -> p n e", n=2), flip, both[:, :, ROW:SEEK],
                      start=True, stop=True).then_inc(ms["flip"], 1)
            pe.sem_inc(ms["down"], 1)

            def tpx(e, u, slot_count):
                pe.wait_ge(ms[f"gath{u}"], slot_count + base[f"gath{u}"])
                for k in range(KT):
                    last = pe.transpose(pair(6)[:, k * P:(k + 1) * P], xin[u][:, k * P:(k + 1) * P], ident)
                last.then_inc(ms["tpx"], 1)

            def product(bank, lhs, w, half_):
                for k in range(KT):
                    last = pe.matmul(ps[:, bank + half_, :], lhs[:, k, :], w[:, k, half_ * HALF:(half_ + 1) * HALF],
                                     start=(k == 0), stop=(k == KT - 1))
                return last

            def gate(e, u, slot_count):
                pe.wait_ge(ms["xt"], e + 1 + base["xt"])
                pe.wait_ge(ms[f"wg{u}"], slot_count + base[f"wg{u}"])
                if later(e, 1):
                    pe.wait_ge(ms["silu"], e + base["silu"])
                product(0, xT, WG[u], 0)
                product(0, xT, WG[u], 1).then_inc(ms["gate"], 1)

            def up(e, u, slot_count):
                pe.wait_ge(ms[f"wu{u}"], slot_count + base[f"wu{u}"])
                pe.wait_ge(ms["hid"], e + 1 + base["hid"])
                product(2, xT, WU[u], 0)
                product(2, xT, WU[u], 1).then_inc(ms["up"], 1)

            def tph(e):
                pe.wait_ge(ms["hid"], e + 2 + base["hid"])
                pe.wait_ge(ms["xt"], e + 2 + base["xt"])
                for k in range(KT):
                    last = pe.transpose(pair(6)[:, k * P:(k + 1) * P], HD[:, k * P:(k + 1) * P], ident)
                last.then_inc(ms["tph"], 1)

            def down(e, between):
                pe.wait_ge(ms["ht"], e + 1 + base["ht"])
                pe.wait_ge(ms["wd"], e * 16 + 16 + base["wd"])
                pe.wait_ge(ms["y"], e + 1 + base["y"])
                product(4, hT, WD, 0)
                between()
                product(4, hT, WD, 1).then_inc(ms["down"], 1)

            pe.wait_ge(ms["idx"], 2 + base["idx"])
            tpx(0, 0, 16)
            gate(0, 0, 16)
            up(0, 0, 16)
            tpx(1, 1, 16)
            with pe.Fori(0, E // 2 - 1) as it:
                for u in range(2):
                    e = it * 2 + u
                    nxt = it * 16 + 16 * (1 + u)
                    gate(e + 1, 1 - u, nxt)
                    tph(e)
                    up(e + 1, 1 - u, nxt)

                    def next_x():
                        pe.wait_ge(ms["ht"], e + 1 + base["ht"])
                        tpx(e + 2, u, it * 16 + 32)
                    down(e, next_x)
            gate(E - 1, 1, 8 * E)
            tph(E - 2)
            up(E - 1, 1, 8 * E)
            down(E - 2, lambda: None)
            pe.wait_ge(ms["hid"], E + 1 + base["hid"])
            pe.wait_ge(ms["ht"], E - 1 + base["ht"])
            for k in range(KT):
                last = pe.transpose(pair(6)[:, k * P:(k + 1) * P], HD[:, k * P:(k + 1) * P], ident)
            last.then_inc(ms["tph"], 1)
            down(E - 1, lambda: None)

        moe_pe(0, 1)
        stage_end(pe, 3)
        norm_pe(pe, 2)
        pe.wait_ge(ht_done, NT + 2 + before(2, "ht_done"))
        with pe.Fori(0, KT // 2) as it:
            for u in range(2):
                ch = it * 2 + u
                pe.wait_ge(e_w[u], it * 32 + 32)
                pe.wait_ge(e_pre, ch + 1)
                for n in range(2):
                    for half_ in range(2):
                        for k in range(KT):
                            last = pe.matmul(ps[:, 4 * u + 2 * n + half_, :], wag[u][n][:, k, :],
                                             HT[:, k, half_ * HALF:(half_ + 1) * HALF],
                                             start=(k == 0), stop=(k == KT - 1))
                last.then_inc(e_mm, 1)
        pe.wait_ge(e_pre, KT + 2)
        for k in range(KT):
            pe.wait_ge(e_conv, k + 3)
            for half_ in range(2):
                last = pe.matmul(ps[:, half_, :], ones, U[:, k, half_ * HALF:(half_ + 1) * HALF],
                                 start=(k == 0), stop=(k == KT - 1))
        last.then_inc(e_mean, 1)
        for k in range(KT):
            pe.wait_ge(e_sq, k + 1)
            for half_ in range(2):
                last = pe.matmul(ps[:, 2 + half_, :], ones, sq_e[k % 2][:, half_ * HALF:(half_ + 1) * HALF],
                                 start=(k == 0), stop=(k == KT - 1))
            last.then_inc(e_sqmm, 1)
        pe.wait_ge(w2_loaded, 16)
        pe.sem_inc(tp_done, 2)
        for t in range(NT):
            pe.wait_ge(e_u, KT if t < NT // 2 else 2 * KT)
            if t >= 2:
                pe.wait_ge(e_add, t - 1)
            for half_ in range(2):
                for k in range(KT):
                    last = pe.matmul(ps[:, 4 + 2 * (t % 2) + half_, :], U[:, k, t * P:(t + 1) * P],
                                     w2[:, k, half_ * HALF:(half_ + 1) * HALF], start=(k == 0), stop=(k == KT - 1))
            last.then_inc(e_pw2, 1)
            if t >= 2:
                norm_turn(pe, 3, t - 2, t % 2, 2, 2)
        moe_pe(1, 3)
        stage_end(pe, 4)


def laid_out(inputs):
    x = {k: np.asarray(v) for k, v in inputs.items()}
    w_in = x["dn_w_in"][0]
    gates = w_in[:, 4 * D:].reshape(KT, P, 2, 2, H)
    gate_columns = np.zeros((P, KT, P), np.float32)
    for n in range(2):
        gate_columns[:, :, 32 * n:32 * n + E] = gates[:, :, :, 1 - n].transpose(1, 0, 2, 3).reshape(P, KT, E)
    tiled = lambda w: np.ascontiguousarray(w.reshape(KT, P, -1, P).transpose(2, 1, 0, 3))
    cols = lambda v: np.ascontiguousarray(v.reshape(-1, P).T)
    return {
        "x": x["x"][0],
        "consts": constants(),
        "norm_mix": x["norm_mix"], "norm_ffn": x["norm_ffn"], "final_norm": x["final_norm"],
        "w_in": tiled(w_in[:, :4 * D]),
        "w_gates": gate_columns,
        "conv_w": np.ascontiguousarray(x["dn_conv_w"][0].reshape(TAPS, 3 * H, P).transpose(2, 1, 0)),
        "gate_bias": np.stack([x["dn_a_log"][0].reshape(-1), x["dn_dt_bias"][0].reshape(-1)], 1),
        "dn_norm_w": x["dn_norm_w"][0],
        "dn_w_out": x["dn_w_out"][0],
        "w_pw1": tiled(x["cf_w_pw1"][0]),
        "cf_cols": np.concatenate([cols(x["cf_b_pw1"][0]), cols(x["cf_dw_b"][0]), cols(x["cf_ln_g"][0]),
                                   cols(x["cf_ln_b"][0])], 1),
        "cf_dw_w": np.ascontiguousarray(x["cf_dw_w"][0].reshape(CF_TAPS, KT, P).transpose(2, 1, 0)),
        "w_pw2": x["cf_w_pw2"][0],
        "b_pw2": x["cf_b_pw2"][0],
        "w_router": np.ascontiguousarray(x["moe_w_router"].reshape(2, KT, P, E).transpose(0, 2, 1, 3)),
        "w_gate": x["moe_w_gate"], "w_up": x["moe_w_up"], "w_down": x["moe_w_down"],
    }


def kernel(**inputs):
    import concourse.bacc as bacc
    from concourse.bass_utils import run_bass_kernel_spmd

    nc = bacc.Bacc("TRN2", target_bir_lowering=False, num_devices=1)
    arrays = laid_out(inputs)
    aps = {n: nc.dram_tensor(f"in_{n}", v.shape, mybir.dt.from_np(v.dtype), kind="ExternalInput").ap()
           for n, v in arrays.items()}
    out = nc.dram_tensor("out", (1, T, D), F32, kind="ExternalOutput").ap()
    build(nc, aps, out)
    r = run_bass_kernel_spmd(nc, [{f"in_{n}": v for n, v in arrays.items()}], core_ids=[0])
    return r.results[0]["out"]
```
